# Optimizing a Trainium2 kernel written in Bass

```python
import math
import jax
import jax.numpy as jnp
from jax import lax
import numpy as np

D_MODEL = 1024
BATCH = 1
SEQ = 1024
DEPTH = 2

N_HEADS_A = 8
HEAD_DIM_A = 64
ROPE_DIM_A = HEAD_DIM_A // 4
DILATED_BRANCHES = ((128, 1), (512, 4), (2048, 16))
MLA_HEADS = 8
MLA_NOPE = 64
MLA_ROPE = 32
MLA_V = 64
MLA_Q_RANK = 256
MLA_KV_RANK = 128
ROPE_THETA = 500000.0
Q_BLOCK = 128
MIX_A = N_HEADS_A * HEAD_DIM_A
MIX_B = MLA_HEADS * MLA_V
ATTN_IN = 3 * MIX_A + MLA_Q_RANK + MLA_KV_RANK + MLA_ROPE
D_INNER = 2 * D_MODEL
SSD_HEADDIM = 64
SSD_HEADS = D_INNER // SSD_HEADDIM
SSD_GROUPS = 4
D_STATE = 128
D_CONV = 4
CHUNK = 256
XBC_DIM = D_INNER + 2 * SSD_GROUPS * D_STATE
SSD_IN = D_INNER + XBC_DIM + SSD_HEADS
N_GROUPS = 4
EXPERTS_PER_GROUP = 8
N_EXPERTS = N_GROUPS * EXPERTS_PER_GROUP
TOP_K_IN_GROUP = 2
D_EXPERT = 512
MOE_BLOCK = 128
NORM_EPS = 1e-6

kernel_name = 'hybrid_dilated_mla_ssd_hmoe'

def rmsnorm(x, g):
    xf = x.astype(jnp.float32)
    y = xf * lax.rsqrt(jnp.mean(xf * xf, axis=-1, keepdims=True) + NORM_EPS)
    return (y * g.astype(jnp.float32)).astype(x.dtype)

def rope_tables(positions, rot_dim):
    inv_freq = ROPE_THETA ** (-jnp.arange(0, rot_dim, 2, dtype=jnp.float32) / rot_dim)
    ang = positions.astype(jnp.float32)[..., None] * inv_freq
    return jnp.cos(ang), jnp.sin(ang)

def apply_rope(x, cos, sin):
    half = x.shape[-1] // 2
    c = cos[:, :, None, :].astype(x.dtype)
    s = sin[:, :, None, :].astype(x.dtype)
    x1, x2 = x[..., :half], x[..., half:]
    return jnp.concatenate([x1 * c - x2 * s, x2 * c + x1 * s], axis=-1)

def partial_rope(x, cos, sin):
    return jnp.concatenate([apply_rope(x[..., :ROPE_DIM_A], cos, sin), x[..., ROPE_DIM_A:]], axis=-1)

def dilated_branch(q, k, v, window, dilation):
    Bsz, S, H, Dh = q.shape
    span = window // dilation
    unit = span * dilation
    Sp = -(-S // unit) * unit
    nb = Sp // unit

    def residue_blocks(t):
        t = jnp.pad(t, ((0, 0), (0, Sp - S), (0, 0), (0, 0)))
        return t.reshape(Bsz, nb, span, dilation, H, Dh)

    def with_prev(t):
        prev = jnp.pad(t, ((0, 0), (1, 0), (0, 0), (0, 0), (0, 0), (0, 0)))[:, :-1]
        return jnp.concatenate([prev, t], axis=2)

    qs = residue_blocks(q)
    ks = with_prev(residue_blocks(k))
    vs = with_prev(residue_blocks(v))
    s = jnp.einsum('bnqrhd,bnkrhd->bnrhqk', qs, ks).astype(jnp.float32) * (Dh ** -0.5)
    qi = jnp.arange(span)[:, None]
    ki = jnp.arange(2 * span)[None, :]
    dist = qi + span - ki
    band = (dist >= 0) & (dist <= span)
    has_prev = (jnp.arange(nb)[:, None, None] > 0) | (ki[None] >= span)
    valid = band[None] & has_prev
    s = jnp.where(valid[None, :, None, None], s, -jnp.inf)
    m = jnp.max(s, axis=-1, keepdims=True)
    p = jnp.exp(s - m)
    l = jnp.sum(p, axis=-1)
    o = jnp.einsum('bnrhqk,bnkrhd->bnqrhd', p.astype(v.dtype), vs).astype(jnp.float32)
    l_q = jnp.moveaxis(l, -1, 2)
    o = o / l_q[..., None]
    lse = jnp.moveaxis(m[..., 0], -1, 2) + jnp.log(l_q)
    return o.reshape(Bsz, Sp, H, Dh)[:, :S], lse.reshape(Bsz, Sp, H)[:, :S]

def dilated_mixture_attention(q, k, v):
    outs, lses = [], []
    for window, dilation in DILATED_BRANCHES:
        o, lse = dilated_branch(q, k, v, window, dilation)
        outs.append(o)
        lses.append(lse)
    alpha = jax.nn.softmax(jnp.stack(lses), axis=0)
    return jnp.sum(alpha[..., None] * jnp.stack(outs), axis=0).astype(q.dtype)

def causal_block_attention(q, k, v):
    Bsz, S, H, Dk = q.shape
    nq = S // Q_BLOCK
    scale = Dk ** -0.5
    q_blocks = q.reshape(Bsz, nq, Q_BLOCK, H, Dk).swapaxes(0, 1)
    k_pos = jnp.arange(S)

    def one_block(args):
        qb, start = args
        s = jnp.einsum('bqhd,bkhd->bhqk', qb, k).astype(jnp.float32) * scale
        q_pos = start + jnp.arange(Q_BLOCK)
        s = jnp.where(k_pos[None, :] <= q_pos[:, None], s, -jnp.inf)
        p = jax.nn.softmax(s, axis=-1).astype(v.dtype)
        return jnp.einsum('bhqk,bkhd->bqhd', p, v)

    out = lax.map(one_block, (q_blocks, jnp.arange(nq) * Q_BLOCK))
    return out.swapaxes(0, 1).reshape(Bsz, S, H, v.shape[-1])

def hybrid_attention_mixer(h, rope_a, rope_b, w_in, q_norm, w_uq, kv_norm, w_ukv, w_out):
    Bsz, S, _ = h.shape
    proj = h @ w_in
    cuts = [MIX_A, 2 * MIX_A, 3 * MIX_A, 3 * MIX_A + MLA_Q_RANK, 3 * MIX_A + MLA_Q_RANK + MLA_KV_RANK]
    qa, ka, va, cq, ckv, kr = jnp.split(proj, cuts, axis=-1)
    qa = partial_rope(qa.reshape(Bsz, S, N_HEADS_A, HEAD_DIM_A), *rope_a)
    ka = partial_rope(ka.reshape(Bsz, S, N_HEADS_A, HEAD_DIM_A), *rope_a)
    va = va.reshape(Bsz, S, N_HEADS_A, HEAD_DIM_A)
    o_a = dilated_mixture_attention(qa, ka, va).reshape(Bsz, S, MIX_A)
    q = (rmsnorm(cq, q_norm) @ w_uq).reshape(Bsz, S, MLA_HEADS, MLA_NOPE + MLA_ROPE)
    q = jnp.concatenate([q[..., :MLA_NOPE], apply_rope(q[..., MLA_NOPE:], *rope_b)], axis=-1)
    kv = (rmsnorm(ckv, kv_norm) @ w_ukv).reshape(Bsz, S, MLA_HEADS, MLA_NOPE + MLA_V)
    k_rope = apply_rope(kr.reshape(Bsz, S, 1, MLA_ROPE), *rope_b)
    k = jnp.concatenate([kv[..., :MLA_NOPE], jnp.broadcast_to(k_rope, (Bsz, S, MLA_HEADS, MLA_ROPE))], axis=-1)
    v = kv[..., MLA_NOPE:]
    o_b = causal_block_attention(q, k, v).reshape(Bsz, S, MIX_B)
    return jnp.concatenate([o_a, o_b], axis=-1) @ w_out

def causal_depthwise_conv(u, w, b):
    width, ch = w.shape
    y = lax.conv_general_dilated(u, w[:, None, :], window_strides=(1,), padding=[(width - 1, 0)],
                                 dimension_numbers=('NWC', 'WIO', 'NWC'), feature_group_count=ch)
    return y + b

def ssd_chunked_scan(xs, dt, a, bm, cm):
    Bsz, S, H, P = xs.shape
    G, N = bm.shape[2], bm.shape[3]
    hg = H // G
    Sp = -(-S // CHUNK) * CHUNK
    nc = Sp // CHUNK

    def chunks(t):
        t = jnp.pad(t, [(0, 0), (0, Sp - S)] + [(0, 0)] * (t.ndim - 2))
        return t.reshape((Bsz, nc, CHUNK) + t.shape[2:]).swapaxes(0, 1)

    xc = chunks(xs.astype(jnp.float32).reshape(Bsz, S, G, hg, P))
    dtc = chunks(dt.reshape(Bsz, S, G, hg))
    bc = chunks(bm.astype(jnp.float32))
    cc = chunks(cm.astype(jnp.float32))
    a_g = a.reshape(G, hg)
    causal = jnp.tril(jnp.ones((CHUNK, CHUNK), dtype=bool))

    def step(state, inp):
        x, dtq, bq, cq = inp
        cs = jnp.cumsum(dtq * a_g, axis=1)
        seg = cs[:, :, None] - cs[:, None, :]
        decay = jnp.exp(jnp.where(causal[None, :, :, None, None], seg, -jnp.inf))
        xdt = x * dtq[..., None]
        cb = jnp.einsum('bign,bjgn->bijg', cq, bq)
        y = jnp.einsum('bijgh,bjghp->bighp', cb[..., None] * decay, xdt)
        y = y + jnp.einsum('bign,bghpn->bighp', cq, state) * jnp.exp(cs)[..., None]
        to_end = jnp.exp(cs[:, -1:] - cs)
        state = state * jnp.exp(cs[:, -1])[..., None, None] + jnp.einsum('bjgn,bjghp->bghpn', bq, to_end[..., None] * xdt)
        return state, y

    state0 = jnp.zeros((Bsz, G, hg, P, N), jnp.float32)
    _, ys = lax.scan(step, state0, (xc, dtc, bc, cc))
    return ys.swapaxes(0, 1).reshape(Bsz, Sp, H, P)[:, :S]

def ssd_mixer(h, w_in, conv_w, conv_b, dt_bias, a_log, d_skip, gate_norm, w_out):
    Bsz, S, _ = h.shape
    z, xbc, dt = jnp.split(h @ w_in, [D_INNER, D_INNER + XBC_DIM], axis=-1)
    xbc = jax.nn.silu(causal_depthwise_conv(xbc, conv_w, conv_b))
    xs, bm, cm = jnp.split(xbc, [D_INNER, D_INNER + SSD_GROUPS * D_STATE], axis=-1)
    xs = xs.reshape(Bsz, S, SSD_HEADS, SSD_HEADDIM)
    bm = bm.reshape(Bsz, S, SSD_GROUPS, D_STATE)
    cm = cm.reshape(Bsz, S, SSD_GROUPS, D_STATE)
    dt = jax.nn.softplus(dt.astype(jnp.float32) + dt_bias.astype(jnp.float32))
    a = -jnp.exp(a_log.astype(jnp.float32))
    y = ssd_chunked_scan(xs, dt, a, bm, cm) + d_skip.astype(jnp.float32)[:, None] * xs.astype(jnp.float32)
    y = y.reshape(Bsz, S, D_INNER) * jax.nn.silu(z.astype(jnp.float32))
    y = rmsnorm(y.reshape(Bsz, S, SSD_GROUPS, D_INNER // SSD_GROUPS), gate_norm.reshape(SSD_GROUPS, -1))
    return y.reshape(Bsz, S, D_INNER).astype(h.dtype) @ w_out

def hierarchical_moe(h, w_group, b_group, w_router, b_router, w_gate, w_up, w_down):
    Bsz, S, D = h.shape
    T = Bsz * S
    t = h.reshape(T, D)
    g_prob = jax.nn.softmax((t @ w_group).astype(jnp.float32) + b_group.astype(jnp.float32), axis=-1)
    g_val, g_idx = lax.top_k(g_prob, 1)
    e_logits = ((t @ w_router).astype(jnp.float32) + b_router.astype(jnp.float32)).reshape(T, N_GROUPS, EXPERTS_PER_GROUP)
    in_group = e_logits[jnp.arange(T), g_idx[:, 0]]
    e_val, e_idx = lax.top_k(in_group, TOP_K_IN_GROUP)
    gates = jax.nn.softmax(e_val, axis=-1) * g_val
    experts = g_idx * EXPERTS_PER_GROUP + e_idx
    tk = T * TOP_K_IN_GROUP
    flat_e = experts.reshape(tk)
    flat_g = gates.reshape(tk)
    flat_tok = jnp.repeat(jnp.arange(T, dtype=jnp.int32), TOP_K_IN_GROUP)
    order = jnp.argsort(flat_e)
    se, stok, sg = flat_e[order], flat_tok[order], flat_g[order]
    counts = jnp.bincount(flat_e, length=N_EXPERTS)
    starts = jnp.cumsum(counts) - counts
    padded = (counts + MOE_BLOCK - 1) // MOE_BLOCK * MOE_BLOCK
    pad_ends = jnp.cumsum(padded)
    pad_starts = pad_ends - padded
    dest = pad_starts[se] + jnp.arange(tk) - starts[se]
    n_blocks = -(-tk // MOE_BLOCK) + N_EXPERTS
    rows = n_blocks * MOE_BLOCK
    row_tok = jnp.zeros((rows,), jnp.int32).at[dest].set(stok)
    row_gate = jnp.zeros((rows,), jnp.float32).at[dest].set(sg)
    block_expert = jnp.minimum(jnp.searchsorted(pad_ends, jnp.arange(n_blocks) * MOE_BLOCK, side='right'), N_EXPERTS - 1)

    def expert_block(args):
        toks, gts, e = args
        xb = t[toks]
        hid = jax.nn.silu(xb @ w_gate[e]) * (xb @ w_up[e])
        return (hid @ w_down[e]) * gts[:, None].astype(xb.dtype)

    y_rows = lax.map(expert_block, (row_tok.reshape(n_blocks, MOE_BLOCK), row_gate.reshape(n_blocks, MOE_BLOCK), block_expert))
    y = jnp.zeros((T, D), h.dtype).at[row_tok].add(y_rows.reshape(rows, D).astype(h.dtype))
    return y.reshape(Bsz, S, D)

def setup_inputs(seed: int = 0) -> dict:
    key = jax.random.key(seed)
    ks = iter(jax.random.split(key, 32))
    f32 = jnp.float32
    n_even = (DEPTH + 1) // 2
    n_odd = DEPTH // 2

    def normal(shape, scale):
        return jax.random.normal(next(ks), shape, f32) * scale

    def gain(shape):
        return 1.0 + normal(shape, 0.02)

    x = normal((BATCH, SEQ, D_MODEL), 1.0)
    start = jax.random.randint(next(ks), (BATCH, 1), 0, 4096, dtype=jnp.int32)
    positions = start + jnp.arange(SEQ, dtype=jnp.int32)[None, :]
    attn_norm = gain((n_even, D_MODEL))
    w_in_attn = normal((n_even, D_MODEL, ATTN_IN), D_MODEL ** -0.5)
    mla_q_norm = gain((n_even, MLA_Q_RANK))
    w_uq = normal((n_even, MLA_Q_RANK, MLA_HEADS * (MLA_NOPE + MLA_ROPE)), MLA_Q_RANK ** -0.5)
    mla_kv_norm = gain((n_even, MLA_KV_RANK))
    w_ukv = normal((n_even, MLA_KV_RANK, MLA_HEADS * (MLA_NOPE + MLA_V)), MLA_KV_RANK ** -0.5)
    w_out_attn = normal((n_even, MIX_A + MIX_B, D_MODEL), (MIX_A + MIX_B) ** -0.5)
    ssd_norm = gain((n_odd, D_MODEL))
    w_in_ssd = normal((n_odd, D_MODEL, SSD_IN), D_MODEL ** -0.5)
    conv_w = normal((n_odd, D_CONV, XBC_DIM), D_CONV ** -0.5)
    conv_b = normal((n_odd, XBC_DIM), 0.02)
    dt0 = jnp.exp(jax.random.uniform(next(ks), (n_odd, SSD_HEADS), f32, math.log(1e-3), math.log(1e-1)))
    dt_bias = dt0 + jnp.log(-jnp.expm1(-dt0))
    a_log = jnp.log(jax.random.uniform(next(ks), (n_odd, SSD_HEADS), f32, 1.0, 16.0))
    d_skip = gain((n_odd, SSD_HEADS))
    gate_norm = gain((n_odd, D_INNER))
    w_out_ssd = normal((n_odd, D_INNER, D_MODEL), D_INNER ** -0.5)
    moe_norm = gain((DEPTH, D_MODEL))
    w_group = normal((DEPTH, D_MODEL, N_GROUPS), D_MODEL ** -0.5)
    b_group = normal((DEPTH, N_GROUPS), 0.01)
    w_router = normal((DEPTH, D_MODEL, N_EXPERTS), D_MODEL ** -0.5)
    b_router = normal((DEPTH, N_EXPERTS), 0.01)
    w_gate = normal((DEPTH, N_EXPERTS, D_MODEL, D_EXPERT), D_MODEL ** -0.5)
    w_up = normal((DEPTH, N_EXPERTS, D_MODEL, D_EXPERT), D_MODEL ** -0.5)
    w_down = normal((DEPTH, N_EXPERTS, D_EXPERT, D_MODEL), D_EXPERT ** -0.5)
    final_norm = gain((D_MODEL,))
    return {'x': x, 'positions': positions, 'attn_norm': attn_norm, 'w_in_attn': w_in_attn,
            'mla_q_norm': mla_q_norm, 'w_uq': w_uq, 'mla_kv_norm': mla_kv_norm, 'w_ukv': w_ukv,
            'w_out_attn': w_out_attn, 'ssd_norm': ssd_norm, 'w_in_ssd': w_in_ssd, 'conv_w': conv_w,
            'conv_b': conv_b, 'dt_bias': dt_bias, 'a_log': a_log, 'd_skip': d_skip,
            'gate_norm': gate_norm, 'w_out_ssd': w_out_ssd, 'moe_norm': moe_norm,
            'w_group': w_group, 'b_group': b_group, 'w_router': w_router, 'b_router': b_router,
            'w_gate': w_gate, 'w_up': w_up, 'w_down': w_down, 'final_norm': final_norm}

def reference(x, positions, attn_norm, w_in_attn, mla_q_norm, w_uq, mla_kv_norm, w_ukv, w_out_attn,
              ssd_norm, w_in_ssd, conv_w, conv_b, dt_bias, a_log, d_skip, gate_norm, w_out_ssd,
              moe_norm, w_group, b_group, w_router, b_router, w_gate, w_up, w_down, final_norm):
    rope_a = rope_tables(positions, ROPE_DIM_A)
    rope_b = rope_tables(positions, MLA_ROPE)
    for layer in range(DEPTH):
        i = layer // 2
        if layer % 2 == 0:
            x = x + hybrid_attention_mixer(rmsnorm(x, attn_norm[i]), rope_a, rope_b, w_in_attn[i],
                                           mla_q_norm[i], w_uq[i], mla_kv_norm[i], w_ukv[i], w_out_attn[i])
        else:
            x = x + ssd_mixer(rmsnorm(x, ssd_norm[i]), w_in_ssd[i], conv_w[i], conv_b[i], dt_bias[i],
                              a_log[i], d_skip[i], gate_norm[i], w_out_ssd[i])
        x = x + hierarchical_moe(rmsnorm(x, moe_norm[layer]), w_group[layer], b_group[layer],
                                 w_router[layer], b_router[layer], w_gate[layer], w_up[layer], w_down[layer])
    return rmsnorm(x, final_norm)


_drawn_inputs = setup_inputs


def setup_inputs(seed=0):
    import zlib

    import numpy as np

    out = dict(_drawn_inputs(seed))
    spreads = {}
    factors = {'attn_norm': 2.995,
     'mla_q_norm': 7.372,
     'd_skip': 160.935,
     'final_norm': 21.901,
     'mla_kv_norm': 3.864,
     'ssd_norm': 3.633,
     'conv_b': 4.314,
     'gate_norm': 5.209,
     'moe_norm': 2.783,
     'b_group': 7.535,
     'b_router': 5.154}
    for name, (base, spread) in spreads.items():
        noise = np.random.default_rng([zlib.crc32(name.encode()), seed]).standard_normal(out[name].shape)
        drawn = base * np.exp(spread * noise) if base else spread * noise
        out[name] = jnp.asarray(drawn.astype(out[name].dtype))
    for name, factor in factors.items():
        out[name] = (out[name] * factor).astype(out[name].dtype)
    return out
```

```python
import math
from contextlib import ExitStack

import numpy as np

import concourse.bass as bass
from concourse import mybir

F32 = mybir.dt.float32
I32 = mybir.dt.int32
ALU = mybir.AluOpType
ACT = mybir.ActivationFunctionType
AX = mybir.AxisListType

P = 128
D = 1024
S = 1024
NT = S // P
ND = D // P
HALF = 512
EPS = 1e-6
NEG = -1e30

HA, DH, ROPE_A = 8, 64, 16
HB, NOPE, ROPE_B, DV = 8, 64, 32, 64
KB = NOPE + ROPE_B
QR, KVR = 256, 128
MIX_A = HA * DH
ATTN_IN = 3 * MIX_A + QR + KVR + ROPE_B
THETA = 500000.0
BRANCHES = ((128, 1), (512, 4), (2048, 16))

DI, HS, G, N, HD = 2048, 32, 4, 128, 64
HG = HS // G
XBC = DI + 2 * G * N
SSD_IN = DI + XBC + HS
CONV = 4

NG, EPG, NE, DE = 4, 8, 32, 512
NL = NG + NE
NBLK = NE + 2 * S // P
MAGIC = 1.5 * 2.0 ** 23

V_ATTN, V_MOE, V_SSD = 0, ND, 3 * ND
V_QN = 4 * ND
V_KVN = V_QN + QR // P
V_GATE = V_KVN + 1
V_BR = V_GATE + DI // P
V_DTB = V_BR + 2 * NL
V_ALOG = V_DTB + HS
V_DSKIP = V_ALOG + HS
NV = V_DSKIP + HS

C_ID = 0
C_MASKA = C_ID + P
C_MASKB = C_MASKA + S
C_UPPER = C_MASKB + S
C_STRICT = C_UPPER + P
C_ROTA = C_STRICT + P
C_ROTB = C_ROTA + P
C_ONES = C_ROTB + KB
C_IOTA = C_ONES + P
C_TOK = C_IOTA + P
C_FA = C_TOK + NT
C_FB = C_FA + 1
C_DESC = C_FB + 1
C_GDESC = C_DESC + EPG
C_BLK = C_GDESC + NG
NC_ = C_BLK + (NBLK - NE)


def constants():
    c = np.zeros((P, NC_), np.float32)
    c[:, C_ID:C_ID + P] = np.eye(P)
    q = np.arange(P)[:, None]
    dist = q + (S - P) - np.arange(S)[None, :]
    many = sum(((dist >= 0) & (dist <= w) & (dist % d == 0)).astype(np.float64) for w, d in BRANCHES)
    c[:, C_MASKA:C_MASKA + S] = np.where(many > 0, np.log(np.maximum(many, 1)), NEG)
    c[:, C_MASKB:C_MASKB + S] = np.where(dist >= 0, 0.0, NEG)
    i = np.arange(P)[None, :]
    c[:, C_UPPER:C_UPPER + P] = q <= i
    c[:, C_STRICT:C_STRICT + P] = q < i

    def rotation(size, starts, half):
        r = np.zeros((size, size), np.float32)
        for s in starts:
            for n in range(half):
                r[s + half + n, s + n] = -1.0
                r[s + n, s + half + n] = 1.0
        return r

    c[:, C_ROTA:C_ROTA + P] = rotation(P, (0, DH), ROPE_A // 2)
    c[:KB, C_ROTB:C_ROTB + KB] = rotation(KB, (0,), ROPE_B // 2)
    c[:, C_ONES:C_ONES + P] = 1.0
    c[:, C_IOTA:C_IOTA + P] = i
    c[:, C_TOK:C_TOK + NT] = q + P * np.arange(NT)[None, :]

    def frequencies(rot):
        return (np.float32(THETA) ** (-np.arange(0, rot, 2, dtype=np.float32) / np.float32(rot))).astype(np.float32)

    for s in (0, DH):
        c[s:s + ROPE_A, C_FA] = np.tile(frequencies(ROPE_A), 2)
    c[:ROPE_B, C_FB] = np.tile(frequencies(ROPE_B), 2)
    c[:, C_DESC:C_DESC + EPG] = EPG - np.arange(EPG)
    c[:, C_GDESC:C_GDESC + NG] = NG - np.arange(NG)
    c[:, C_BLK:C_BLK + NBLK - NE] = np.arange(NBLK - NE)
    return c


PRIMED = 1


class Stage:

    def __init__(self, nc, name):
        self.nc, self.name, self.ctx, self.sems, self.loop_sems = nc, name, ExitStack(), [], []

    def __enter__(self):
        return self

    def sb(self, name, shape, dt=F32):
        return self.ctx.enter_context(self.nc.sbuf_tensor(f"{self.name}_{name}", shape, dt))

    def ps(self, name, shape, dt=F32):
        return self.ctx.enter_context(self.nc.psum_tensor(f"{self.name}_{name}", shape, dt))

    def sem(self, name, primed=True):
        s = self.nc.alloc_semaphore(f"{self.name}_{name}")
        self.sems.append(s)
        if primed:
            self.loop_sems.append(s)
        return s

    def primed_block(self):
        for s in self.loop_sems:
            self.nc.sync.sem_inc(s, PRIMED)
        self.nc.all_engine_barrier()
        return self.ctx.enter_context(self.nc.Block())

    def __exit__(self, kind, *rest):
        self.ctx.close()
        if kind is None:
            self.nc.clear_and_free_semaphores(self.sems)
            self.nc.all_engine_barrier()


class Names:
    pass


class Chain:

    def __init__(self, eng, sem, base=0):
        self.eng, self.sem, self.base, self.n = eng, sem, base, 0

    def __call__(self, ins):
        self.n += 1
        ins.then_inc(self.sem, 1)
        self.eng.wait_ge(self.sem, self.base + self.n)


def load_stage(nc, K, A):
    with Stage(nc, "load") as st:
        loaded, chain, angle, sine = st.sem("loaded"), st.sem("chain"), st.sem("angle"), st.sem("sine")
        pos = st.sb("pos", [P, S], I32)
        ang, turns, *r = (K.B3[:, n, :] for n in range(6))
        block = st.ctx.enter_context(nc.Block())

        @block.sync
        def _(sp):
            sp.dma_start(pos[:, :], A["positions"].partition_broadcast(P)).then_inc(loaded, 16)
            sp.dma_start(K.consts[:, :], A["consts"]).then_inc(loaded, 16)
            sp.dma_start(K.vecs[:, :], A["vecs"]).then_inc(loaded, 16)
            sp.dma_start(K.X[:, :, :], A["x"].rearrange("(t p) d -> p t d", p=P)).then_inc(loaded, 16)

        @block.vector
        def _(dve):
            step = Chain(dve, chain)
            dve.wait_ge(loaded, 64)
            for n, (size, freq) in enumerate(((P, C_FA), (KB, C_FB))):
                a, k = ang[0:size, :], turns[0:size, :]
                red, cos_arg = r[2 * n][0:size, :], r[2 * n + 1][0:size, :]
                step(nc.vector.tensor_copy(a, pos[0:size, :]))
                step(nc.vector.tensor_scalar(a, a, K.consts[0:size, freq:freq + 1], None, ALU.mult))
                step(nc.vector.tensor_scalar(k, a, 1 / (2 * math.pi), MAGIC, ALU.mult, ALU.add))
                step(nc.vector.tensor_scalar(k, k, MAGIC, None, ALU.subtract))
                c1 = 6.28125
                c2 = float(np.float32(round((2 * math.pi - c1) * 2 ** 21) / 2 ** 21))
                c3 = float(np.float32(2 * math.pi - c1 - c2))
                step(nc.vector.scalar_tensor_tensor(out=a, in0=k, scalar=-c1, in1=a, op0=ALU.mult, op1=ALU.add))
                step(nc.vector.scalar_tensor_tensor(out=a, in0=k, scalar=-c2, in1=a, op0=ALU.mult, op1=ALU.add))
                step(nc.vector.scalar_tensor_tensor(out=a, in0=k, scalar=-c3, in1=a, op0=ALU.mult, op1=ALU.add))
                pi = 3.1415925
                step(nc.vector.tensor_scalar(red, a, pi, -pi, ALU.min, ALU.max))
                step(nc.vector.scalar_tensor_tensor(out=a, in0=red, scalar=-1.0, in1=red, op0=ALU.mult, op1=ALU.max))
                nc.vector.tensor_scalar(cos_arg, a, -1.0, math.pi / 2, ALU.mult, ALU.add).then_inc(angle, 1)
                dve.wait_ge(angle, n + 1)

        @block.scalar
        def _(act):
            for n, (size, c, s) in enumerate(((P, K.cosA, K.sinA), (KB, K.cosB, K.sinB))):
                act.wait_ge(angle, n + 1)
                nc.scalar.activation(s[0:size, :], r[2 * n][0:size, :], ACT.Sin)
                nc.scalar.activation(c[0:size, :], r[2 * n + 1][0:size, :], ACT.Sin).then_inc(sine, 1)


def norm_stage(nc, K, gain, name, hn_dram=None, final=None, prefetch=None):
    with Stage(nc, name) as st:
        loaded, squares, mean, root, rstd_ok = (st.sem(n) for n in ("loaded", "squares", "mean", "root", "rstd_ok"))
        rows, turned, kept = (st.sem(n) for n in ("rows", "turned", "kept"))
        stored = [st.sem(f"stored{a}") for a in range(2)]
        junk = st.sb("junk", [P, 2, D])
        ss, rstd = st.sb("ss", [P, NT]), st.sb("rstd", [P, NT])
        hn = [st.sb(f"hn{a}", [P, D]) for a in range(2)]
        gf = st.sb("gf", [P, D]) if final is not None else None
        tp = [st.ps(f"tp{a}", [P, ND, P]) for a in range(2)]
        block = st.ctx.enter_context(nc.Block())

        @block.vector
        def _(dve):
            for t in range(NT):
                if t >= 2:
                    dve.wait_ge(squares, t - 1)
                nc.vector.tensor_tensor_reduce(junk[:, t % 2, :], K.X[:, t, :], K.X[:, t, :], 1.0, 0.0, ALU.mult,
                                               ALU.add, ss[:, t:t + 1]).then_inc(squares, 1)
            dve.wait_ge(squares, NT)
            nc.vector.tensor_scalar(ss[:, :], ss[:, :], 1.0 / D, EPS, ALU.mult, ALU.add).then_inc(mean, 1)
            dve.wait_ge(root, 1)
            nc.vector.reciprocal(rstd[:, :], ss[:, :]).then_inc(rstd_ok, 1)
            if final is not None:
                dve.wait_ge(loaded, 16)
            for t in range(NT):
                if final is not None:
                    dve.wait_ge(rows, t + 1)
                    nc.vector.tensor_tensor(hn[t % 2][:, :], hn[t % 2][:, :], gf[:, :], ALU.mult).then_inc(kept, 1)
                    continue
                dve.wait_ge(turned, t + 1)
                g = K.vecs[:, gain:gain + ND].unsqueeze(2).to_broadcast([P, ND, P])
                nc.vector.tensor_tensor(K.B1[:, :, t * P:(t + 1) * P], tp[t % 2][:, :, :], g, ALU.mult).then_inc(kept, 1)

        @block.scalar
        def _(act):
            act.wait_ge(mean, 1)
            nc.scalar.activation(ss[:, :], ss[:, :], ACT.Sqrt).then_inc(root, 1)
            act.wait_ge(rstd_ok, 1)
            for t in range(NT):
                if t >= 2:
                    if final is None:
                        act.wait_ge(turned, t - 1)
                    if final is not None or hn_dram is not None:
                        act.wait_ge(stored[t % 2], 16 * (t // 2))
                nc.scalar.activation(hn[t % 2][:, :], K.X[:, t, :], ACT.Copy, scale=rstd[:, t:t + 1]).then_inc(rows, 1)

        @block.tensor
        def _(pe):
            if final is not None:
                return
            for t in range(NT):
                pe.wait_ge(rows, t + 1)
                if t >= 2:
                    pe.wait_ge(kept, t - 1)
                for j in range(ND):
                    last = nc.tensor.transpose(tp[t % 2][:, j, :], hn[t % 2][:, j * P:(j + 1) * P], K.ident)
                last.then_inc(turned, 1)

        @block.sync
        def _(sp):
            if final is not None:
                sp.dma_start(gf[:, :], final.partition_broadcast(P)).then_inc(loaded, 16)
            if prefetch is not None:
                prefetch(sp)
            dram = K.out if final is not None else hn_dram
            if dram is None:
                return
            for t in range(NT):
                sp.wait_ge(kept if final is not None else rows, t + 1)
                sp.dma_start(dram[t * P:(t + 1) * P, :], hn[t % 2][:, :]).then_inc(stored[t % 2], 16)
            for a in range(2):
                sp.wait_ge(stored[a], 16 * (NT // 2))
            sp.nop()


def qk_stage(nc, K, A):
    with Stage(nc, "qk") as st:
        SETS = range(2)
        w = [st.sb(f"w{s}", [P, ND, P]) for s in SETS]
        raw, t1, res = ([K.B2[:, 2 * n + s, :] for s in SETS] for n in range(3))
        prj = [st.ps(f"prj{s}", [P, S]) for s in SETS]
        rot = [st.ps(f"rot{s}", [P, S]) for s in SETS]
        wl, pd, rd, td, ro, st_ = ([st.sem(f"{n}{s}") for s in SETS] for n in
                                   ("w_loaded", "projected", "raw_ready", "turned", "rope_steps", "stored"))
        zeroed, filled = st.sem("zeroed"), st.sem("filled", primed=False)
        block = st.primed_block()
        win = A["w_in_attn"].rearrange("(k p) n -> p k n", p=P)
        dst = [x.rearrange("(i a) r n -> i (a r) n", a=2) for x in (K.QA, K.KA)]
        zeros = K.B2[:, 6, :]

        @block.gpsimd
        def _(pool):
            nc.gpsimd.memset(zeros, 0.0).then_inc(zeroed, 1)
            pool.wait_ge(zeroed, 1 + PRIMED)
            for b in range(NE, NBLK):
                pool.dma_start(K.Y[b * P:(b + 1) * P, :], zeros).then_inc(filled, 16)
            pool.wait_ge(filled, 16 * (NBLK - NE))
            pool.nop()

        @block.sync
        def _(sp):
            with sp.Fori(0, HA // 2) as i:
                for s in SETS:
                    sp.wait_ge(pd[s], i + PRIMED)
                    sp.dma_start(w[s][:, :, :], win[:, :, bass.ds(i * P + s * MIX_A, P)]).then_inc(wl[s], 16)

        @block.tensor
        def _(pe):
            with pe.Fori(0, HA // 2) as i:
                for s in SETS:
                    pe.wait_ge(wl[s], (i + 1) * 16 + PRIMED)
                    pe.wait_ge(rd[s], i + PRIMED)
                    for h in range(2):
                        for k in range(ND):
                            last = nc.tensor.matmul(prj[s][:, h * HALF:(h + 1) * HALF], w[s][:, k, :],
                                                    K.B1[:, k, h * HALF:(h + 1) * HALF], start=(k == 0), stop=(k == ND - 1))
                    last.then_inc(pd[s], 1)
                for s in SETS:
                    pe.wait_ge(rd[s], i + 1 + PRIMED)
                    pe.wait_ge(ro[s], i * 4 + PRIMED)
                    for h in range(2):
                        last = nc.tensor.matmul(rot[s][:, h * HALF:(h + 1) * HALF], K.rotA, raw[s][:, h * HALF:(h + 1) * HALF],
                                                start=True, stop=True)
                    last.then_inc(td[s], 1)

        @block.scalar
        def _(act):
            with act.Fori(0, HA // 2) as i:
                for s in SETS:
                    act.wait_ge(pd[s], i + 1 + PRIMED)
                    act.wait_ge(ro[s], i * 4 + PRIMED)
                    nc.scalar.activation(raw[s], prj[s][:, :], ACT.Copy,
                                         scale=DH ** -0.5 if s == 0 else 1.0).then_inc(rd[s], 1)
                for s in SETS:
                    act.wait_ge(ro[s], i * 4 + 4 + PRIMED)
                    act.dma_start(dst[s][bass.ds(i, 1)].rearrange("a p n -> p (a n)"), res[s]).then_inc(st_[s], 16)
            for s in SETS:
                act.wait_ge(st_[s], 16 * (HA // 2) + PRIMED)
            act.nop()

        @block.vector
        def _(dve):
            with dve.Fori(0, HA // 2) as i:
                for s in SETS:
                    dve.wait_ge(rd[s], i + 1 + PRIMED)
                    nc.vector.tensor_tensor(t1[s], raw[s], K.cosA[:, :], ALU.mult).then_inc(ro[s], 1)
                    dve.wait_ge(td[s], i + 1 + PRIMED)
                    dve.wait_ge(st_[s], i * 16 + PRIMED)
                    nc.vector.tensor_tensor(res[s], rot[s][:, :], K.sinA[:, :], ALU.mult).then_inc(ro[s], 1)
                    dve.wait_ge(ro[s], i * 4 + 2 + PRIMED)
                    nc.vector.tensor_tensor(res[s], res[s], t1[s], ALU.add).then_inc(ro[s], 2)


def v_stage(nc, K, A):
    LOW = QR + KVR + ROPE_B
    with Stage(nc, "v") as st:
        wv, wl = st.sb("wv", [P, ND, MIX_A]), st.sb("wl", [P, ND, LOW])
        low = [st.sb(f"low{a}", [P, LOW]) for a in range(2)]
        junk, junk2 = st.sb("junk", [P, QR]), st.sb("junk2", [P, KVR])
        ss, rstd = st.sb("ss", [P, 2 * NT]), st.sb("rstd", [P, 2 * NT])
        pv = [st.ps(f"pv{a}", [P, MIX_A]) for a in range(2)]
        pl = [st.ps(f"pl{a}", [P, LOW]) for a in range(2)]
        tp = [st.ps(f"tp{a}", [P, 4, P]) for a in range(2)]
        loaded, loaded2, vdone, ldone, vkept, lkept, sq, sc, root, td, tk = (st.sem(n) for n in (
            "wv_loaded", "wl_loaded", "v_done", "low_done", "v_kept", "low_kept", "squares", "scaled", "root", "turned", "turn_kept"))
        block = st.ctx.enter_context(nc.Block())
        win = A["w_in_attn"].rearrange("(k p) n -> p k n", p=P)

        @block.sync
        def _(sp):
            sp.dma_start(wv[:, :, :], win[:, :, 2 * MIX_A:3 * MIX_A]).then_inc(loaded, 16)
            sp.dma_start(wl[:, :, :], win[:, :, 3 * MIX_A:ATTN_IN]).then_inc(loaded2, 16)

        @block.tensor
        def _(pe):
            def turn(t):
                pe.wait_ge(sc, 4 * t + 4)
                if t >= 2:
                    pe.wait_ge(tk, 3 * (t - 1))
                for j in range(3):
                    nc.tensor.transpose(tp[t % 2][:, j, :], low[t % 2][:, j * P:(j + 1) * P], K.ident)
                nc.tensor.transpose(tp[t % 2][0:ROPE_B, 3, :], low[t % 2][:, QR + KVR:LOW], K.ident).then_inc(td, 1)

            for t in range(NT):
                pe.wait_ge(loaded, 16)
                if t >= 2:
                    pe.wait_ge(vkept, t - 1)
                for k in range(ND):
                    last = nc.tensor.matmul(pv[t % 2][:, :], K.B1[:, k, t * P:(t + 1) * P], wv[:, k, :], start=(k == 0), stop=(k == ND - 1))
                last.then_inc(vdone, 1)
                if t >= 1:
                    turn(t - 1)
                pe.wait_ge(loaded2, 16)
                if t >= 2:
                    pe.wait_ge(lkept, t - 1)
                for k in range(ND):
                    last = nc.tensor.matmul(pl[t % 2][:, :], K.B1[:, k, t * P:(t + 1) * P], wl[:, k, :], start=(k == 0), stop=(k == ND - 1))
                last.then_inc(ldone, 1)
            turn(NT - 1)

        @block.scalar
        def _(act):
            for t in range(NT):
                act.wait_ge(vdone, t + 1)
                nc.scalar.activation(K.B3[:, t, 0:MIX_A], pv[t % 2][:, :], ACT.Copy).then_inc(vkept, 1)
                act.wait_ge(ldone, t + 1)
                if t >= 2:
                    act.wait_ge(td, t - 1)
                nc.scalar.activation(low[t % 2][:, :], pl[t % 2][:, :], ACT.Copy).then_inc(lkept, 1)
                act.wait_ge(sq, 4 * t + 4)
                nc.scalar.activation(rstd[:, 2 * t:2 * t + 2], ss[:, 2 * t:2 * t + 2], ACT.Sqrt).then_inc(root, 1)

        @block.vector
        def _(dve):
            for t in range(NT):
                a, c = t % 2, 2 * t
                dve.wait_ge(lkept, t + 1)
                if t:
                    dve.wait_ge(sq, 4 * t)
                nc.vector.tensor_tensor_reduce(junk[:, 0:QR], low[a][:, 0:QR], low[a][:, 0:QR], 1.0, 0.0, ALU.mult, ALU.add,
                                               ss[:, c:c + 1]).then_inc(sq, 1)
                nc.vector.tensor_tensor_reduce(junk2[:, :], low[a][:, QR:QR + KVR], low[a][:, QR:QR + KVR], 1.0, 0.0, ALU.mult,
                                               ALU.add, ss[:, c + 1:c + 2]).then_inc(sq, 1)
                dve.wait_ge(sq, 4 * t + 2)
                nc.vector.tensor_scalar(ss[:, c:c + 1], ss[:, c:c + 1], 1.0 / QR, EPS, ALU.mult, ALU.add).then_inc(sq, 1)
                nc.vector.tensor_scalar(ss[:, c + 1:c + 2], ss[:, c + 1:c + 2], 1.0 / KVR, EPS, ALU.mult, ALU.add).then_inc(sq, 1)
                dve.wait_ge(root, t + 1)
                nc.vector.reciprocal(rstd[:, c:c + 2], rstd[:, c:c + 2]).then_inc(sc, 1)
                dve.wait_ge(sc, 4 * t + 1)
                nc.vector.tensor_scalar(low[a][:, 0:QR], low[a][:, 0:QR], rstd[:, c:c + 1], None, ALU.mult).then_inc(sc, 1)
                nc.vector.tensor_scalar(low[a][:, QR:QR + KVR], low[a][:, QR:QR + KVR], rstd[:, c + 1:c + 2], None, ALU.mult).then_inc(sc, 2)
                dve.wait_ge(td, t + 1)
                g = K.vecs[:, V_QN:V_QN + 3].unsqueeze(2).to_broadcast([P, 3, P])
                nc.vector.tensor_tensor(K.lowT[:, :, t * P:(t + 1) * P], tp[a][:, 0:3, :], g, ALU.mult).then_inc(tk, 1)
                nc.vector.tensor_copy(K.krT[:, t * P:(t + 1) * P], tp[a][0:ROPE_B, 3, :]).then_inc(tk, 2)


def mla_stage(nc, K, A):
    with Stage(nc, "mla") as st:
        wq, wkv = st.sb("wq", [P, QR // P, HB * KB]), st.sb("wkv", [P, HB, NOPE + DV])
        raw, t1, res, kn = ([K.B2[0:r, 2 * n + a, :] for a in range(2)] for n, r in enumerate((KB, KB, KB, NOPE)))
        prj, rot = st.ps("prj", [P, S]), st.ps("rot", [P, S])
        pk = st.ps("pk", [P, S])
        pv = [st.ps(f"pv{a}", [P, HB * DV]) for a in range(2)]
        loaded, projected, raw_ok, turned, ro, shared, kdone, kkept, vdone, vkept = (st.sem(n) for n in (
            "loaded", "projected", "raw_ready", "turned", "rope_steps", "shared_stored", "k_done", "k_kept", "v_done", "v_kept"))
        stored = [st.sem(f"stored{a}") for a in range(2)]
        kstored = [st.sem(f"k_stored{a}") for a in range(2)]
        block = st.ctx.enter_context(nc.Block())

        @block.sync
        def _(sp):
            sp.dma_start(wq[:, :, :], A["w_uq"].rearrange("(k p) n -> p k n", p=P)).then_inc(loaded, 16)
            sp.dma_start(wkv[:, :, :], A["w_ukv"].rearrange("p (h n) -> p h n", h=HB)).then_inc(loaded, 16)
            for n in range(HB + 1):
                sp.wait_ge(ro, 4 * n + 4)
                if n == 0:
                    for h in range(HB):
                        sp.dma_start(K.KB[h, 0:ROPE_B, :], res[0][0:ROPE_B, :]).then_inc(shared, 16)
                    continue
                sp.dma_start(K.QB[n - 1, :, :], res[n % 2][:, :]).then_inc(stored[n % 2], 16)
                sp.wait_ge(kkept, n)
                sp.dma_start(K.KB[n - 1, ROPE_B:KB, :], kn[n % 2][:, :]).then_inc(kstored[n % 2], 16)
            sp.wait_ge(shared, 16 * HB)
            for a in range(2):
                sp.wait_ge(stored[a], 16 * (HB // 2))
                sp.wait_ge(kstored[a], 16 * (HB // 2))
            sp.nop()

        @block.tensor
        def _(pe):
            pe.wait_ge(loaded, 32)
            for n in range(HB + 1):
                rows = ROPE_B if n == 0 else KB
                if n:
                    h = n - 1
                    pe.wait_ge(raw_ok, n)
                    for half in range(2):
                        for k in range(QR // P):
                            last = nc.tensor.matmul(prj[0:KB, half * HALF:(half + 1) * HALF], wq[:, k, h * KB:(h + 1) * KB],
                                                    K.lowT[:, k, half * HALF:(half + 1) * HALF], start=(k == 0), stop=(k == 1))
                    last.then_inc(projected, 1)
                    if n >= 2:
                        pe.wait_ge(kkept, n - 1)
                    for half in range(2):
                        last = nc.tensor.matmul(pk[0:NOPE, half * HALF:(half + 1) * HALF], wkv[:, h, 0:NOPE],
                                                K.lowT[:, 2, half * HALF:(half + 1) * HALF], start=True, stop=True)
                    last.then_inc(kdone, 1)
                    t = n - 1
                    if t >= 2:
                        pe.wait_ge(vkept, t - 1)
                    nc.tensor.matmul(pv[t % 2][:, :], K.lowT[:, 2, t * P:(t + 1) * P], wkv[:, :, NOPE:NOPE + DV],
                                     start=True, stop=True).then_inc(vdone, 1)
                pe.wait_ge(raw_ok, n + 1)
                if n:
                    pe.wait_ge(ro, 4 * n)
                for half in range(2):
                    last = nc.tensor.matmul(rot[0:rows, half * HALF:(half + 1) * HALF], K.rotB[0:rows, 0:rows],
                                            raw[n % 2][0:rows, half * HALF:(half + 1) * HALF], start=True, stop=True)
                last.then_inc(turned, 1)

        @block.scalar
        def _(act):
            nc.scalar.activation(raw[0][0:ROPE_B, :], K.krT[:, :], ACT.Copy).then_inc(raw_ok, 1)
            for n in range(1, HB + 1):
                act.wait_ge(projected, n)
                if n >= 2:
                    act.wait_ge(ro, 4 * (n - 1))
                nc.scalar.activation(raw[n % 2][:, :], prj[0:KB, :], ACT.Copy, scale=KB ** -0.5).then_inc(raw_ok, 1)
                act.wait_ge(kdone, n)
                if n >= 3:
                    act.wait_ge(kstored[n % 2], 16 * ((n - 1) // 2))
                nc.scalar.activation(kn[n % 2][:, :], pk[0:NOPE, :], ACT.Copy).then_inc(kkept, 1)
                act.wait_ge(vdone, n)
                nc.scalar.activation(K.B3[:, n - 1, MIX_A:], pv[(n - 1) % 2][:, :], ACT.Copy).then_inc(vkept, 1)

        @block.vector
        def _(dve):
            for n in range(HB + 1):
                rows, a = ROPE_B if n == 0 else KB, n % 2
                dve.wait_ge(raw_ok, n + 1)
                nc.vector.tensor_tensor(t1[a][0:rows, :], raw[a][0:rows, :], K.cosB[0:rows, :], ALU.mult).then_inc(ro, 1)
                dve.wait_ge(turned, n + 1)
                if n == 2:
                    dve.wait_ge(shared, 16 * HB)
                if n >= 3:
                    dve.wait_ge(stored[n % 2], 16 * ((n - 1) // 2))
                nc.vector.tensor_tensor(res[a][0:rows, :], rot[0:rows, :], K.sinB[0:rows, :], ALU.mult).then_inc(ro, 1)
                dve.wait_ge(ro, 4 * n + 2)
                nc.vector.tensor_tensor(res[a][0:rows, :], res[a][0:rows, :], t1[a][0:rows, :], ALU.add).then_inc(ro, 2)


def attention_stage(nc, K, name, rows, q_dram, k_dram, mask, first_head):
    HEADS = 8
    TILES = [(a, t) for a in range(2) for t in range(NT)]
    NN = len(TILES)
    with Stage(nc, name) as st:
        q = [st.sb(f"q{a}", [rows, S]) for a in range(2)]
        k = [st.sb(f"k{a}", [rows, S]) for a in range(2)]
        sm = [st.sb(f"sm{a}", [P, S]) for a in range(2)]
        pr = [st.sb(f"pr{a}", [P, S]) for a in range(2)]
        pT = [st.sb(f"pT{a}", [P, NT, P]) for a in range(2)]
        mx, nmx, den, rden, spare = (st.sb(n, [P, 2]) for n in ("mx", "nmx", "den", "rden", "spare"))
        sc = [st.ps(f"sc{a}", [P, S]) for a in range(2)]
        tp = [st.ps(f"tp{a}", [P, 4, P]) for a in range(2)]
        ov = [st.ps(f"ov{a}", [P, DH]) for a in range(2)]
        loaded = [st.sem(f"loaded{a}") for a in range(2)]
        scored, masked, negated, exped, t_lo, t_hi, lo_kept, hi_kept, summed, recip, out_ok = (st.sem(n) for n in (
            "scored", "masked", "negated", "exped", "turned_low", "turned_high", "low_kept", "high_kept", "summed", "recip", "out_ready"))
        block = st.primed_block()
        high = [sum(t >= 4 for _, t in TILES[:n]) for n in range(NN + 1)]

        @block.sync
        def _(sp):
            def load(i, a):
                for buf, dram in ((q[a], q_dram), (k[a], k_dram)):
                    src = dram[bass.ds(i * 2 + a, 1)].rearrange("a r n -> r (a n)")
                    sp.dma_start(buf[:, :], src).then_inc(loaded[a], 16)

            for a in range(2):
                load(0, a)
            with sp.Fori(0, HEADS // 2 - 1) as i:
                for a in range(2):
                    sp.wait_ge(scored, i * NN + (a + 1) * NT + PRIMED)
                    load(i + 1, a)

        @block.tensor
        def _(pe):
            with pe.Fori(0, HEADS // 2) as i:
                base, hbase = i * NN, i * high[NN]

                def scores(n):
                    a, t = TILES[n]
                    if t == 0:
                        pe.wait_ge(loaded[a], i * 32 + 32 + PRIMED)
                    if n >= 2:
                        pe.wait_ge(masked, base + n - 1 + PRIMED)
                    else:
                        pe.wait_ge(masked, base + PRIMED)
                    w = (t + 1) * P
                    for c in range(0, w, HALF):
                        e = min(c + HALF, w)
                        last = nc.tensor.matmul(sc[n % 2][:, c:e], q[a][:, t * P:(t + 1) * P], k[a][:, c:e], start=True, stop=True)
                    last.then_inc(scored, 1)

                def turn(n):
                    _, t = TILES[n]
                    pe.wait_ge(exped, base + n + 1 + PRIMED)
                    pe.wait_ge(lo_kept, base + n + PRIMED)
                    for j in range(min(t + 1, 4)):
                        last = nc.tensor.transpose(tp[0][:, j, :], pr[n % 2][:, j * P:(j + 1) * P], K.ident)
                    last.then_inc(t_lo, 1)
                    if t >= 4:
                        pe.wait_ge(hi_kept, hbase + high[n] + PRIMED)
                        for j in range(4, t + 1):
                            last = nc.tensor.transpose(tp[1][:, j - 4, :], pr[n % 2][:, j * P:(j + 1) * P], K.ident)
                        last.then_inc(t_hi, 1)

                def weigh(n):
                    a, t = TILES[n]
                    pe.wait_ge(lo_kept, base + n + 1 + PRIMED)
                    if t >= 4:
                        pe.wait_ge(hi_kept, hbase + high[n + 1] + PRIMED)
                    if n >= 2:
                        pe.wait_ge(out_ok, base + n - 1 + PRIMED)
                    else:
                        pe.wait_ge(out_ok, base + PRIMED)
                    for j in range(t + 1):
                        v = K.B3[:, j, bass.ds((i * 2 + (a + first_head)) * DH, DH)]
                        last = nc.tensor.matmul(ov[n % 2][:, :], pT[n % 2][:, j, :], v, start=(j == 0), stop=(j == t))
                    last.then_inc(summed, 1)

                scores(0)
                for n in range(NN):
                    if n + 1 < NN:
                        scores(n + 1)
                    if n >= 1:
                        weigh(n - 1)
                    turn(n)
                weigh(NN - 1)

        @block.vector
        def _(dve):
            with dve.Fori(0, HEADS // 2) as i:
                base, hbase = i * NN, i * high[NN]

                def keep_low(n):
                    _, t = TILES[n]
                    dve.wait_ge(t_lo, base + n + 1 + PRIMED)
                    dve.wait_ge(summed, (base + n - 1 if n >= 2 else base) + PRIMED)
                    c = min(t + 1, 4)
                    nc.vector.tensor_copy(pT[n % 2][:, 0:c, :], tp[0][:, 0:c, :]).then_inc(lo_kept, 1)

                def invert(n):
                    dve.wait_ge(exped, base + n + 1 + PRIMED)
                    if n >= 2:
                        dve.wait_ge(out_ok, base + n - 1 + PRIMED)
                    else:
                        dve.wait_ge(out_ok, base + PRIMED)
                    nc.vector.reciprocal(rden[:, n % 2:n % 2 + 1], den[:, n % 2:n % 2 + 1]).then_inc(recip, 1)

                for n, (a, t) in enumerate(TILES):
                    w = (t + 1) * P
                    dve.wait_ge(scored, base + n + 1 + PRIMED)
                    dve.wait_ge(exped, (base + n - 1 if n >= 2 else base) + PRIMED)
                    if n >= 2:
                        invert(n - 2)
                    else:
                        nc.vector.memset(spare[:, n:n + 1], 0.0)
                    nc.vector.tensor_tensor_reduce(sm[n % 2][:, 0:w], sc[n % 2][:, 0:w], mask[:, S - w:S], 1.0, NEG, ALU.add, ALU.max,
                                                   mx[:, n % 2:n % 2 + 1]).then_inc(masked, 1)
                    dve.wait_ge(masked, base + n + 1 + PRIMED)
                    nc.vector.tensor_scalar(nmx[:, n % 2:n % 2 + 1], mx[:, n % 2:n % 2 + 1], -1.0, None, ALU.mult).then_inc(negated, 1)
                    if n >= 1:
                        keep_low(n - 1)
                invert(NN - 2)
                keep_low(NN - 1)
                invert(NN - 1)

        @block.scalar
        def _(act):
            with act.Fori(0, HEADS // 2) as i:
                base, hbase = i * NN, i * high[NN]

                def finish(n):
                    a, t = TILES[n]
                    act.wait_ge(summed, base + n + 1 + PRIMED)
                    act.wait_ge(recip, base + n + 1 + PRIMED)
                    o = K.B2[:, t, bass.ds((i * 2 + (a + first_head)) * DH, DH)]
                    nc.scalar.activation(o, ov[n % 2][:, :], ACT.Copy, scale=rden[:, n % 2:n % 2 + 1]).then_inc(out_ok, 1)

                def keep_high(n):
                    _, t = TILES[n]
                    if t >= 4:
                        act.wait_ge(t_hi, hbase + high[n + 1] + PRIMED)
                        act.wait_ge(summed, (base + n - 1 if n >= 2 else base) + PRIMED)
                        nc.scalar.activation(pT[n % 2][:, 4:t + 1, :], tp[1][:, 0:t - 3, :], ACT.Copy).then_inc(hi_kept, 1)

                for n, (a, t) in enumerate(TILES):
                    w = (t + 1) * P
                    act.wait_ge(negated, base + n + 1 + PRIMED)
                    if n >= 2:
                        act.wait_ge(t_lo, base + n - 1 + PRIMED)
                        act.wait_ge(t_hi, hbase + high[n - 1] + PRIMED)
                        act.wait_ge(recip, base + n - 1 + PRIMED)
                    else:
                        act.wait_ge(recip, base + PRIMED)
                    nc.scalar.activation(pr[n % 2][:, 0:w], sm[n % 2][:, 0:w], ACT.Exp, bias=nmx[:, n % 2:n % 2 + 1],
                                         accum_out=den[:, n % 2:n % 2 + 1]).then_inc(exped, 1)
                    if n >= 1:
                        keep_high(n - 1)
                    if n >= 2:
                        finish(n - 2)
                keep_high(NN - 1)
                finish(NN - 2)
                finish(NN - 1)


def out_stage(nc, K, A):
    with Stage(nc, "out") as st:
        oT = [st.sb(f"oT{a}", [P, ND, P]) for a in range(2)]
        tp = [st.ps(f"tp{a}", [P, ND, P]) for a in range(2)]
        py = [st.ps(f"py{a}", [P, D]) for a in range(2)]
        loaded, turned, kept, done, added = (st.sem(n) for n in ("loaded", "turned", "kept", "done", "added"))
        block = st.ctx.enter_context(nc.Block())

        @block.sync
        def _(sp):
            sp.dma_start(K.B1[:, :, :], A["w_out_attn"].rearrange("(k p) n -> p k n", p=P)).then_inc(loaded, 16)

        @block.tensor
        def _(pe):
            def turn(t):
                if t >= 2:
                    pe.wait_ge(kept, t - 1)
                for j in range(ND):
                    last = nc.tensor.transpose(tp[t % 2][:, j, :], K.B2[:, t, j * P:(j + 1) * P], K.ident)
                last.then_inc(turned, 1)

            turn(0)
            pe.wait_ge(loaded, 16)
            for t in range(NT):
                if t + 1 < NT:
                    turn(t + 1)
                pe.wait_ge(kept, t + 1)
                if t >= 2:
                    pe.wait_ge(added, t - 1)
                for h in range(2):
                    for k in range(ND):
                        last = nc.tensor.matmul(py[t % 2][:, h * HALF:(h + 1) * HALF], oT[t % 2][:, k, :],
                                                K.B1[:, k, h * HALF:(h + 1) * HALF], start=(k == 0), stop=(k == ND - 1))
                last.then_inc(done, 1)

        @block.scalar
        def _(act):
            for t in range(NT):
                act.wait_ge(turned, t + 1)
                if t >= 2:
                    act.wait_ge(done, t - 1)
                nc.scalar.activation(oT[t % 2][:, :, :], tp[t % 2][:, :, :], ACT.Copy).then_inc(kept, 1)

        @block.vector
        def _(dve):
            for t in range(NT):
                dve.wait_ge(done, t + 1)
                nc.vector.tensor_tensor(K.X[:, t, :], K.X[:, t, :], py[t % 2][:, :], ALU.add).then_inc(added, 1)


def attention_layer(nc, K, A):
    with ExitStack() as ctx:
        def sb(name, shape):
            return ctx.enter_context(nc.sbuf_tensor(name, shape, F32))

        K.B2, K.B3, K.B1 = (sb(n, [P, ND, S]) for n in ("B2", "B3", "B1"))
        with ExitStack() as early:
            def tmp(name, shape):
                return early.enter_context(nc.sbuf_tensor(name, shape, F32))

            K.lowT, K.krT = tmp("lowT", [P, 3, S]), tmp("krT", [ROPE_B, S])
            K.cosA, K.sinA, K.cosB, K.sinB = (tmp(n, [P, S]) for n in ("cosA", "sinA", "cosB", "sinB"))
            load_stage(nc, K, A)
            norm_stage(nc, K, V_ATTN, "norm_a")
            qk_stage(nc, K, A)
            v_stage(nc, K, A)
            mla_stage(nc, K, A)
        attention_stage(nc, K, "att_a", DH, K.QA, K.KA, K.maskA, 0)
        attention_stage(nc, K, "att_b", KB, K.QB, K.KB, K.maskB, HA)
        out_stage(nc, K, A)


DT, DTA, CS, ECS, TOEND, ETOT, SKIP = range(7)


def gate_stage(nc, K, A):
    with Stage(nc, "gate") as st:
        w = [st.sb(f"w{a}", [P, ND, HALF]) for a in range(2)]
        wdt = st.sb("wdt", [P, ND, HS])
        z = [st.sb(f"z{a}", [P, HALF]) for a in range(2)]
        pos, ab, u, ln, rate = (st.sb(n, [P, NT, HS]) for n in ("pos", "ab", "u", "ln", "rate"))
        pz = [st.ps(f"pz{a}", [P, HALF]) for a in range(2)]
        pdt, pcs = st.ps("pdt", [P, NT, HS]), st.ps("pcs", [P, 2, NT, HS])
        w_loaded = [st.sem(f"w_loaded{a}") for a in range(2)]
        z_stored = [st.sem(f"z_stored{a}") for a in range(2)]
        dt_loaded, dt_done, dta_ok, cs_done, chain, small_in, small_out, z_done, z_kept = (st.sem(n) for n in (
            "dt_loaded", "dt_done", "dta_ready", "cs_done", "chain", "small_in", "small_out", "z_done", "z_kept"))
        block = st.primed_block()
        win = A["w_in_ssd"].rearrange("(k p) n -> p k n", p=P)
        ROUNDS = DI // HALF // 2
        PER = 2 * NT

        @block.sync
        def _(sp):
            sp.dma_start(wdt[:, :, :], win[:, :, DI + XBC:SSD_IN]).then_inc(dt_loaded, 16)
            with sp.Fori(0, ROUNDS) as i:
                for a in range(2):
                    sp.wait_ge(z_done, i * PER + PRIMED)
                    sp.dma_start(w[a][:, :, :], win[:, :, bass.ds((i * 2 + a) * HALF, HALF)]).then_inc(w_loaded[a], 16)

        @block.tensor
        def _(pe):
            pe.wait_ge(dt_loaded, 16 + PRIMED)
            for t in range(NT):
                for k in range(ND):
                    last = nc.tensor.matmul(pdt[:, t, :], K.B1[:, k, t * P:(t + 1) * P], wdt[:, k, :], start=(k == 0), stop=(k == ND - 1))
            last.then_inc(dt_done, 1)
            with pe.Fori(0, ROUNDS) as i:
                for a in range(2):
                    pe.wait_ge(w_loaded[a], i * 16 + 16 + PRIMED)
                    for t in range(NT):
                        n = a * NT + t
                        pe.wait_ge(z_kept, (i * PER + (n - 1) if n else i * PER) + PRIMED)
                        for k in range(ND):
                            last = nc.tensor.matmul(pz[n % 2][:, :], K.B1[:, k, t * P:(t + 1) * P], w[a][:, k, :],
                                                    start=(k == 0), stop=(k == ND - 1))
                        last.then_inc(z_done, 1)
            pe.wait_ge(dta_ok, 1 + PRIMED)
            nc.tensor.matmul(pcs[:, 0, :, :], K.upper, K.heads[:, DTA, :, :], start=True, stop=True)
            nc.tensor.matmul(pcs[:, 1, :, :], K.ones, K.heads[:, DTA, :, :], start=True, stop=True).then_inc(cs_done, 1)

        @block.scalar
        def _(act):
            act.wait_ge(small_in, 1 + PRIMED)
            nc.scalar.activation(ab[:, :, :], ab[:, :, :], ACT.Exp)
            nc.scalar.activation(rate[:, :, :], rate[:, :, :], ACT.Exp).then_inc(small_out, 1)
            act.wait_ge(small_in, 2 + PRIMED)
            nc.scalar.activation(ln[:, :, :], u[:, :, :], ACT.Ln).then_inc(small_out, 1)
            with act.Fori(0, ROUNDS) as i:
                for n in range(PER):
                    a, t = n // NT, n % NT
                    act.wait_ge(z_done, i * PER + (n + 1) + PRIMED)
                    act.wait_ge(z_stored[n % 2], i * (PER // 2 * 16) + (n // 2) * 16 + PRIMED)
                    nc.scalar.activation(z[n % 2][:, :], pz[n % 2][:, :], ACT.Silu).then_inc(z_kept, 1)
                    act.wait_ge(z_kept, i * PER + (n + 1) + PRIMED)
                    act.dma_start(K.Z[t * P:(t + 1) * P, bass.ds((i * 2 + a) * HALF, HALF)], z[n % 2][:, :]).then_inc(z_stored[n % 2], 16)
            for a in range(2):
                act.wait_ge(z_stored[a], ROUNDS * PER // 2 * 16 + PRIMED)
            act.wait_ge(small_in, 3 + PRIMED)
            H = K.heads
            for q in (ECS, TOEND, ETOT):
                last = nc.scalar.activation(H[:, q, :, :], H[:, q, :, :], ACT.Exp)
            last.then_inc(small_out, 1)

        @block.vector
        def _(dve):
            step, V, H = Chain(dve, chain, PRIMED), nc.vector, K.heads

            def per_head(column):
                return K.vecs[:, column:column + HS].unsqueeze(1).to_broadcast([P, NT, HS])

            step(V.tensor_copy(H[:, SKIP, :, :], per_head(V_DSKIP)))
            step(V.tensor_copy(rate[:, :, :], per_head(V_ALOG)))
            dve.wait_ge(dt_done, 1 + PRIMED)
            step(V.tensor_tensor(pos[:, :, :], pdt[:, :, :], per_head(V_DTB), ALU.add))
            step(V.scalar_tensor_tensor(out=ab[:, :, :], in0=pos[:, :, :], scalar=-1.0, in1=pos[:, :, :], op0=ALU.mult, op1=ALU.min))
            V.tensor_scalar(pos[:, :, :], pos[:, :, :], 0.0, None, ALU.max).then_inc(small_in, 1)
            dve.wait_ge(small_out, 1 + PRIMED)
            V.tensor_scalar(u[:, :, :], ab[:, :, :], 1.0, None, ALU.add).then_inc(small_in, 1)
            dve.wait_ge(small_out, 2 + PRIMED)
            step(V.tensor_scalar(u[:, :, :], u[:, :, :], -1.0, None, ALU.add))
            step(V.tensor_tensor(ln[:, :, :], ln[:, :, :], ab[:, :, :], ALU.mult))
            step(V.scalar_tensor_tensor(out=ab[:, :, :], in0=u[:, :, :], scalar=0.0, in1=ab[:, :, :], op0=ALU.is_equal, op1=ALU.mult))
            step(V.scalar_tensor_tensor(out=ln[:, :, :], in0=u[:, :, :], scalar=0.0, in1=ln[:, :, :], op0=ALU.is_gt, op1=ALU.mult))
            step(V.tensor_scalar(u[:, :, :], u[:, :, :], 2.0 ** -24, None, ALU.max))
            step(V.reciprocal(u[:, :, :], u[:, :, :]))
            step(V.tensor_tensor(ln[:, :, :], ln[:, :, :], u[:, :, :], ALU.mult))
            step(V.tensor_tensor(ln[:, :, :], ln[:, :, :], ab[:, :, :], ALU.add))
            step(V.tensor_tensor(H[:, DT, :, :], pos[:, :, :], ln[:, :, :], ALU.add))
            V.scalar_tensor_tensor(out=H[:, DTA, :, :], in0=rate[:, :, :], scalar=-1.0, in1=H[:, DT, :, :], op0=ALU.mult,
                                   op1=ALU.mult).then_inc(dta_ok, 1)
            dve.wait_ge(cs_done, 1 + PRIMED)
            step(V.tensor_copy(H[:, CS, :, :], pcs[:, 0, :, :]))
            step(V.tensor_copy(H[:, ECS, :, :], pcs[:, 0, :, :]))
            step(V.tensor_copy(H[:, ETOT, :, :], pcs[:, 1, :, :]))
            V.tensor_tensor(H[:, TOEND, :, :], H[:, ETOT, :, :], H[:, CS, :, :], ALU.subtract).then_inc(small_in, 1)


def conv_stage(nc, K, A):
    LEFT = CONV - 1
    with Stage(nc, "conv") as st:
        w = [st.sb(f"w{a}", [P, ND, P]) for a in range(2)]
        tap = [st.sb(f"tap{a}", [P, CONV + 1]) for a in range(2)]
        u = [st.sb(f"u{a}", [P, LEFT + S]) for a in range(2)]
        acc = [st.sb(f"acc{a}", [P, S]) for a in range(2)]
        c = [st.sb(f"c{a}", [P, S]) for a in range(2)]
        prj = [st.ps(f"prj{a}", [P, S]) for a in range(2)]
        w_loaded, tap_loaded, done, u_ok, steps, c_ok, stored = ([st.sem(f"{n}{a}") for a in range(2)] for n in (
            "w_loaded", "tap_loaded", "done", "u_ready", "steps", "c_ready", "stored"))
        padded = st.sem("padded")
        block = st.primed_block()
        win = A["w_in_ssd"].rearrange("(k p) n -> p k n", p=P)
        ROUNDS = XBC // P // 2

        @block.sync
        def _(sp):
            with sp.Fori(0, ROUNDS) as i:
                for a in range(2):
                    sp.wait_ge(done[a], i + PRIMED)
                    sp.dma_start(w[a][:, :, :], win[:, :, bass.ds((i * 2 + a) * P + DI, P)]).then_inc(w_loaded[a], 16)
                    sp.wait_ge(c_ok[a], i + PRIMED)
                    sp.dma_start(tap[a][:, :], A["conv"][bass.ds(i * 2 + a, 1)].rearrange("a p n -> p (a n)")).then_inc(tap_loaded[a], 16)

        @block.tensor
        def _(pe):
            with pe.Fori(0, ROUNDS) as i:
                for a in range(2):
                    pe.wait_ge(w_loaded[a], i * 16 + 16 + PRIMED)
                    pe.wait_ge(u_ok[a], i + PRIMED)
                    for h in range(2):
                        for k in range(ND):
                            last = nc.tensor.matmul(prj[a][:, h * HALF:(h + 1) * HALF], w[a][:, k, :], K.B1[:, k, h * HALF:(h + 1) * HALF],
                                                    start=(k == 0), stop=(k == ND - 1))
                    last.then_inc(done[a], 1)

        @block.vector
        def _(dve):
            for a in range(2):
                last = nc.vector.memset(u[a][:, 0:LEFT], 0.0)
            last.then_inc(padded, 1)
            dve.wait_ge(padded, 1 + PRIMED)
            with dve.Fori(0, ROUNDS) as i:
                for a in range(2):
                    dve.wait_ge(u_ok[a], i + 1 + PRIMED)
                    dve.wait_ge(tap_loaded[a], i * 16 + 16 + PRIMED)
                    dve.wait_ge(c_ok[a], i + PRIMED)
                    nc.vector.tensor_scalar(acc[a][:, :], u[a][:, 0:S], tap[a][:, 0:1], None, ALU.mult).then_inc(steps[a], 1)
                    for n in range(1, CONV):
                        dve.wait_ge(steps[a], i * CONV + n + PRIMED)
                        nc.vector.scalar_tensor_tensor(out=acc[a][:, :], in0=u[a][:, n:n + S], scalar=tap[a][:, n:n + 1], in1=acc[a][:, :],
                                                       op0=ALU.mult, op1=ALU.add).then_inc(steps[a], 1)

        @block.scalar
        def _(act):
            act.wait_ge(padded, 1 + PRIMED)
            with act.Fori(0, ROUNDS) as i:
                def keep(a):
                    act.wait_ge(done[a], i + 1 + PRIMED)
                    nc.scalar.activation(u[a][:, LEFT:], prj[a][:, :], ACT.Copy).then_inc(u_ok[a], 1)

                def silu(a):
                    act.wait_ge(steps[a], i * CONV + CONV + PRIMED)
                    act.wait_ge(stored[a], i * 16 + PRIMED)
                    nc.scalar.activation(c[a][:, :], acc[a][:, :], ACT.Silu, bias=tap[a][:, CONV:CONV + 1]).then_inc(c_ok[a], 1)
                    act.wait_ge(c_ok[a], i + 1 + PRIMED)
                    act.dma_start(K.XC[bass.ds(i * 2 + a, 1)].rearrange("a p n -> p (a n)"), c[a][:, :]).then_inc(stored[a], 16)

                keep(0)
                silu(0)
                keep(1)
                silu(1)
            for a in range(2):
                act.wait_ge(stored[a], ROUNDS * 16 + PRIMED)
            act.nop()


def scan_stage(nc, K, A):
    GW = HG * HD
    with Stage(nc, "scan") as st:
        PAR = range(2)
        xT = [st.sb(f"xT{a}", [P, GW // P, P]) for a in PAR]
        bT, cT = [st.sb(f"bT{a}", [P, P]) for a in PAR], [st.sb(f"cT{a}", [P, P]) for a in PAR]
        z = [st.sb(f"z{a}", [P, GW]) for a in PAR]
        H = st.sb("H", [P, 7, NT, HG])
        cbm = [st.sb(f"cbm{a}", [P, P]) for a in PAR]
        dec, W = ([st.sb(f"{n}{a}", [P, HG, P]) for a in PAR] for n in ("dec", "W"))
        bt = [st.sb(f"bt{a}", [P, N]) for a in PAR]
        xs, xdt, xde, xsk, yi, y, sq = ([st.sb(f"{n}{a}", [P, GW]) for a in PAR] for n in ("xs", "xdt", "xde", "xsk", "yi", "y", "sq"))
        state = st.sb("state", [P, GW])
        ssg = st.sb("ssg", [P, NT])
        pcb, pbt = st.ps("pcb", [P, HALF])[:, 0:P], st.ps("pbt", [P, HALF])[:, 0:P]
        pr, px, pyi, py, pst = st.ps("pr", [P, HG, P]), st.ps("px", [P, GW]), st.ps("pyi", [P, GW]), st.ps("py", [P, GW]), st.ps("pst", [P, GW])
        loaded, y_stored = ([st.sem(f"{n}{a}") for a in PAR] for n in ("loaded", "y_stored"))
        heads_ok, cb_done, r_done, x_turned, yi_done, st_done, y_done = (st.sem(n) for n in (
            "heads_ready", "cb_done", "r_done", "x_turned", "yi_done", "st_done", "y_done"))
        bt_ok, xs_ok, e_ok, ss_ok = (st.sem(n) for n in ("bt_ready", "xs_ready", "decay_ready", "squares"))
        cbm_ok, seg_ok, xdt_ok, yi_ok, y_ok, st_ok = (st.sem(n) for n in ("cbm_ready", "seg_ready", "xdt_ready", "yi_ready", "y_ready", "state_ready"))
        w_ok, xde_ok, faded, skip_ok, skipped, gated = (st.sem(n) for n in ("w_ready", "xde_ready", "faded", "skip_ready", "skipped", "gated"))
        block = st.primed_block()

        def heads(q, c, width):
            return H[:, q, c, :].unsqueeze(2).to_broadcast([P, HG, width])

        def byhead(x):
            return x.rearrange("p (h d) -> p h d", h=HG)

        def before(base, c, back):
            return base + (c - back + 1) if c >= back else base

        @block.sync
        def _(sp):
            with sp.Fori(0, G) as i:
                base = i * NT
                for c in range(NT):
                    a, tok = c % 2, slice(c * P, (c + 1) * P)
                    sp.wait_ge(y_done, before(base, c, 2) + PRIMED)
                    sp.wait_ge(gated, before(base, c, 2) + PRIMED)
                    sp.dma_start(xT[a][:, :, :], K.XC[bass.ds(i * (GW // P), GW // P), :, tok].rearrange("k p n -> p k n")).then_inc(loaded[a], 16)
                    for buf, first in ((bT, DI // P), (cT, DI // P + G)):
                        sp.dma_start(buf[a][:, :], K.XC[bass.ds(i + first, 1), :, tok].rearrange("k p n -> p (k n)")).then_inc(loaded[a], 16)
                    sp.dma_start(z[a][:, :], K.Z[tok, bass.ds(i * GW, GW)]).then_inc(loaded[a], 16)

        def arrived(eng, i, c):
            eng.wait_ge(loaded[c % 2], i * (NT // 2 * 64) + (c // 2 + 1) * 64 + PRIMED)

        @block.tensor
        def _(pe):
            with pe.Fori(0, G) as i:
                base = i * NT

                def front(c):
                    a = c % 2
                    arrived(pe, i, c)
                    pe.wait_ge(cbm_ok, base + c + PRIMED)
                    pe.wait_ge(bt_ok, base + c + PRIMED)
                    nc.tensor.matmul(pcb[:, :], bT[a][:, :], cT[a][:, :], start=True, stop=True).then_inc(cb_done, 1)
                    if c == 0:
                        pe.wait_ge(heads_ok, i + 1 + PRIMED)
                    pe.wait_ge(seg_ok, base + c + PRIMED)
                    for h in range(HG):
                        last = nc.tensor.matmul(pr[:, h, :], H[:, DTA, c, h:h + 1].to_broadcast([P, P]), K.upper, start=True, stop=True)
                    last.then_inc(r_done, 1)
                    pe.wait_ge(xs_ok, base + c + PRIMED)
                    for k in range(GW // P):
                        nc.tensor.transpose(px[:, k * P:(k + 1) * P], xT[a][:, k, :], K.ident)
                    nc.tensor.transpose(pbt[:, :], bT[a][:, :], K.ident).then_inc(x_turned, 1)

                def back(c):
                    a = c % 2
                    pe.wait_ge(st_ok, base + (c + 1) + PRIMED)
                    pe.wait_ge(y_ok, base + c + PRIMED)
                    nc.tensor.matmul(pyi[:, :], cT[a][:, :], state[:, :], start=True, stop=True).then_inc(yi_done, 1)
                    if c + 1 < NT:
                        pe.wait_ge(bt_ok, base + (c + 1) + PRIMED)
                        pe.wait_ge(xde_ok, base + (c + 1) + PRIMED)
                        nc.tensor.matmul(pst[:, :], bt[a][:, :], xde[a][:, :], start=True, stop=True).then_inc(st_done, 1)
                    pe.wait_ge(w_ok, base + (c + 1) + PRIMED)
                    pe.wait_ge(xdt_ok, base + (c + 1) + PRIMED)
                    for h in range(HG):
                        last = nc.tensor.matmul(py[:, h * HD:(h + 1) * HD], W[a][:, h, :], xdt[a][:, h * HD:(h + 1) * HD], start=True, stop=True)
                    last.then_inc(y_done, 1)

                front(0)
                for c in range(NT):
                    if c + 1 < NT:
                        front(c + 1)
                    back(c)

        @block.scalar
        def _(act):
            with act.Fori(0, G) as i:
                base = i * NT

                def squares(c):
                    a = c % 2
                    act.wait_ge(gated, base + (c + 1) + PRIMED)
                    if c == 0:
                        act.wait_ge(heads_ok, i + 1 + PRIMED)
                    nc.scalar.activation(sq[a][:, :], y[a][:, :], ACT.Square, accum_out=ssg[:, c:c + 1]).then_inc(ss_ok, 1)
                    act.dma_start(K.YS[c * P:(c + 1) * P, bass.ds(i * GW, GW)], y[a][:, :]).then_inc(y_stored[a], 16)

                for c in range(NT):
                    a = c % 2
                    act.wait_ge(x_turned, base + (c + 1) + PRIMED)
                    act.wait_ge(y_done, before(base, c, 2) + PRIMED)
                    nc.scalar.activation(bt[a][:, :], pbt[:, :], ACT.Copy).then_inc(bt_ok, 1)
                    act.wait_ge(skip_ok, before(base, c, 2) + PRIMED)
                    act.wait_ge(xdt_ok, before(base, c, 2) + PRIMED)
                    nc.scalar.activation(xs[a][:, :], px[:, :], ACT.Copy).then_inc(xs_ok, 1)
                    act.wait_ge(seg_ok, base + (c + 1) + PRIMED)
                    nc.scalar.activation(dec[a][:, :, :], dec[a][:, :, :], ACT.Exp).then_inc(e_ok, 1)
                    if c >= 1:
                        act.wait_ge(ss_ok, before(base, c, 2) + PRIMED)
                        squares(c - 1)
                act.wait_ge(ss_ok, base + NT - 1 + PRIMED)
                squares(NT - 1)
            for a in PAR:
                act.wait_ge(y_stored[a], G * NT // 2 * 16 + PRIMED)
            act.nop()

        @block.vector
        def _(dve):
            V = nc.vector
            with dve.Fori(0, G) as i:
                base = i * NT

                def front(c):
                    a = c % 2
                    dve.wait_ge(cb_done, base + (c + 1) + PRIMED)
                    dve.wait_ge(w_ok, before(base, c, 2) + PRIMED)
                    V.tensor_tensor(cbm[a][:, :], pcb[:, :], K.upper, ALU.mult).then_inc(cbm_ok, 1)
                    dve.wait_ge(r_done, base + (c + 1) + PRIMED)
                    for h in range(HG):
                        last = V.tensor_scalar(dec[a][:, h, :], pr[:, h, :], H[:, CS, c, h:h + 1], 0.0, ALU.subtract, ALU.min)
                    last.then_inc(seg_ok, 1)
                    dve.wait_ge(xs_ok, base + (c + 1) + PRIMED)
                    dve.wait_ge(y_done, before(base, c, 2) + PRIMED)
                    dve.wait_ge(xde_ok, before(base, c, 2) + PRIMED)
                    V.tensor_tensor(byhead(xdt[a][:, :]), byhead(xs[a][:, :]), heads(DT, c, HD), ALU.mult).then_inc(xdt_ok, 1)

                def back(c):
                    a = c % 2
                    dve.wait_ge(yi_done, base + (c + 1) + PRIMED)
                    dve.wait_ge(skipped, before(base, c, 2) + PRIMED)
                    V.tensor_tensor(byhead(yi[a][:, :]), byhead(pyi[:, :]), heads(ECS, c, HD), ALU.mult).then_inc(yi_ok, 1)
                    if c + 1 < NT:
                        dve.wait_ge(faded, i * (NT - 1) + (c + 1) + PRIMED)
                        dve.wait_ge(st_done, i * (NT - 1) + (c + 1) + PRIMED)
                        V.tensor_tensor(state[:, :], state[:, :], pst[:, :], ALU.add).then_inc(st_ok, 1)
                    dve.wait_ge(y_done, base + (c + 1) + PRIMED)
                    dve.wait_ge(yi_ok, base + (c + 1) + PRIMED)
                    V.tensor_tensor(yi[a][:, :], yi[a][:, :], py[:, :], ALU.add).then_inc(y_ok, 1)

                dve.wait_ge(gated, base + PRIMED)
                dve.wait_ge(ss_ok, base + PRIMED)
                V.tensor_copy(H[:, :, :, :], K.heads[:, :, :, bass.ds(i * HG, HG)]).then_inc(heads_ok, 1)
                V.memset(state[:, :], 0.0).then_inc(st_ok, 1)
                dve.wait_ge(heads_ok, i + 1 + PRIMED)
                front(0)
                for c in range(NT):
                    if c + 1 < NT:
                        front(c + 1)
                    back(c)
                dve.wait_ge(ss_ok, base + NT + PRIMED)
                V.tensor_copy(K.ss[:, :, bass.ds(i, 1)].rearrange("p c a -> p (c a)"), ssg[:, :])

        @block.gpsimd
        def _(pool):
            Q = nc.gpsimd
            with pool.Fori(0, G) as i:
                base = i * NT

                def tail(c):
                    a = c % 2
                    pool.wait_ge(xs_ok, base + (c + 1) + PRIMED)
                    Q.tensor_tensor(byhead(xsk[a][:, :]), byhead(xs[a][:, :]), heads(SKIP, c, HD), ALU.mult).then_inc(skip_ok, 1)
                    pool.wait_ge(y_ok, base + (c + 1) + PRIMED)
                    pool.wait_ge(skip_ok, base + (c + 1) + PRIMED)
                    Q.tensor_tensor(xsk[a][:, :], xsk[a][:, :], yi[a][:, :], ALU.add).then_inc(skipped, 1)
                    pool.wait_ge(skipped, base + (c + 1) + PRIMED)
                    pool.wait_ge(y_stored[a], i * (NT // 2 * 16) + (c // 2) * 16 + PRIMED)
                    pool.wait_ge(ss_ok, before(base, c, 2) + PRIMED)
                    arrived(pool, i, c)
                    Q.tensor_tensor(y[a][:, :], xsk[a][:, :], z[a][:, :], ALU.mult).then_inc(gated, 1)

                for c in range(NT):
                    a = c % 2
                    pool.wait_ge(cbm_ok, base + (c + 1) + PRIMED)
                    pool.wait_ge(e_ok, base + (c + 1) + PRIMED)
                    pool.wait_ge(y_done, before(base, c, 2) + PRIMED)
                    Q.tensor_tensor(W[a][:, :, :], dec[a][:, :, :], cbm[a][:, :].unsqueeze(1).to_broadcast([P, HG, P]), ALU.mult).then_inc(w_ok, 1)
                    pool.wait_ge(xdt_ok, base + (c + 1) + PRIMED)
                    Q.tensor_tensor(byhead(xde[a][:, :]), byhead(xdt[a][:, :]), heads(TOEND, c, HD), ALU.mult).then_inc(xde_ok, 1)
                    if c >= 1:
                        tail(c - 1)
                    if c + 1 < NT:
                        pool.wait_ge(yi_done, base + (c + 1) + PRIMED)
                        Q.tensor_tensor(byhead(state[:, :]), byhead(state[:, :]), heads(ETOT, c, HD), ALU.mult).then_inc(faded, 1)
                tail(NT - 1)


def ssd_out_stage(nc, K, A):
    NK = DI // P
    with Stage(nc, "sout") as st:
        w = st.sb("w", [P, NK, D])
        y = [st.sb(f"y{a}", [P, G, DI // G]) for a in range(2)]
        yT = [st.sb(f"yT{a}", [P, NK, P]) for a in range(2)]
        tp = st.ps("tp", [P, NK, P])
        py = [st.ps(f"py{a}", [P, D]) for a in range(2)]
        loaded, mean, root, rstd_ok, scaled, turned, kept, done, added = (st.sem(n) for n in (
            "loaded", "mean", "root", "rstd_ready", "scaled", "turned", "kept", "done", "added"))
        y_loaded = [st.sem(f"y_loaded{a}") for a in range(2)]
        block = st.ctx.enter_context(nc.Block())

        @block.sync
        def _(sp):
            for t in range(NT):
                if t >= 2:
                    sp.wait_ge(turned, t - 1)
                sp.dma_start(y[t % 2][:, :, :].rearrange("p g n -> p (g n)"), K.YS[t * P:(t + 1) * P, :]).then_inc(y_loaded[t % 2], 16)
                if t == 0:
                    sp.dma_start(w[:, :, :], A["w_out_ssd"].rearrange("(k p) n -> p k n", p=P)).then_inc(loaded, 16)

        @block.scalar
        def _(act):
            act.wait_ge(mean, 1)
            nc.scalar.activation(K.ss[:, :, :], K.ss[:, :, :], ACT.Sqrt).then_inc(root, 1)

        @block.vector
        def _(dve):
            V = nc.vector

            def add(t):
                dve.wait_ge(done, t + 1)
                V.tensor_tensor(K.X[:, t, :], K.X[:, t, :], py[t % 2][:, :], ALU.add).then_inc(added, 1)

            V.tensor_scalar(K.ss[:, :, :], K.ss[:, :, :], 1.0 / (DI // G), EPS, ALU.mult, ALU.add).then_inc(mean, 1)
            dve.wait_ge(root, 1)
            V.reciprocal(K.ss[:, :, :], K.ss[:, :, :]).then_inc(rstd_ok, 1)
            dve.wait_ge(rstd_ok, 1)
            for t in range(NT):
                dve.wait_ge(y_loaded[t % 2], (t // 2 + 1) * 16)
                r = K.ss[:, t, :].unsqueeze(2).to_broadcast([P, G, DI // G])
                V.tensor_tensor(y[t % 2][:, :, :], y[t % 2][:, :, :], r, ALU.mult).then_inc(scaled, 1)
                dve.wait_ge(turned, t + 1)
                if t >= 2:
                    dve.wait_ge(done, t - 1)
                g = K.vecs[:, V_GATE:V_GATE + NK].unsqueeze(2).to_broadcast([P, NK, P])
                V.tensor_tensor(yT[t % 2][:, :, :], tp[:, :, :], g, ALU.mult).then_inc(kept, 1)
                if t >= 1:
                    add(t - 1)
            add(NT - 1)

        @block.tensor
        def _(pe):
            def turn(t):
                pe.wait_ge(scaled, t + 1)
                pe.wait_ge(kept, t)
                rows = y[t % 2][:, :, :].rearrange("p g n -> p (g n)")
                for j in range(NK):
                    last = nc.tensor.transpose(tp[:, j, :], rows[:, j * P:(j + 1) * P], K.ident)
                last.then_inc(turned, 1)

            turn(0)
            pe.wait_ge(loaded, 16)
            for t in range(NT):
                if t + 1 < NT:
                    turn(t + 1)
                pe.wait_ge(kept, t + 1)
                if t >= 2:
                    pe.wait_ge(added, t - 1)
                for h in range(2):
                    for k in range(NK):
                        last = nc.tensor.matmul(py[t % 2][:, h * HALF:(h + 1) * HALF], yT[t % 2][:, k, :], w[:, k, h * HALF:(h + 1) * HALF],
                                                start=(k == 0), stop=(k == NK - 1))
                last.then_inc(done, 1)


def ssd_layer(nc, K, A):
    with ExitStack() as ctx:
        def sb(name, shape):
            return ctx.enter_context(nc.sbuf_tensor(name, shape, F32))

        K.heads, K.ss = sb("heads", [P, 7, NT, HS]), sb("gate_ss", [P, NT, G])
        with ExitStack() as early:
            K.B1 = early.enter_context(nc.sbuf_tensor("ssd_hT", [P, ND, S], F32))
            norm_stage(nc, K, V_SSD, "norm_s")
            gate_stage(nc, K, A)
            conv_stage(nc, K, A)
        scan_stage(nc, K, A)
        ssd_out_stage(nc, K, A)


def router_stage(nc, K, A, layer, M):
    C, T2 = K.consts, 2 * NT
    with Stage(nc, f"route{layer}") as st:
        wr = st.sb("wr", [P, ND, NL])
        L = st.sb("L", [P, NT, NL])
        gm, gv, m1, m2, ex, den = (st.sb(n, [P, NT]) for n in ("gm", "gv", "m1", "m2", "ex", "den"))
        goh, gt = st.sb("goh", [P, NT, NG]), st.sb("gt", [P, NT, NG])
        pick = st.sb("pick", [P, NT, EPG, NG])
        ing, et = st.sb("ing", [P, NT, EPG]), st.sb("et", [P, NT, EPG])
        oh = [st.sb(f"oh{k}", [P, NT, EPG]) for k in range(2)]
        choice = st.sb("choice", [P, 2, NT, NE])
        both = st.sb("both", [P, NT, NE])
        before = st.sb("before", [P, NT + 1, NE])
        cum = st.sb("cum", [P, NT, NE])
        prod = st.sb("prod", [P, 2, NT, NE])
        rank, extra, where, expert, start = (st.sb(n, [P, T2]) for n in ("rank", "extra", "where", "expert", "start"))
        more = st.sb("more", [P, NE])
        upto = [st.sb(f"upto{a}", [P, NE]) for a in range(2)]
        first = st.sb("first", [P, NE])
        owner = st.sb("owner", [P, NBLK - NE, NE])
        planf = st.sb("planf", [P, 1 + NBLK])
        row1 = [st.sb(f"row1{a}", [P, P]) for a in range(2)]
        col1 = [st.sb(f"col1{a}", [P, NBLK]) for a in range(2)]
        plg, pcum, ptab = st.ps("plg", [P, NT, NL]), st.ps("pcum", [P, 2, NT, NE]), st.ps("ptab", [P, NBLK])
        loaded, logits, chain, expin, expd, masked, counted, onehot, placed = (st.sem(n) for n in (
            "loaded", "logits", "chain", "exp_in", "exp_done", "chosen", "counted", "one_hot", "placed"))
        block = st.ctx.enter_context(nc.Block())

        @block.sync
        def _(sp):
            sp.dma_start(wr[:, :, :], A["w_route"][layer].rearrange("(k p) n -> p k n", p=P)).then_inc(loaded, 16)

        @block.tensor
        def _(pe):
            pe.wait_ge(loaded, 16)
            for t in range(NT):
                for k in range(ND):
                    last = nc.tensor.matmul(plg[:, t, :], K.B1[:, k, t * P:(t + 1) * P], wr[:, k, :], start=(k == 0), stop=(k == ND - 1))
            last.then_inc(logits, 1)
            pe.wait_ge(masked, 1)
            nc.tensor.matmul(pcum[:, 0, :, :], K.strict, both[:, :, :], start=True, stop=True)
            nc.tensor.matmul(pcum[:, 1, :, :], K.ones, both[:, :, :], start=True, stop=True).then_inc(counted, 1)
            for n in range(T2):
                pe.wait_ge(onehot, 2 * n + 2)
                nc.tensor.matmul(ptab[:, :], row1[n % 2][:, :], col1[n % 2][:, :], start=(n == 0), stop=(n == T2 - 1)).then_inc(placed, 1)

        @block.scalar
        def _(act):
            act.wait_ge(expin, 1)
            nc.scalar.activation(gt[:, :, :], gt[:, :, :], ACT.Exp).then_inc(expd, 1)
            act.wait_ge(expin, 2)
            nc.scalar.activation(ex[:, :], ex[:, :], ACT.Exp).then_inc(expd, 1)

        @block.vector
        def _(dve):
            step = Chain(dve, chain)
            V = nc.vector

            def over(x, shape, axis):
                return x.unsqueeze(axis).to_broadcast(shape)

            def best(value, top, hot, scratch, width, desc):
                shape = [P, NT, width]
                order = C[:, desc:desc + width].unsqueeze(1).to_broadcast(shape)
                step(V.tensor_reduce(top[:, :], value, AX.X, ALU.max))
                step(V.tensor_tensor(scratch, value, over(top[:, :], shape, 2), ALU.is_equal))
                step(V.tensor_tensor(scratch, scratch, order, ALU.mult))
                step(V.tensor_reduce(den[:, :], scratch, AX.X, ALU.max))
                step(V.tensor_tensor(hot, scratch, over(den[:, :], shape, 2), ALU.is_equal))

            def whole(out, x, unit):
                step(V.tensor_scalar(out, x, 1.0 / unit, -(unit - 1) / (2 * unit), ALU.mult, ALU.add))
                step(V.tensor_scalar(out, out, MAGIC, MAGIC, ALU.add, ALU.subtract))

            dve.wait_ge(logits, 1)
            bias = K.vecs[:, V_BR + layer * NL:V_BR + (layer + 1) * NL].unsqueeze(1).to_broadcast([P, NT, NL])
            step(V.tensor_tensor(L[:, :, :], plg[:, :, :], bias, ALU.add))
            group, each = L[:, :, 0:NG], L[:, :, NG:NL].rearrange("p t (g e) -> p t e g", g=NG)
            best(group, gm, goh[:, :, :], gt[:, :, :], NG, C_GDESC)
            V.tensor_tensor(gt[:, :, :], group, over(gm[:, :], [P, NT, NG], 2), ALU.subtract).then_inc(expin, 1)
            step(V.tensor_tensor(pick[:, :, :, :], each, over(goh[:, :, :], [P, NT, EPG, NG], 2), ALU.mult))
            step(V.tensor_reduce(ing[:, :, :], pick[:, :, :, :], AX.X, ALU.add))
            best(ing[:, :, :], m1, oh[0][:, :, :], et[:, :, :], EPG, C_DESC)
            step(V.scalar_tensor_tensor(out=ing[:, :, :], in0=oh[0][:, :, :], scalar=NEG, in1=ing[:, :, :], op0=ALU.mult, op1=ALU.add))
            best(ing[:, :, :], m2, oh[1][:, :, :], et[:, :, :], EPG, C_DESC)
            V.tensor_tensor(ex[:, :], m2[:, :], m1[:, :], ALU.subtract).then_inc(expin, 1)
            dve.wait_ge(expd, 2)
            step(V.tensor_reduce(gv[:, :], gt[:, :, :], AX.X, ALU.add))
            step(V.tensor_scalar(den[:, :], ex[:, :], 1.0, None, ALU.add))
            step(V.tensor_tensor(den[:, :], den[:, :], gv[:, :], ALU.mult))
            step(V.reciprocal(M.weight[:, 0, :], den[:, :]))
            step(V.tensor_tensor(M.weight[:, 1, :], M.weight[:, 0, :], ex[:, :], ALU.mult))
            for k in range(2):
                hot = choice[:, k, :, :].rearrange("p t (g e) -> p t g e", g=NG)
                shape = [P, NT, NG, EPG]
                step(V.tensor_tensor(hot, over(goh[:, :, :], shape, 3), over(oh[k][:, :, :], shape, 2), ALU.mult))
            V.tensor_tensor(both[:, :, :], choice[:, 0, :, :], choice[:, 1, :, :], ALU.add).then_inc(masked, 1)
            dve.wait_ge(counted, 1)
            step(V.memset(before[:, 0, :], 0.0))
            for t in range(NT):
                step(V.tensor_tensor(before[:, t + 1, :], before[:, t, :], pcum[:, 1, t, :], ALU.add))
            step(V.tensor_tensor(cum[:, :, :], before[:, 0:NT, :], pcum[:, 0, :, :], ALU.add))
            step(V.tensor_scalar(more[:, :], before[:, NT, :], -1.0, 0.0, ALU.add, ALU.max))
            whole(more[:, :], more[:, :], P)
            step(V.tensor_copy(upto[0][:, :], more[:, :]))
            a, d = 0, 1
            while d < NE:
                step(V.tensor_copy(upto[1 - a][:, 0:d], upto[a][:, 0:d]))
                step(V.tensor_tensor(upto[1 - a][:, d:], upto[a][:, d:], upto[a][:, 0:NE - d], ALU.add))
                a, d = 1 - a, 2 * d
            total = upto[a]
            step(V.tensor_tensor(first[:, :], total[:, :], more[:, :], ALU.subtract))
            flat = choice[:, :, :, :].rearrange("p k t e -> p (k t) e")
            pflat = prod[:, :, :, :].rearrange("p k t e -> p (k t) e")
            for k in range(2):
                step(V.tensor_tensor(prod[:, k, :, :], choice[:, k, :, :], cum[:, :, :], ALU.mult))
            step(V.tensor_reduce(rank[:, :], pflat, AX.X, ALU.add))
            for out, row in ((expert, C[:, C_IOTA:C_IOTA + NE]), (start, first[:, :])):
                step(V.tensor_tensor(pflat, flat, row.unsqueeze(1).to_broadcast([P, T2, NE]), ALU.mult))
                step(V.tensor_reduce(out[:, :], pflat, AX.X, ALU.add))
            whole(extra[:, :], rank[:, :], P)
            step(V.scalar_tensor_tensor(out=rank[:, :], in0=extra[:, :], scalar=-float(P), in1=rank[:, :], op0=ALU.mult, op1=ALU.add))
            step(V.tensor_tensor(start[:, :], start[:, :], extra[:, :], ALU.add))
            step(V.scalar_tensor_tensor(out=start[:, :], in0=start[:, :], scalar=float(NE - 1), in1=expert[:, :], op0=ALU.add, op1=ALU.subtract))
            step(V.tensor_scalar(extra[:, :], extra[:, :], 0.0, None, ALU.is_gt))
            step(V.tensor_tensor(start[:, :], start[:, :], extra[:, :], ALU.mult))
            step(V.tensor_tensor(where[:, :], expert[:, :], start[:, :], ALU.add))
            step(V.scalar_tensor_tensor(out=expert[:, :], in0=where[:, :], scalar=float(P), in1=rank[:, :], op0=ALU.mult, op1=ALU.add))
            step(V.tensor_copy(M.slot[:, :], expert[:, :]))
            step(V.tensor_copy(planf[:, 1:1 + NE], C[:, C_IOTA:C_IOTA + NE]))
            shape = [P, NBLK - NE, NE]
            step(V.tensor_tensor(owner[:, :, :], over(total[:, :], shape, 1), over(C[:, C_BLK:C_BLK + NBLK - NE], shape, 2), ALU.is_le))
            step(V.tensor_reduce(planf[:, 1 + NE:], owner[:, :, :], AX.X, ALU.add))
            step(V.tensor_scalar(planf[:, 1 + NE:], planf[:, 1 + NE:], float(NE - 1), None, ALU.min))
            step(V.tensor_scalar(planf[:, 0:1], total[:, NE - 1:NE], 1.0, None, ALU.add))
            whole(planf[:, 0:1], planf[:, 0:1], 2)
            step(V.tensor_scalar(planf[:, 0:1], planf[:, 0:1], float(NE // 2 - 1), None, ALU.add))
            step(V.tensor_copy(M.plan[:, :], planf[:, :]))
            for n in range(T2):
                if n >= 2:
                    dve.wait_ge(placed, n - 1)
                V.tensor_scalar(row1[n % 2][:, :], C[:, C_IOTA:C_IOTA + P], rank[:, n:n + 1], None, ALU.is_equal).then_inc(onehot, 1)
                V.tensor_scalar(col1[n % 2][:, :], C[:, C_IOTA:C_IOTA + NBLK], where[:, n:n + 1], C[:, C_TOK + n % NT:C_TOK + n % NT + 1],
                                ALU.is_equal, ALU.mult).then_inc(onehot, 1)
            step(V.memset(M.tokens[:, NBLK:], 0))
            dve.wait_ge(placed, T2)
            step(V.tensor_copy(M.tokens[:, 0:NBLK], ptab[:, :]))


def expert_stage(nc, K, A, layer, M):
    Y = K.Y
    FK = DE // P
    with Stage(nc, f"moe{layer}") as st:
        pick = [st.sb(f"pick{a}", [P, 1], I32) for a in range(2)]
        spare = st.sb("spare", [P, 2], I32)
        xg = [st.sb(f"xg{a}", [P, D]) for a in range(2)]
        xT = [st.sb(f"xT{a}", [P, ND, P]) for a in range(2)]
        sg = [st.sb(f"sg{a}", [P, DE]) for a in range(2)]
        hid = [st.sb(f"hid{a}", [P, DE]) for a in range(2)]
        hT = [st.sb(f"hT{a}", [P, FK, P]) for a in range(2)]
        y = [st.sb(f"y{a}", [P, D]) for a in range(2)]
        pg = [st.ps(f"pg{a}", [P, DE]) for a in range(2)]
        pu = [st.ps(f"pu{a}", [P, DE]) for a in range(2)]
        px, ph = st.ps("px", [P, FK, P]), st.ps("ph", [P, FK, P])
        py = [st.ps(f"py{h}", [P, HALF]) for h in range(2)]
        x_turned, x_kept, h_kept = (st.sem(n) for n in ("x_turned", "x_kept", "h_kept"))
        gathered = [st.sem(f"gathered{a}", primed=False) for a in range(2)]
        picked, gate_done, up_done, silu_done, hid_ok, h_turned, stored = (
            [st.sem(f"{n}{a}") for a in range(2)] for n in
            ("picked", "gate_done", "up_done", "silu_done", "hidden", "h_turned", "stored"))
        y_done, y_kept = ([st.sem(f"{n}{h}") for h in range(2)] for n in ("y_done", "y_kept"))
        block = st.primed_block()

        def rounds_less_one(eng):
            return eng.value_load(M.plan[0:1, 0:1], min_val=NE // 2 - 1, max_val=NBLK // 2 - 1)

        def rounds(eng):
            return rounds_less_one(eng) + 1

        @block.sync
        def _(sp):
            n = rounds_less_one(sp)

            def expert(b):
                return sp.value_load(M.plan[0:1, bass.ds(b + 1, 1)], min_val=0, max_val=NE - 1)

            def load_down(e, a):
                sp.dma_start(M.wd[a][:, :, :], M.down(e)).then_inc(M.wd_loaded[a], 16)

            with sp.Fori(0, n) as i:
                for a in range(2):
                    e, e_down = expert(i * 2 + (2 + a)), expert(i * 2 + (1 + a))
                    sp.wait_ge(up_done[a], i + 1 + PRIMED)
                    sp.dma_start(M.wg[a][:, :, :], M.gate(e)).then_inc(M.wg_loaded[a], 16)
                    sp.dma_start(M.wu[a][:, :, :], M.up(e)).then_inc(M.wu_loaded[a], 16)
                    if a == 0:
                        sp.wait_ge(y_done[1], i * 2 + PRIMED)
                        load_down(e_down, 1)
                    else:
                        sp.wait_ge(y_done[1], i * 2 + 1 + PRIMED)
                        load_down(e_down, 0)
            e_down = expert(n * 2 + 1)
            sp.wait_ge(y_done[1], n * 2 + PRIMED)
            load_down(e_down, 1)

        @block.gpsimd
        def _(pool):
            n = rounds(pool)

            def gather(b, a, done):
                nc.gpsimd.tensor_copy(pick[a][:, :], M.tokens[:, bass.ds(b, 1)]).then_inc(picked[a], 1)
                pool.wait_ge(picked[a], done + 1 + PRIMED)
                nc.gpsimd.tensor_tensor(spare[:, a:a + 1], pick[a][:, :], pick[a][:, :], ALU.add)
                nc.gpsimd.indirect_dma_start(out=xg[a][:, :], out_offset=None, in_=K.HN[:, :],
                                             in_offset=bass.IndirectOffsetOnAxis(ap=pick[a][:, :], axis=0)).then_inc(gathered[a], 16)

            for a in range(2):
                gather(a, a, 0)
            with pool.Fori(0, n) as i:
                for a in range(2):
                    pool.wait_ge(gathered[a], i * 16 + 16)
                    pool.wait_ge(x_turned, i * 4 + 2 * (a + 1) + PRIMED)
                    gather(i * 2 + (2 + a), a, i + 1)

        @block.tensor
        def _(pe):
            def turn_x(a, half, seq, round_):
                pe.wait_ge(gathered[a], round_ * 16 + 16)
                pe.wait_ge(x_kept, seq + PRIMED)
                for j in range(FK):
                    c = (half * FK + j) * P
                    last = nc.tensor.transpose(px[:, j, :], xg[a][:, c:c + P], K.ident)
                last.then_inc(x_turned, 1)

            n = rounds(pe)
            for a in range(2):
                for half in range(2):
                    turn_x(a, half, 2 * a + half, 0)
            with pe.Fori(0, n) as i:
                def first(a, out, w, loaded, done):
                    pe.wait_ge(loaded[a], i * 16 + 16)
                    for k in range(ND):
                        last = nc.tensor.matmul(out[a][:, :], xT[a][:, k, :], w[a][:, k, :], start=(k == 0), stop=(k == ND - 1))
                    last.then_inc(done[a], 1)

                def gate(a):
                    pe.wait_ge(x_kept, i * 4 + 2 * (a + 1) + PRIMED)
                    pe.wait_ge(hid_ok[a], i + PRIMED)
                    first(a, pg, M.wg, M.wg_loaded, gate_done)

                def up(a):
                    first(a, pu, M.wu, M.wu_loaded, up_done)

                def turn_h(a):
                    pe.wait_ge(hid_ok[a], i + 1 + PRIMED)
                    pe.wait_ge(h_kept, i * 2 + a + PRIMED)
                    for j in range(FK):
                        last = nc.tensor.transpose(ph[:, j, :], hid[a][:, j * P:(j + 1) * P], K.ident)
                    last.then_inc(h_turned[a], 1)

                def down(a, h):
                    pe.wait_ge(h_kept, i * 2 + (a + 1) + PRIMED)
                    pe.wait_ge(M.wd_loaded[a], i * 16 + 16)
                    pe.wait_ge(y_kept[h], i * 2 + a + PRIMED)
                    for k in range(FK):
                        last = nc.tensor.matmul(py[h][:, :], hT[a][:, k, :], M.wd[a][:, k, h * HALF:(h + 1) * HALF],
                                                start=(k == 0), stop=(k == FK - 1))
                    last.then_inc(y_done[h], 1)

                gate(0)
                up(0)
                gate(1)
                turn_h(0)
                turn_x(0, 0, i * 4 + 4, i + 1)
                up(1)
                turn_x(0, 1, i * 4 + 5, i + 1)
                down(0, 0)
                turn_h(1)
                turn_x(1, 0, i * 4 + 6, i + 1)
                down(0, 1)
                turn_x(1, 1, i * 4 + 7, i + 1)
                down(1, 0)
                down(1, 1)
            for a in range(2):
                pe.wait_ge(stored[a], n * 16 + PRIMED)

        @block.scalar
        def _(act):
            n = rounds(act)
            with act.Fori(0, n) as i:
                def silu(a):
                    act.wait_ge(gate_done[a], i + 1 + PRIMED)
                    act.wait_ge(hid_ok[a], i + PRIMED)
                    nc.scalar.activation(sg[a][:, :], pg[a][:, :], ACT.Silu).then_inc(silu_done[a], 1)

                def keep_h(a):
                    act.wait_ge(h_turned[a], i + 1 + PRIMED)
                    act.wait_ge(y_done[1], i * 2 + PRIMED)
                    nc.scalar.activation(hT[a][:, :, :], ph[:, :, :], ACT.Copy).then_inc(h_kept, 1)

                def keep_y(a, h):
                    act.wait_ge(y_done[h], i * 2 + (a + 1) + PRIMED)
                    act.wait_ge(stored[a], i * 16 + PRIMED)
                    nc.scalar.activation(y[a][:, h * HALF:(h + 1) * HALF], py[h][:, :], ACT.Copy).then_inc(y_kept[h], 1)

                def store(a):
                    for h in range(2):
                        act.wait_ge(y_kept[h], i * 2 + (a + 1) + PRIMED)
                    act.dma_start(Y[bass.ds((i * 2 + a) * P, P), :], y[a][:, :]).then_inc(stored[a], 16)

                silu(0)
                silu(1)
                keep_h(0)
                keep_y(0, 0)
                keep_h(1)
                keep_y(0, 1)
                store(0)
                keep_y(1, 0)
                keep_y(1, 1)
                store(1)

        @block.vector
        def _(dve):
            n = rounds(dve)

            def keep_x(a, half, seq, used):
                dve.wait_ge(x_turned, seq + 1 + PRIMED)
                dve.wait_ge(up_done[a], used + PRIMED)
                c = V_MOE + layer * ND + half * FK
                g = K.vecs[:, c:c + FK].unsqueeze(2).to_broadcast([P, FK, P])
                nc.vector.tensor_tensor(xT[a][:, half * FK:(half + 1) * FK, :], px[:, :, :], g, ALU.mult).then_inc(x_kept, 1)

            for a in range(2):
                for half in range(2):
                    keep_x(a, half, 2 * a + half, 0)
            with dve.Fori(0, n) as i:
                def hidden(a):
                    dve.wait_ge(silu_done[a], i + 1 + PRIMED)
                    dve.wait_ge(up_done[a], i + 1 + PRIMED)
                    dve.wait_ge(h_turned[a], i + PRIMED)
                    nc.vector.tensor_tensor(hid[a][:, :], sg[a][:, :], pu[a][:, :], ALU.mult).then_inc(hid_ok[a], 1)

                hidden(0)
                keep_x(0, 0, i * 4 + 4, i + 1)
                keep_x(0, 1, i * 4 + 5, i + 1)
                hidden(1)
                keep_x(1, 0, i * 4 + 6, i + 1)
                keep_x(1, 1, i * 4 + 7, i + 1)


def combine_stage(nc, K, layer, M):
    with Stage(nc, f"comb{layer}") as st:
        rows = [[st.sb(f"rows{k}{a}", [P, D]) for a in range(2)] for k in range(2)]
        got = [[st.sem(f"got{k}{a}") for a in range(2)] for k in range(2)]
        added = [st.sem(f"added{k}") for k in range(2)]
        block = st.ctx.enter_context(nc.Block())

        @block.gpsimd
        def _(pool):
            for t in range(NT):
                for k in range(2):
                    if t >= 2:
                        pool.wait_ge(added[k], t - 1)
                    c = k * NT + t
                    nc.gpsimd.indirect_dma_start(out=rows[k][t % 2][:, :], out_offset=None, in_=K.Y[:, :],
                                                 in_offset=bass.IndirectOffsetOnAxis(ap=M.slot[:, c:c + 1], axis=0)).then_inc(got[k][t % 2], 16)

        @block.vector
        def _(dve):
            for t in range(NT):
                for k in range(2):
                    dve.wait_ge(got[k][t % 2], 16 * (t // 2 + 1))
                    if k:
                        dve.wait_ge(added[0], t + 1)
                    nc.vector.scalar_tensor_tensor(out=K.X[:, t, :], in0=rows[k][t % 2][:, :], scalar=M.weight[:, k, t:t + 1],
                                                   in1=K.X[:, t, :], op0=ALU.mult, op1=ALU.add).then_inc(added[k], 1)


def moe_layer(nc, K, A, layer):
    M = Names()
    with Stage(nc, f"moes{layer}") as st:
        M.wg, M.wu = ([st.sb(f"{n}{a}", [P, ND, DE]) for a in range(2)] for n in ("wg", "wu"))
        M.wd = [st.sb(f"wd{a}", [P, DE // P, D]) for a in range(2)]
        M.wg_loaded, M.wu_loaded, M.wd_loaded = ([st.sem(f"{n}_loaded{a}") for a in range(2)] for n in ("wg", "wu", "wd"))
        M.weight, M.slot = st.sb("weight", [P, 2, NT]), st.sb("slot", [P, 2 * NT], I32)
        M.plan, M.tokens = st.sb("plan", [P, 1 + NBLK], I32), st.sb("tokens", [P, NBLK + 2], I32)

        def weights(name):
            w = A[name][layer].rearrange("e (k p) n -> e p k n", p=P)
            return lambda e: w[bass.ds(e, 1)].rearrange("a p k n -> p (a k) n")

        M.gate, M.up, M.down = (weights(n) for n in ("w_gate", "w_up", "w_down"))

        def first_weights(sp):
            for a in range(2):
                sp.dma_start(M.wg[a][:, :, :], M.gate(a)).then_inc(M.wg_loaded[a], 16)
                sp.dma_start(M.wu[a][:, :, :], M.up(a)).then_inc(M.wu_loaded[a], 16)
                if a == 0:
                    sp.dma_start(M.wd[a][:, :, :], M.down(a)).then_inc(M.wd_loaded[a], 16)

        with ExitStack() as early:
            K.B1 = early.enter_context(nc.sbuf_tensor(f"moe_hT{layer}", [P, ND, S], F32))
            norm_stage(nc, K, V_MOE + layer * ND, f"norm_m{layer}", hn_dram=K.HN, prefetch=first_weights)
            router_stage(nc, K, A, layer, M)
        expert_stage(nc, K, A, layer, M)
        combine_stage(nc, K, layer, M)






def program(nc, A, out):
    K = Names()
    K.out = out
    K.QA = nc.dram_tensor("QA", (HA, DH, S), F32).ap()
    K.KA = nc.dram_tensor("KA", (HA, DH, S), F32).ap()
    K.QB = nc.dram_tensor("QB_", (HB, KB, S), F32).ap()
    K.KB = nc.dram_tensor("KB_", (HB, KB, S), F32).ap()
    K.HN = nc.dram_tensor("HN", (S, D), F32).ap()
    K.Z, K.YS = (nc.dram_tensor(n, (S, DI), F32).ap() for n in ("Z", "YS"))
    K.XC = nc.dram_tensor("XC", (XBC // P, P, S), F32).ap()
    K.Y = nc.dram_tensor("Y", (NBLK * P, D), F32).ap()
    with ExitStack() as ctx:
        def sb(name, shape):
            return ctx.enter_context(nc.sbuf_tensor(name, shape, F32))

        K.X, K.consts, K.vecs = sb("X", [P, NT, D]), sb("consts", [P, NC_]), sb("vecs", [P, NV])
        c = K.consts
        K.ident, K.rotA, K.rotB = c[:, C_ID:C_ID + P], c[:, C_ROTA:C_ROTA + P], c[:, C_ROTB:C_ROTB + KB]
        K.maskA, K.maskB = c[:, C_MASKA:C_MASKA + S], c[:, C_MASKB:C_MASKB + S]
        K.upper, K.strict, K.ones = (c[:, n:n + P] for n in (C_UPPER, C_STRICT, C_ONES))
        attention_layer(nc, K, A)
        moe_layer(nc, K, A, 0)
        ssd_layer(nc, K, A)
        moe_layer(nc, K, A, 1)
        norm_stage(nc, K, None, "norm_f", final=A["final_norm"])


def arrange(inputs):
    a = {k: np.asarray(v) for k, v in inputs.items()}

    def columns(v):
        return v.reshape(-1, P).T

    def rows(v):
        return np.broadcast_to(v.reshape(1, -1), (P, v.size))

    vecs = [columns(a["attn_norm"][0]), columns(a["moe_norm"][0]), columns(a["moe_norm"][1]), columns(a["ssd_norm"][0]),
            columns(a["mla_q_norm"][0]), columns(a["mla_kv_norm"][0]), columns(a["gate_norm"][0])]
    for layer in range(2):
        vecs += [rows(a["b_group"][layer]), rows(a["b_router"][layer])]
    vecs += [rows(a["dt_bias"][0]), rows(a["a_log"][0]), rows(a["d_skip"][0])]
    uq = a["w_uq"][0].reshape(QR, HB, KB)
    conv = np.concatenate([a["conv_w"][0], a["conv_b"][0][None]], axis=0)
    wr = np.concatenate([a["w_group"], a["w_router"]], axis=2)
    out = {
        "consts": constants(), "vecs": np.concatenate(vecs, axis=1),
        "x": a["x"].reshape(S, D), "positions": a["positions"].reshape(S),
        "w_in_attn": a["w_in_attn"][0],
        "w_uq": np.concatenate([uq[:, :, NOPE:], uq[:, :, :NOPE]], axis=2).reshape(QR, HB * KB),
        "w_ukv": a["w_ukv"][0], "w_out_attn": a["w_out_attn"][0],
        "w_in_ssd": a["w_in_ssd"][0], "conv": conv.T.reshape(XBC // P, P, CONV + 1),
        "w_out_ssd": a["w_out_ssd"][0],
        "w_route": wr, "w_gate": a["w_gate"], "w_up": a["w_up"], "w_down": a["w_down"],
        "final_norm": a["final_norm"],
    }
    return {k: np.ascontiguousarray(v) for k, v in out.items()}


def declare(nc, arrays):
    A = {n: nc.dram_tensor(f"in_{n}", v.shape, mybir.dt.from_np(v.dtype), kind="ExternalInput").ap() for n, v in arrays.items()}
    out = nc.dram_tensor("out", (S, D), F32, kind="ExternalOutput").ap()
    program(nc, A, out)


def kernel(**inputs):
    import concourse.bacc as bacc
    from concourse.bass_utils import run_bass_kernel_spmd

    nc = bacc.Bacc("TRN2", target_bir_lowering=False, num_devices=1)
    arrays = arrange(inputs)
    declare(nc, arrays)
    r = run_bass_kernel_spmd(nc, [{f"in_{n}": v for n, v in arrays.items()}], core_ids=[0])
    return r.results[0]["out"].reshape(1, S, D)
```

```python
import math
from contextlib import ExitStack

import numpy as np

import concourse.bass as bass
from concourse import mybir

F32 = mybir.dt.float32
I32 = mybir.dt.int32
F32R = mybir.dt.float32r
ALU = mybir.AluOpType
ACT = mybir.ActivationFunctionType
AX = mybir.AxisListType

P = 128
D = 1024
S = 1024
NT = S // P
ND = D // P
HALF = 512
EPS = 1e-6
NEG = -1e30

HA, DH, ROPE_A = 8, 64, 16
HB, NOPE, ROPE_B, DV = 8, 64, 32, 64
KB = NOPE + ROPE_B
QR, KVR = 256, 128
MIX_A = HA * DH
ATTN_IN = 3 * MIX_A + QR + KVR + ROPE_B
THETA = 500000.0
BRANCHES = ((128, 1), (512, 4), (2048, 16))

DI, HS, G, N, HD = 2048, 32, 4, 128, 64
HG = HS // G
XBC = DI + 2 * G * N
SSD_IN = DI + XBC + HS
CONV = 4

NG, EPG, NE, DE = 4, 8, 32, 512
NL = NG + NE
NBLK = NE + 2 * S // P
MAGIC = 1.5 * 2.0 ** 23

V_ATTN, V_MOE, V_SSD = 0, ND, 3 * ND
V_QN = 4 * ND
V_KVN = V_QN + QR // P
V_GATE = V_KVN + 1
V_BR = V_GATE + DI // P
V_DTB = V_BR + 2 * NL
V_ALOG = V_DTB + HS
V_DSKIP = V_ALOG + HS
NV = V_DSKIP + HS

C_ID = 0
C_MASKA = C_ID + P
C_MASKB = C_MASKA + S
C_UPPER = C_MASKB + S
C_STRICT = C_UPPER + P
C_ROTA = C_STRICT + P
C_ROTB = C_ROTA + P
C_ONES = C_ROTB + KB
C_IOTA = C_ONES + P
C_TOK = C_IOTA + P
C_FA = C_TOK + NT
C_FB = C_FA + 1
C_DESC = C_FB + 1
C_GDESC = C_DESC + EPG
C_BLK = C_GDESC + NG
NC_ = C_BLK + (NBLK - NE)


def constants():
    c = np.zeros((P, NC_), np.float32)
    c[:, C_ID:C_ID + P] = np.eye(P)
    q = np.arange(P)[:, None]
    dist = q + (S - P) - np.arange(S)[None, :]
    many = sum(((dist >= 0) & (dist <= w) & (dist % d == 0)).astype(np.float64) for w, d in BRANCHES)
    c[:, C_MASKA:C_MASKA + S] = np.where(many > 0, np.log(np.maximum(many, 1)), NEG)
    c[:, C_MASKB:C_MASKB + S] = np.where(dist >= 0, 0.0, NEG)
    i = np.arange(P)[None, :]
    c[:, C_UPPER:C_UPPER + P] = q <= i
    c[:, C_STRICT:C_STRICT + P] = q < i

    def rotation(size, starts, half):
        r = np.zeros((size, size), np.float32)
        for s in starts:
            for n in range(half):
                r[s + half + n, s + n] = -1.0
                r[s + n, s + half + n] = 1.0
        return r

    c[:, C_ROTA:C_ROTA + P] = rotation(P, (0, DH), ROPE_A // 2)
    c[:KB, C_ROTB:C_ROTB + KB] = rotation(KB, (0,), ROPE_B // 2)
    c[:, C_ONES:C_ONES + P] = 1.0
    c[:, C_IOTA:C_IOTA + P] = i
    c[:, C_TOK:C_TOK + NT] = q + P * np.arange(NT)[None, :]

    def frequencies(rot):
        return (np.float32(THETA) ** (-np.arange(0, rot, 2, dtype=np.float32) / np.float32(rot))).astype(np.float32)

    for s in (0, DH):
        c[s:s + ROPE_A, C_FA] = np.tile(frequencies(ROPE_A), 2)
    c[:ROPE_B, C_FB] = np.tile(frequencies(ROPE_B), 2)
    c[:, C_DESC:C_DESC + EPG] = EPG - np.arange(EPG)
    c[:, C_GDESC:C_GDESC + NG] = NG - np.arange(NG)
    c[:, C_BLK:C_BLK + NBLK - NE] = np.arange(NBLK - NE)
    return c


PRIMED = 4


class Stage:

    def __init__(self, nc, name):
        self.nc, self.name, self.ctx, self.sems, self.loop_sems = nc, name, ExitStack(), [], []

    def __enter__(self):
        return self

    def sb(self, name, shape, dt=F32):
        return self.ctx.enter_context(self.nc.sbuf_tensor(f"{self.name}_{name}", shape, dt))

    def ps(self, name, shape, dt=F32):
        return self.ctx.enter_context(self.nc.psum_tensor(f"{self.name}_{name}", shape, dt))

    def sem(self, name, primed=True):
        s = self.nc.alloc_semaphore(f"{self.name}_{name}")
        self.sems.append(s)
        if primed:
            self.loop_sems.append(s)
        return s

    def primed_block(self):
        for s in self.loop_sems:
            self.nc.sync.sem_inc(s, PRIMED)
        self.nc.all_engine_barrier()
        return self.ctx.enter_context(self.nc.Block())

    def __exit__(self, kind, *rest):
        self.ctx.close()
        if kind is None:
            self.nc.clear_and_free_semaphores(self.sems)
            self.nc.all_engine_barrier()


class Names:
    pass


def bits(x):
    return x.bitcast(F32)


def split_product(nc, out, left, right, start, stop):
    (lh, ll), (rh, rl) = left, right
    nc.tensor.matmul(out, lh, rh, start=start, stop=False)
    nc.tensor.matmul(out, lh, rl, start=False, stop=False)
    return nc.tensor.matmul(out, ll, rh, start=False, stop=stop)


class Chain:

    def __init__(self, eng, sem, base=0):
        self.eng, self.sem, self.base, self.n = eng, sem, base, 0

    def __call__(self, ins):
        self.n += 1
        ins.then_inc(self.sem, 1)
        self.eng.wait_ge(self.sem, self.base + self.n)


def load_stage(nc, K, A):
    with Stage(nc, "load") as st:
        loaded, chain, angle, sine = st.sem("loaded"), st.sem("chain"), st.sem("angle"), st.sem("sine")
        pos = st.sb("pos", [P, S], I32)
        ang, turns, *r = (K.B3[:, n, :] for n in range(6))
        block = st.ctx.enter_context(nc.Block())

        @block.sync
        def _(sp):
            sp.dma_start(pos[:, :], A["positions"].partition_broadcast(P)).then_inc(loaded, 16)
            sp.dma_start(K.consts[:, :], A["consts"]).then_inc(loaded, 16)
            sp.dma_start(K.vecs[:, :], A["vecs"]).then_inc(loaded, 16)
            sp.dma_start(K.X[:, :, :], A["x"].rearrange("(t p) d -> p t d", p=P)).then_inc(loaded, 16)

        @block.vector
        def _(dve):
            step = Chain(dve, chain)
            dve.wait_ge(loaded, 64)
            for n, (size, freq) in enumerate(((P, C_FA), (KB, C_FB))):
                a, k = ang[0:size, :], turns[0:size, :]
                red, cos_arg = r[2 * n][0:size, :], r[2 * n + 1][0:size, :]
                step(nc.vector.tensor_copy(a, pos[0:size, :]))
                step(nc.vector.tensor_scalar(a, a, K.consts[0:size, freq:freq + 1], None, ALU.mult))
                step(nc.vector.tensor_scalar(k, a, 1 / (2 * math.pi), MAGIC, ALU.mult, ALU.add))
                step(nc.vector.tensor_scalar(k, k, MAGIC, None, ALU.subtract))
                c1 = 6.28125
                c2 = float(np.float32(round((2 * math.pi - c1) * 2 ** 21) / 2 ** 21))
                c3 = float(np.float32(2 * math.pi - c1 - c2))
                step(nc.vector.scalar_tensor_tensor(out=a, in0=k, scalar=-c1, in1=a, op0=ALU.mult, op1=ALU.add))
                step(nc.vector.scalar_tensor_tensor(out=a, in0=k, scalar=-c2, in1=a, op0=ALU.mult, op1=ALU.add))
                step(nc.vector.scalar_tensor_tensor(out=a, in0=k, scalar=-c3, in1=a, op0=ALU.mult, op1=ALU.add))
                pi = 3.1415925
                step(nc.vector.tensor_scalar(red, a, pi, -pi, ALU.min, ALU.max))
                step(nc.vector.scalar_tensor_tensor(out=a, in0=red, scalar=-1.0, in1=red, op0=ALU.mult, op1=ALU.max))
                nc.vector.tensor_scalar(cos_arg, a, -1.0, math.pi / 2, ALU.mult, ALU.add).then_inc(angle, 1)
                dve.wait_ge(angle, n + 1)

        @block.scalar
        def _(act):
            for n, (size, c, s) in enumerate(((P, K.cosA, K.sinA), (KB, K.cosB, K.sinB))):
                act.wait_ge(angle, n + 1)
                nc.scalar.activation(s[0:size, :], r[2 * n][0:size, :], ACT.Sin)
                nc.scalar.activation(c[0:size, :], r[2 * n + 1][0:size, :], ACT.Sin).then_inc(sine, 1)


def norm_stage(nc, K, gain, name, hn_dram=None, final=None, prefetch=None, split=False):
    with Stage(nc, name) as st:
        loaded, squares, mean, root, rstd_ok = (st.sem(n) for n in ("loaded", "squares", "mean", "root", "rstd_ok"))
        rows, turned, kept, lowered = (st.sem(n) for n in ("rows", "turned", "kept", "lowered"))
        squares_act, high_ok = st.sem("squares_act"), st.sem("high_ready")
        stored = [st.sem(f"stored{a}") for a in range(2)]
        junk, junk_act = st.sb("junk", [P, 2, D]), st.sb("junk_act", [P, 2, D])
        whole = [st.sb(f"whole{a}", [P, ND, P]) for a in range(2)] if split else None
        ss, rstd = st.sb("ss", [P, NT]), st.sb("rstd", [P, NT])
        hn = [st.sb(f"hn{a}", [P, D]) for a in range(2)]
        gf = st.sb("gf", [P, D]) if final is not None else None
        tp = [st.ps(f"tp{a}", [P, ND, P]) for a in range(2)]
        block = st.ctx.enter_context(nc.Block())

        @block.vector
        def _(dve):
            def low_part(t):
                dve.wait_ge(high_ok, t + 1)
                cols = slice(t * P, (t + 1) * P)
                nc.vector.tensor_tensor(K.HL[:, :, cols], whole[t % 2][:, :, :], bits(K.HH[:, :, cols]), ALU.subtract).then_inc(lowered, 1)

            for t in range(NT // 2):
                if t >= 2:
                    dve.wait_ge(squares, t - 1)
                nc.vector.tensor_tensor_reduce(junk[:, t % 2, :], K.X[:, t, :], K.X[:, t, :], 1.0, 0.0, ALU.mult,
                                               ALU.add, ss[:, t:t + 1]).then_inc(squares, 1)
            dve.wait_ge(squares, NT // 2)
            dve.wait_ge(squares_act, NT // 2)
            nc.vector.tensor_scalar(ss[:, :], ss[:, :], 1.0 / D, EPS, ALU.mult, ALU.add).then_inc(mean, 1)
            dve.wait_ge(root, 1)
            nc.vector.reciprocal(rstd[:, :], ss[:, :]).then_inc(rstd_ok, 1)
            if final is not None:
                dve.wait_ge(loaded, 16)
            for t in range(NT):
                if final is not None:
                    dve.wait_ge(rows, t + 1)
                    nc.vector.tensor_tensor(hn[t % 2][:, :], hn[t % 2][:, :], gf[:, :], ALU.mult).then_inc(kept, 1)
                    continue
                dve.wait_ge(turned, t + 1)
                g = K.vecs[:, gain:gain + ND].unsqueeze(2).to_broadcast([P, ND, P])
                if not split:
                    nc.vector.tensor_tensor(K.B1[:, :, t * P:(t + 1) * P], tp[t % 2][:, :, :], g, ALU.mult).then_inc(kept, 1)
                    continue
                if t >= 2:
                    dve.wait_ge(lowered, t - 1)
                nc.vector.tensor_tensor(whole[t % 2][:, :, :], tp[t % 2][:, :, :], g, ALU.mult).then_inc(kept, 1)
                if t:
                    low_part(t - 1)
            if split:
                low_part(NT - 1)

        @block.scalar
        def _(act):
            def high_part(t):
                act.wait_ge(kept, t + 1)
                nc.scalar.activation(K.HH[:, :, t * P:(t + 1) * P], whole[t % 2][:, :, :], ACT.Copy).then_inc(high_ok, 1)

            for t in range(NT // 2, NT):
                if t >= NT // 2 + 2:
                    act.wait_ge(squares_act, t - NT // 2 - 1)
                nc.scalar.activation(junk_act[:, t % 2, :], K.X[:, t, :], ACT.Square, accum_out=ss[:, t:t + 1]).then_inc(squares_act, 1)
            act.wait_ge(mean, 1)
            nc.scalar.activation(ss[:, :], ss[:, :], ACT.Sqrt).then_inc(root, 1)
            act.wait_ge(rstd_ok, 1)
            for t in range(NT):
                if t >= 2:
                    if final is None:
                        act.wait_ge(turned, t - 1)
                    if final is not None or hn_dram is not None:
                        act.wait_ge(stored[t % 2], 16 * (t // 2))
                nc.scalar.activation(hn[t % 2][:, :], K.X[:, t, :], ACT.Copy, scale=rstd[:, t:t + 1]).then_inc(rows, 1)
                if split and t >= 2:
                    high_part(t - 2)
            if split:
                high_part(NT - 2)
                high_part(NT - 1)

        @block.tensor
        def _(pe):
            if final is not None:
                return
            for t in range(NT):
                pe.wait_ge(rows, t + 1)
                if t >= 2:
                    pe.wait_ge(kept, t - 1)
                for j in range(ND):
                    last = nc.tensor.transpose(tp[t % 2][:, j, :], hn[t % 2][:, j * P:(j + 1) * P], K.ident)
                last.then_inc(turned, 1)

        @block.sync
        def _(sp):
            if final is not None:
                sp.dma_start(gf[:, :], final.partition_broadcast(P)).then_inc(loaded, 16)
            dram = K.out if final is not None else hn_dram
            if dram is None:
                return
            for t in range(NT):
                sp.wait_ge(kept if final is not None else rows, t + 1)
                sp.dma_start(dram[t * P:(t + 1) * P, :], hn[t % 2][:, :]).then_inc(stored[t % 2], 16)
            if prefetch is not None:
                prefetch(sp)
            for a in range(2):
                sp.wait_ge(stored[a], 16 * (NT // 2))
            sp.nop()


def qk_stage(nc, K, A):
    with Stage(nc, "qk") as st:
        SETS = range(2)
        w = [st.sb(f"w{s}", [P, ND, P]) for s in SETS]
        raw, t1, res = ([K.B2[:, 2 * n + s, :] for s in SETS] for n in range(3))
        prj = [st.ps(f"prj{s}", [P, S]) for s in SETS]
        rot = [st.ps(f"rot{s}", [P, S]) for s in SETS]
        wl, pd, rd, td, ro, st_ = ([st.sem(f"{n}{s}") for s in SETS] for n in
                                   ("w_loaded", "projected", "raw_ready", "turned", "rope_steps", "stored"))
        zeroed, filled = st.sem("zeroed"), st.sem("filled", primed=False)
        block = st.primed_block()
        win = A["w_in_attn"].rearrange("(k p) n -> p k n", p=P)
        dst = [x.rearrange("(i a) r n -> i (a r) n", a=2) for x in (K.QA, K.KA)]
        zeros = K.B2[:, 6, :]

        @block.gpsimd
        def _(pool):
            nc.gpsimd.memset(zeros, 0.0).then_inc(zeroed, 1)
            pool.wait_ge(zeroed, 1 + PRIMED)
            for b in range(NE, NBLK):
                pool.dma_start(K.Y[b * P:(b + 1) * P, :], zeros).then_inc(filled, 16)
            pool.wait_ge(filled, 16 * (NBLK - NE))
            pool.nop()

        @block.sync
        def _(sp):
            with sp.Fori(0, HA // 2) as i:
                for s in SETS:
                    sp.wait_ge(pd[s], i + PRIMED)
                    sp.dma_start(w[s][:, :, :], win[:, :, bass.ds(i * P + s * MIX_A, P)]).then_inc(wl[s], 16)

        @block.tensor
        def _(pe):
            with pe.Fori(0, HA // 2) as i:
                for s in SETS:
                    pe.wait_ge(wl[s], (i + 1) * 16 + PRIMED)
                    pe.wait_ge(rd[s], i + PRIMED)
                    for h in range(2):
                        for k in range(ND):
                            last = nc.tensor.matmul(prj[s][:, h * HALF:(h + 1) * HALF], w[s][:, k, :],
                                                    K.B1[:, k, h * HALF:(h + 1) * HALF], start=(k == 0), stop=(k == ND - 1))
                    last.then_inc(pd[s], 1)
                for s in SETS:
                    pe.wait_ge(rd[s], i + 1 + PRIMED)
                    pe.wait_ge(ro[s], i * 4 + PRIMED)
                    for h in range(2):
                        last = nc.tensor.matmul(rot[s][:, h * HALF:(h + 1) * HALF], K.rotA, raw[s][:, h * HALF:(h + 1) * HALF],
                                                start=True, stop=True)
                    last.then_inc(td[s], 1)

        @block.scalar
        def _(act):
            with act.Fori(0, HA // 2) as i:
                for s in SETS:
                    act.wait_ge(pd[s], i + 1 + PRIMED)
                    act.wait_ge(ro[s], i * 4 + PRIMED)
                    nc.scalar.activation(raw[s], prj[s][:, :], ACT.Copy,
                                         scale=DH ** -0.5 if s == 0 else 1.0).then_inc(rd[s], 1)
                for s in SETS:
                    act.wait_ge(ro[s], i * 4 + 4 + PRIMED)
                    act.dma_start(dst[s][bass.ds(i, 1)].rearrange("a p n -> p (a n)"), res[s]).then_inc(st_[s], 16)
            for s in SETS:
                act.wait_ge(st_[s], 16 * (HA // 2) + PRIMED)
            act.nop()

        @block.vector
        def _(dve):
            with dve.Fori(0, HA // 2) as i:
                for s in SETS:
                    dve.wait_ge(rd[s], i + 1 + PRIMED)
                    nc.vector.tensor_tensor(t1[s], raw[s], K.cosA[:, :], ALU.mult).then_inc(ro[s], 1)
                    dve.wait_ge(td[s], i + 1 + PRIMED)
                    dve.wait_ge(st_[s], i * 16 + PRIMED)
                    nc.vector.tensor_tensor(res[s], rot[s][:, :], K.sinA[:, :], ALU.mult).then_inc(ro[s], 1)
                    dve.wait_ge(ro[s], i * 4 + 2 + PRIMED)
                    nc.vector.tensor_tensor(res[s], res[s], t1[s], ALU.add).then_inc(ro[s], 2)


def v_stage(nc, K, A):
    LOW = QR + KVR + ROPE_B
    with Stage(nc, "v") as st:
        wv, wl = st.sb("wv", [P, ND, MIX_A]), st.sb("wl", [P, ND, LOW])
        low = [st.sb(f"low{a}", [P, LOW]) for a in range(2)]
        junk, junk2 = st.sb("junk", [P, QR]), st.sb("junk2", [P, KVR])
        ss, rstd = st.sb("ss", [P, 2 * NT]), st.sb("rstd", [P, 2 * NT])
        pv = [st.ps(f"pv{a}", [P, MIX_A]) for a in range(2)]
        pl = [st.ps(f"pl{a}", [P, LOW]) for a in range(2)]
        tp = [st.ps(f"tp{a}", [P, 4, P]) for a in range(2)]
        loaded, loaded2, vdone, ldone, vkept, lkept, sq, sc, root, td, tk = (st.sem(n) for n in (
            "wv_loaded", "wl_loaded", "v_done", "low_done", "v_kept", "low_kept", "squares", "scaled", "root", "turned", "turn_kept"))
        block = st.ctx.enter_context(nc.Block())
        win = A["w_in_attn"].rearrange("(k p) n -> p k n", p=P)

        @block.sync
        def _(sp):
            sp.dma_start(wv[:, :, :], win[:, :, 2 * MIX_A:3 * MIX_A]).then_inc(loaded, 16)
            sp.dma_start(wl[:, :, :], win[:, :, 3 * MIX_A:ATTN_IN]).then_inc(loaded2, 16)

        @block.tensor
        def _(pe):
            def turn(t):
                pe.wait_ge(sc, 4 * t + 4)
                if t >= 2:
                    pe.wait_ge(tk, 3 * (t - 1))
                for j in range(3):
                    nc.tensor.transpose(tp[t % 2][:, j, :], low[t % 2][:, j * P:(j + 1) * P], K.ident)
                nc.tensor.transpose(tp[t % 2][0:ROPE_B, 3, :], low[t % 2][:, QR + KVR:LOW], K.ident).then_inc(td, 1)

            for t in range(NT):
                pe.wait_ge(loaded, 16)
                if t >= 2:
                    pe.wait_ge(vkept, t - 1)
                for k in range(ND):
                    last = nc.tensor.matmul(pv[t % 2][:, :], K.B1[:, k, t * P:(t + 1) * P], wv[:, k, :], start=(k == 0), stop=(k == ND - 1))
                last.then_inc(vdone, 1)
                if t >= 1:
                    turn(t - 1)
                pe.wait_ge(loaded2, 16)
                if t >= 2:
                    pe.wait_ge(lkept, t - 1)
                for k in range(ND):
                    last = nc.tensor.matmul(pl[t % 2][:, :], K.B1[:, k, t * P:(t + 1) * P], wl[:, k, :], start=(k == 0), stop=(k == ND - 1))
                last.then_inc(ldone, 1)
            turn(NT - 1)

        @block.scalar
        def _(act):
            for t in range(NT):
                act.wait_ge(vdone, t + 1)
                nc.scalar.activation(K.B3[:, t, 0:MIX_A], pv[t % 2][:, :], ACT.Copy).then_inc(vkept, 1)
                act.wait_ge(ldone, t + 1)
                if t >= 2:
                    act.wait_ge(td, t - 1)
                nc.scalar.activation(low[t % 2][:, :], pl[t % 2][:, :], ACT.Copy).then_inc(lkept, 1)
                act.wait_ge(sq, 4 * t + 4)
                nc.scalar.activation(rstd[:, 2 * t:2 * t + 2], ss[:, 2 * t:2 * t + 2], ACT.Sqrt).then_inc(root, 1)

        @block.vector
        def _(dve):
            for t in range(NT):
                a, c = t % 2, 2 * t
                dve.wait_ge(lkept, t + 1)
                if t:
                    dve.wait_ge(sq, 4 * t)
                nc.vector.tensor_tensor_reduce(junk[:, 0:QR], low[a][:, 0:QR], low[a][:, 0:QR], 1.0, 0.0, ALU.mult, ALU.add,
                                               ss[:, c:c + 1]).then_inc(sq, 1)
                nc.vector.tensor_tensor_reduce(junk2[:, :], low[a][:, QR:QR + KVR], low[a][:, QR:QR + KVR], 1.0, 0.0, ALU.mult,
                                               ALU.add, ss[:, c + 1:c + 2]).then_inc(sq, 1)
                dve.wait_ge(sq, 4 * t + 2)
                nc.vector.tensor_scalar(ss[:, c:c + 1], ss[:, c:c + 1], 1.0 / QR, EPS, ALU.mult, ALU.add).then_inc(sq, 1)
                nc.vector.tensor_scalar(ss[:, c + 1:c + 2], ss[:, c + 1:c + 2], 1.0 / KVR, EPS, ALU.mult, ALU.add).then_inc(sq, 1)
                dve.wait_ge(root, t + 1)
                nc.vector.reciprocal(rstd[:, c:c + 2], rstd[:, c:c + 2]).then_inc(sc, 1)
                dve.wait_ge(sc, 4 * t + 1)
                nc.vector.tensor_scalar(low[a][:, 0:QR], low[a][:, 0:QR], rstd[:, c:c + 1], None, ALU.mult).then_inc(sc, 1)
                nc.vector.tensor_scalar(low[a][:, QR:QR + KVR], low[a][:, QR:QR + KVR], rstd[:, c + 1:c + 2], None, ALU.mult).then_inc(sc, 2)
                dve.wait_ge(td, t + 1)
                g = K.vecs[:, V_QN:V_QN + 3].unsqueeze(2).to_broadcast([P, 3, P])
                nc.vector.tensor_tensor(K.lowT[:, :, t * P:(t + 1) * P], tp[a][:, 0:3, :], g, ALU.mult).then_inc(tk, 1)
                nc.vector.tensor_copy(K.krT[:, t * P:(t + 1) * P], tp[a][0:ROPE_B, 3, :]).then_inc(tk, 2)


def mla_stage(nc, K, A):
    with Stage(nc, "mla") as st:
        wq, wkv = st.sb("wq", [P, QR // P, HB * KB]), st.sb("wkv", [P, HB, NOPE + DV])
        raw, t1, res, kn = ([K.B2[0:r, 2 * n + a, :] for a in range(2)] for n, r in enumerate((KB, KB, KB, NOPE)))
        prj, rot = st.ps("prj", [P, S]), st.ps("rot", [P, S])
        pk = st.ps("pk", [P, S])
        pv = [st.ps(f"pv{a}", [P, HB * DV]) for a in range(2)]
        loaded, projected, raw_ok, turned, ro, shared, kdone, kkept, vdone, vkept = (st.sem(n) for n in (
            "loaded", "projected", "raw_ready", "turned", "rope_steps", "shared_stored", "k_done", "k_kept", "v_done", "v_kept"))
        stored = [st.sem(f"stored{a}") for a in range(2)]
        kstored = [st.sem(f"k_stored{a}") for a in range(2)]
        block = st.ctx.enter_context(nc.Block())

        @block.sync
        def _(sp):
            sp.dma_start(wq[:, :, :], A["w_uq"].rearrange("(k p) n -> p k n", p=P)).then_inc(loaded, 16)
            sp.dma_start(wkv[:, :, :], A["w_ukv"].rearrange("p (h n) -> p h n", h=HB)).then_inc(loaded, 16)
            for n in range(HB + 1):
                sp.wait_ge(ro, 4 * n + 4)
                if n == 0:
                    for h in range(HB):
                        sp.dma_start(K.KB[h, 0:ROPE_B, :], res[0][0:ROPE_B, :]).then_inc(shared, 16)
                    continue
                sp.dma_start(K.QB[n - 1, :, :], res[n % 2][:, :]).then_inc(stored[n % 2], 16)
                sp.wait_ge(kkept, n)
                sp.dma_start(K.KB[n - 1, ROPE_B:KB, :], kn[n % 2][:, :]).then_inc(kstored[n % 2], 16)
            sp.wait_ge(shared, 16 * HB)
            for a in range(2):
                sp.wait_ge(stored[a], 16 * (HB // 2))
                sp.wait_ge(kstored[a], 16 * (HB // 2))
            sp.nop()

        @block.tensor
        def _(pe):
            pe.wait_ge(loaded, 32)
            for n in range(HB + 1):
                rows = ROPE_B if n == 0 else KB
                if n:
                    h = n - 1
                    pe.wait_ge(raw_ok, n)
                    for half in range(2):
                        for k in range(QR // P):
                            last = nc.tensor.matmul(prj[0:KB, half * HALF:(half + 1) * HALF], wq[:, k, h * KB:(h + 1) * KB],
                                                    K.lowT[:, k, half * HALF:(half + 1) * HALF], start=(k == 0), stop=(k == 1))
                    last.then_inc(projected, 1)
                    if n >= 2:
                        pe.wait_ge(kkept, n - 1)
                    for half in range(2):
                        last = nc.tensor.matmul(pk[0:NOPE, half * HALF:(half + 1) * HALF], wkv[:, h, 0:NOPE],
                                                K.lowT[:, 2, half * HALF:(half + 1) * HALF], start=True, stop=True)
                    last.then_inc(kdone, 1)
                    t = n - 1
                    if t >= 2:
                        pe.wait_ge(vkept, t - 1)
                    nc.tensor.matmul(pv[t % 2][:, :], K.lowT[:, 2, t * P:(t + 1) * P], wkv[:, :, NOPE:NOPE + DV],
                                     start=True, stop=True).then_inc(vdone, 1)
                pe.wait_ge(raw_ok, n + 1)
                if n:
                    pe.wait_ge(ro, 4 * n)
                for half in range(2):
                    last = nc.tensor.matmul(rot[0:rows, half * HALF:(half + 1) * HALF], K.rotB[0:rows, 0:rows],
                                            raw[n % 2][0:rows, half * HALF:(half + 1) * HALF], start=True, stop=True)
                last.then_inc(turned, 1)

        @block.scalar
        def _(act):
            nc.scalar.activation(raw[0][0:ROPE_B, :], K.krT[:, :], ACT.Copy).then_inc(raw_ok, 1)
            for n in range(1, HB + 1):
                act.wait_ge(projected, n)
                if n >= 2:
                    act.wait_ge(ro, 4 * (n - 1))
                nc.scalar.activation(raw[n % 2][:, :], prj[0:KB, :], ACT.Copy, scale=KB ** -0.5).then_inc(raw_ok, 1)
                act.wait_ge(kdone, n)
                if n >= 3:
                    act.wait_ge(kstored[n % 2], 16 * ((n - 1) // 2))
                nc.scalar.activation(kn[n % 2][:, :], pk[0:NOPE, :], ACT.Copy).then_inc(kkept, 1)
                act.wait_ge(vdone, n)
                nc.scalar.activation(K.B3[:, n - 1, MIX_A:], pv[(n - 1) % 2][:, :], ACT.Copy).then_inc(vkept, 1)

        @block.vector
        def _(dve):
            for n in range(HB + 1):
                rows, a = ROPE_B if n == 0 else KB, n % 2
                dve.wait_ge(raw_ok, n + 1)
                nc.vector.tensor_tensor(t1[a][0:rows, :], raw[a][0:rows, :], K.cosB[0:rows, :], ALU.mult).then_inc(ro, 1)
                dve.wait_ge(turned, n + 1)
                if n == 2:
                    dve.wait_ge(shared, 16 * HB)
                if n >= 3:
                    dve.wait_ge(stored[n % 2], 16 * ((n - 1) // 2))
                nc.vector.tensor_tensor(res[a][0:rows, :], rot[0:rows, :], K.sinB[0:rows, :], ALU.mult).then_inc(ro, 1)
                dve.wait_ge(ro, 4 * n + 2)
                nc.vector.tensor_tensor(res[a][0:rows, :], res[a][0:rows, :], t1[a][0:rows, :], ALU.add).then_inc(ro, 2)


def attention_stage(nc, K, name, rows, q_dram, k_dram, mask, first_head, paired, early_dma=None):
    HEADS = 8
    TILES = [(a, t) for a in range(2) for t in range(NT)]
    NN = len(TILES)
    with Stage(nc, name) as st:
        rows = 2 * DH if paired else rows
        q = [st.sb(f"q{a}", [rows, S]) for a in range(2)]
        k = [st.sb(f"k{a}", [rows, S]) for a in range(2)]
        sm = [st.sb(f"sm{a}", [P, S]) for a in range(2)]
        pr = [st.sb(f"pr{a}", [P, S]) for a in range(2)]
        pT = [st.sb(f"pT{a}", [P, NT, P]) for a in range(2)]
        mx, nmx, den, rden, spare = (st.sb(n, [P, 2]) for n in ("mx", "nmx", "den", "rden", "spare"))
        sc = [st.ps(f"sc{a}", [P, S]) for a in range(2)]
        tp = [st.ps(f"tp{a}", [P, 4, P]) for a in range(2)]
        ov = [st.ps(f"ov{a}", [P, DH]) for a in range(2)]
        loaded = [st.sem(f"loaded{a}") for a in range(2)]
        scored, masked, negated, exped, t_lo, t_hi, lo_kept, hi_kept, summed, recip, out_ok = (st.sem(n) for n in (
            "scored", "masked", "negated", "exped", "turned_low", "turned_high", "low_kept", "high_kept", "summed", "recip", "out_ready"))
        zeroed = st.sem("zeroed", primed=False)
        block = st.primed_block()
        high = [sum(t >= 4 for _, t in TILES[:n]) for n in range(NN + 1)]

        @block.sync
        def _(sp):
            def load(i, a):
                src = q_dram[bass.ds(i * 2 + a, 1)].rearrange("a r n -> r (a n)")
                keys = k_dram[bass.ds(i * 2, 2)] if paired else k_dram[bass.ds(i * 2 + a, 1)]
                mine = slice(a * DH, (a + 1) * DH) if paired else slice(0, rows)
                sp.dma_start(q[a][mine, :], src).then_inc(loaded[a], 16)
                sp.dma_start(k[a][:, :], keys.rearrange("a r n -> (a r) n")).then_inc(loaded[a], 16)

            for a in range(2):
                load(0, a)
            if early_dma is not None:
                early_dma(sp)
            with sp.Fori(0, HEADS // 2 - 1) as i:
                for a in range(2):
                    sp.wait_ge(scored, i * NN + (a + 1) * NT + PRIMED)
                    load(i + 1, a)

        @block.gpsimd
        def _(pool):
            for a in range(2):
                if paired:
                    nc.gpsimd.memset(q[a][(1 - a) * DH:(2 - a) * DH, :], 0.0).then_inc(zeroed, 1)

        @block.tensor
        def _(pe):
            if paired:
                pe.wait_ge(zeroed, 2)
            with pe.Fori(0, HEADS // 2) as i:
                base, hbase = i * NN, i * high[NN]

                def scores(n):
                    a, t = TILES[n]
                    if t == 0:
                        pe.wait_ge(loaded[a], i * 32 + 32 + PRIMED)
                    pe.wait_ge(masked, base + n - 1 + PRIMED)
                    w = (t + 1) * P
                    for c in range(0, w, HALF):
                        e = min(c + HALF, w)
                        last = nc.tensor.matmul(sc[n % 2][:, c:e], q[a][:, t * P:(t + 1) * P], k[a][:, c:e], start=True, stop=True)
                    last.then_inc(scored, 1)

                def turn(n):
                    _, t = TILES[n]
                    pe.wait_ge(exped, base + n + 1 + PRIMED)
                    pe.wait_ge(lo_kept, base + n + PRIMED)
                    for j in range(min(t + 1, 4)):
                        last = nc.tensor.transpose(tp[0][:, j, :], pr[n % 2][:, j * P:(j + 1) * P], K.ident)
                    last.then_inc(t_lo, 1)
                    if t >= 4:
                        pe.wait_ge(hi_kept, hbase + high[n] + PRIMED)
                        for j in range(4, t + 1):
                            last = nc.tensor.transpose(tp[1][:, j - 4, :], pr[n % 2][:, j * P:(j + 1) * P], K.ident)
                        last.then_inc(t_hi, 1)

                def weigh(n):
                    a, t = TILES[n]
                    pe.wait_ge(lo_kept, base + n + 1 + PRIMED)
                    if t >= 4:
                        pe.wait_ge(hi_kept, hbase + high[n + 1] + PRIMED)
                    pe.wait_ge(out_ok, base + n - 1 + PRIMED)
                    for j in range(t + 1):
                        v = K.B3[:, j, bass.ds((i * 2 + (a + first_head)) * DH, DH)]
                        last = nc.tensor.matmul(ov[n % 2][:, :], pT[n % 2][:, j, :], v, start=(j == 0), stop=(j == t))
                    last.then_inc(summed, 1)

                scores(0)
                for n in range(NN):
                    if n + 1 < NN:
                        scores(n + 1)
                    if n >= 1:
                        weigh(n - 1)
                    turn(n)
                weigh(NN - 1)

        @block.vector
        def _(dve):
            with dve.Fori(0, HEADS // 2) as i:
                base, hbase = i * NN, i * high[NN]

                def keep_low(n):
                    _, t = TILES[n]
                    dve.wait_ge(t_lo, base + n + 1 + PRIMED)
                    dve.wait_ge(summed, base + n - 1 + PRIMED)
                    c = min(t + 1, 4)
                    nc.vector.tensor_copy(pT[n % 2][:, 0:c, :], tp[0][:, 0:c, :]).then_inc(lo_kept, 1)

                def invert(n):
                    dve.wait_ge(exped, base + n + 1 + PRIMED)
                    dve.wait_ge(out_ok, base + n - 1 + PRIMED)
                    nc.vector.reciprocal(rden[:, n % 2:n % 2 + 1], den[:, n % 2:n % 2 + 1]).then_inc(recip, 1)

                for n, (a, t) in enumerate(TILES):
                    w = (t + 1) * P
                    dve.wait_ge(scored, base + n + 1 + PRIMED)
                    dve.wait_ge(exped, base + n - 1 + PRIMED)
                    if n >= 2:
                        invert(n - 2)
                    else:
                        nc.vector.memset(spare[:, n:n + 1], 0.0)
                    nc.vector.tensor_tensor_reduce(sm[n % 2][:, 0:w], sc[n % 2][:, 0:w], mask[:, S - w:S], 1.0, NEG, ALU.add, ALU.max,
                                                   mx[:, n % 2:n % 2 + 1]).then_inc(masked, 1)
                    dve.wait_ge(masked, base + n + 1 + PRIMED)
                    nc.vector.tensor_scalar(nmx[:, n % 2:n % 2 + 1], mx[:, n % 2:n % 2 + 1], -1.0, None, ALU.mult).then_inc(negated, 1)
                    if n >= 1:
                        keep_low(n - 1)
                invert(NN - 2)
                keep_low(NN - 1)
                invert(NN - 1)

        @block.scalar
        def _(act):
            with act.Fori(0, HEADS // 2) as i:
                base, hbase = i * NN, i * high[NN]

                def finish(n):
                    a, t = TILES[n]
                    act.wait_ge(summed, base + n + 1 + PRIMED)
                    act.wait_ge(recip, base + n + 1 + PRIMED)
                    o = K.B2[:, t, bass.ds((i * 2 + (a + first_head)) * DH, DH)]
                    nc.scalar.activation(o, ov[n % 2][:, :], ACT.Copy, scale=rden[:, n % 2:n % 2 + 1]).then_inc(out_ok, 1)

                def keep_high(n):
                    _, t = TILES[n]
                    if t >= 4:
                        act.wait_ge(t_hi, hbase + high[n + 1] + PRIMED)
                        act.wait_ge(summed, base + n - 1 + PRIMED)
                        nc.scalar.activation(pT[n % 2][:, 4:t + 1, :], tp[1][:, 0:t - 3, :], ACT.Copy).then_inc(hi_kept, 1)

                for n, (a, t) in enumerate(TILES):
                    w = (t + 1) * P
                    act.wait_ge(negated, base + n + 1 + PRIMED)
                    if n >= 2:
                        act.wait_ge(t_lo, base + n - 1 + PRIMED)
                        act.wait_ge(t_hi, hbase + high[n - 1] + PRIMED)
                        act.wait_ge(recip, base + n - 1 + PRIMED)
                    else:
                        act.wait_ge(recip, base + PRIMED)
                    nc.scalar.activation(pr[n % 2][:, 0:w], sm[n % 2][:, 0:w], ACT.Exp, bias=nmx[:, n % 2:n % 2 + 1],
                                         accum_out=den[:, n % 2:n % 2 + 1]).then_inc(exped, 1)
                    if n >= 1:
                        keep_high(n - 1)
                    if n >= 2:
                        finish(n - 2)
                keep_high(NN - 1)
                finish(NN - 2)
                finish(NN - 1)


def out_stage(nc, K, A):
    with Stage(nc, "out") as st:
        oT = [st.sb(f"oT{a}", [P, ND, P]) for a in range(2)]
        tp = [st.ps(f"tp{a}", [P, ND, P]) for a in range(2)]
        py = [st.ps(f"py{a}", [P, D]) for a in range(2)]
        turned, kept, done, added = (st.sem(n) for n in ("turned", "kept", "done", "added"))
        block = st.ctx.enter_context(nc.Block())

        @block.tensor
        def _(pe):
            def turn(t):
                if t >= 2:
                    pe.wait_ge(kept, t - 1)
                for j in range(ND):
                    last = nc.tensor.transpose(tp[t % 2][:, j, :], K.B2[:, t, j * P:(j + 1) * P], K.ident)
                last.then_inc(turned, 1)

            turn(0)
            pe.wait_ge(K.wo_loaded, 16)
            for t in range(NT):
                if t + 1 < NT:
                    turn(t + 1)
                pe.wait_ge(kept, t + 1)
                if t >= 2:
                    pe.wait_ge(added, t - 1)
                for h in range(2):
                    for k in range(ND):
                        last = nc.tensor.matmul(py[t % 2][:, h * HALF:(h + 1) * HALF], oT[t % 2][:, k, :],
                                                K.B1[:, k, h * HALF:(h + 1) * HALF], start=(k == 0), stop=(k == ND - 1))
                last.then_inc(done, 1)

        @block.scalar
        def _(act):
            for t in range(NT):
                act.wait_ge(turned, t + 1)
                if t >= 2:
                    act.wait_ge(done, t - 1)
                nc.scalar.activation(oT[t % 2][:, :, :], tp[t % 2][:, :, :], ACT.Copy).then_inc(kept, 1)

        @block.vector
        def _(dve):
            for t in range(NT):
                dve.wait_ge(done, t + 1)
                nc.vector.tensor_tensor(K.X[:, t, :], K.X[:, t, :], py[t % 2][:, :], ALU.add).then_inc(added, 1)


def attention_layer(nc, K, A):
    with Stage(nc, "attn_layer") as outer:
        ctx, K.wo_loaded = outer.ctx, outer.sem("wo_loaded")

        def sb(name, shape):
            return ctx.enter_context(nc.sbuf_tensor(name, shape, F32))

        K.B2, K.B3, K.B1 = (sb(n, [P, ND, S]) for n in ("B2", "B3", "B1"))
        with ExitStack() as early:
            def tmp(name, shape):
                return early.enter_context(nc.sbuf_tensor(name, shape, F32))

            K.lowT, K.krT = tmp("lowT", [P, 3, S]), tmp("krT", [ROPE_B, S])
            K.cosA, K.sinA, K.cosB, K.sinB = (tmp(n, [P, S]) for n in ("cosA", "sinA", "cosB", "sinB"))
            load_stage(nc, K, A)
            norm_stage(nc, K, V_ATTN, "norm_a")
            qk_stage(nc, K, A)
            v_stage(nc, K, A)
            mla_stage(nc, K, A)

        def out_weights(sp):
            sp.dma_start(K.B1[:, :, :], A["w_out_attn"].rearrange("(k p) n -> p k n", p=P)).then_inc(K.wo_loaded, 16)

        attention_stage(nc, K, "att_a", DH, K.QA, K.KA, K.maskA, 0, True, out_weights)
        attention_stage(nc, K, "att_b", KB, K.QB, K.KB, K.maskB, HA, False)
        out_stage(nc, K, A)


DT, DTA, CS, ECS, TOEND, ETOT, SKIP = range(7)


def gate_stage(nc, K, A):
    with Stage(nc, "gate") as st:
        raw = [st.sb(f"raw{a}", [P, 2, HALF]) for a in range(2)]
        wh, wl = ([st.sb(f"{n}{a}", [P, ND, HALF], F32R) for a in range(2)] for n in ("w_high", "w_low"))
        wdt = st.sb("wdt", [P, ND, HS])
        wdt_h, wdt_l = st.sb("wdt_high", [P, ND, HS], F32R), st.sb("wdt_low", [P, ND, HS], F32R)
        z = [st.sb(f"z{a}", [P, HALF]) for a in range(2)]
        pos, ab, u, ln, rate = (st.sb(n, [P, NT, HS]) for n in ("pos", "ab", "u", "ln", "rate"))
        pz = [st.ps(f"pz{a}", [P, HALF]) for a in range(2)]
        pdt, pcs = st.ps("pdt", [P, NT, HS]), st.ps("pcs", [P, 2, NT, HS])
        raw_loaded = [st.sem(f"raw_loaded{a}") for a in range(2)]
        high_ok, low_ok, dt_high, dt_low = (st.sem(n) for n in ("w_high_ready", "w_low_ready", "dt_high_ready", "dt_low_ready"))
        z_stored = [st.sem(f"z_stored{a}") for a in range(2)]
        z_done = [st.sem(f"z_done{a}") for a in range(2)]
        dt_loaded, dt_done, dta_ok, cs_done, chain, small_in, small_out, z_kept = (st.sem(n) for n in (
            "dt_loaded", "dt_done", "dta_ready", "cs_done", "chain", "small_in", "small_out", "z_kept"))
        block = st.primed_block()
        win = A["w_in_ssd"].rearrange("(k p) n -> p k n", p=P)
        ROUNDS = DI // HALF // 2
        PER = 2 * NT
        Q = ND // 2

        @block.sync
        def _(sp):
            sp.dma_start(wdt[:, :, :], win[:, :, DI + XBC:SSD_IN]).then_inc(dt_loaded, 16)
            with sp.Fori(0, ROUNDS) as i:
                for a in range(2):
                    for q in range(Q):
                        sp.wait_ge(low_ok, i * (2 * Q) + (a * Q + q - 1) + PRIMED)
                        sp.dma_start(raw[q % 2][:, :, :], win[:, 2 * q:2 * q + 2, bass.ds((i * 2 + a) * HALF, HALF)]).then_inc(raw_loaded[q % 2], 16)

        @block.gpsimd
        def _(pool):
            Qe = nc.gpsimd
            pool.wait_ge(dt_loaded, 16 + PRIMED)
            Qe.tensor_copy(wdt_h[:, :, :], wdt[:, :, :]).then_inc(dt_high, 1)
            pool.wait_ge(dt_high, 1 + PRIMED)
            Qe.tensor_tensor(wdt_l[:, :, :], wdt[:, :, :], bits(wdt_h[:, :, :]), ALU.subtract).then_inc(dt_low, 1)
            with pool.Fori(0, ROUNDS) as i:
                for a in range(2):
                    for q in range(Q):
                        part = slice(2 * q, 2 * q + 2)
                        pool.wait_ge(raw_loaded[q % 2], i * (Q * 16) + (a * (Q // 2) + q // 2 + 1) * 16 + PRIMED)
                        pool.wait_ge(z_done[a], i * NT + PRIMED)
                        Qe.tensor_tensor(wh[a][:, part, :], raw[q % 2][:, :, :], K.ones[:, 0:2].unsqueeze(2).to_broadcast([P, 2, HALF]), ALU.mult).then_inc(high_ok, 1)

        @block.tensor
        def _(pe):
            def left(t, k):
                return (x[:, k, t * P:(t + 1) * P] for x in (K.HH, K.HL))

            pe.wait_ge(dt_low, 1 + PRIMED)
            for t in range(NT):
                for k in range(ND):
                    last = split_product(nc, pdt[:, t, :], left(t, k), (wdt_h[:, k, :], wdt_l[:, k, :]), k == 0, k == ND - 1)
            last.then_inc(dt_done, 1)
            with pe.Fori(0, ROUNDS) as i:
                for a in range(2):
                    pe.wait_ge(low_ok, i * (2 * Q) + Q * (a + 1) + PRIMED)
                    for t in range(NT):
                        n = a * NT + t
                        pe.wait_ge(z_kept, i * PER + (n - 1) + PRIMED)
                        for k in range(ND):
                            last = split_product(nc, pz[n % 2][:, :], left(t, k), (wh[a][:, k, :], wl[a][:, k, :]), k == 0, k == ND - 1)
                        last.then_inc(z_done[a], 1)
            pe.wait_ge(dta_ok, 1 + PRIMED)
            nc.tensor.matmul(pcs[:, 0, :, :], K.upper, K.heads[:, DTA, :, :], start=True, stop=True)
            nc.tensor.matmul(pcs[:, 1, :, :], K.ones, K.heads[:, DTA, :, :], start=True, stop=True).then_inc(cs_done, 1)

        @block.scalar
        def _(act):
            act.wait_ge(small_in, 1 + PRIMED)
            nc.scalar.activation(ab[:, :, :], ab[:, :, :], ACT.Exp)
            nc.scalar.activation(rate[:, :, :], rate[:, :, :], ACT.Exp).then_inc(small_out, 1)
            act.wait_ge(small_in, 2 + PRIMED)
            nc.scalar.activation(ln[:, :, :], u[:, :, :], ACT.Ln).then_inc(small_out, 1)
            with act.Fori(0, ROUNDS) as i:
                for n in range(PER):
                    a, t = n // NT, n % NT
                    act.wait_ge(z_done[a], i * NT + (t + 1) + PRIMED)
                    act.wait_ge(z_stored[n % 2], i * (PER // 2 * 16) + (n // 2) * 16 + PRIMED)
                    nc.scalar.activation(z[n % 2][:, :], pz[n % 2][:, :], ACT.Silu).then_inc(z_kept, 1)
                    act.wait_ge(z_kept, i * PER + (n + 1) + PRIMED)
                    act.dma_start(K.Z[t * P:(t + 1) * P, bass.ds((i * 2 + a) * HALF, HALF)], z[n % 2][:, :]).then_inc(z_stored[n % 2], 16)
            for a in range(2):
                act.wait_ge(z_stored[a], ROUNDS * PER // 2 * 16 + PRIMED)
            act.wait_ge(small_in, 3 + PRIMED)
            H = K.heads
            for q in (ECS, TOEND, ETOT):
                last = nc.scalar.activation(H[:, q, :, :], H[:, q, :, :], ACT.Exp)
            last.then_inc(small_out, 1)

        @block.vector
        def _(dve):
            step, V, H = Chain(dve, chain, PRIMED), nc.vector, K.heads

            def per_head(column):
                return K.vecs[:, column:column + HS].unsqueeze(1).to_broadcast([P, NT, HS])

            def low(a, base):
                for q in range(Q):
                    part = slice(2 * q, 2 * q + 2)
                    dve.wait_ge(high_ok, base + (q + 1) + PRIMED)
                    V.tensor_tensor(wl[a][:, part, :], raw[q % 2][:, :, :], bits(wh[a][:, part, :]), ALU.subtract).then_inc(low_ok, 1)

            low(0, 0)
            step(V.tensor_copy(H[:, SKIP, :, :], per_head(V_DSKIP)))
            step(V.tensor_copy(rate[:, :, :], per_head(V_ALOG)))
            dve.wait_ge(dt_done, 1 + PRIMED)
            step(V.tensor_tensor(pos[:, :, :], pdt[:, :, :], per_head(V_DTB), ALU.add))
            step(V.scalar_tensor_tensor(out=ab[:, :, :], in0=pos[:, :, :], scalar=-1.0, in1=pos[:, :, :], op0=ALU.mult, op1=ALU.min))
            V.tensor_scalar(pos[:, :, :], pos[:, :, :], 0.0, None, ALU.max).then_inc(small_in, 1)
            dve.wait_ge(small_out, 1 + PRIMED)
            V.tensor_scalar(u[:, :, :], ab[:, :, :], 1.0, None, ALU.add).then_inc(small_in, 1)
            dve.wait_ge(small_out, 2 + PRIMED)
            step(V.tensor_scalar(u[:, :, :], u[:, :, :], -1.0, None, ALU.add))
            step(V.tensor_tensor(ln[:, :, :], ln[:, :, :], ab[:, :, :], ALU.mult))
            step(V.scalar_tensor_tensor(out=ab[:, :, :], in0=u[:, :, :], scalar=0.0, in1=ab[:, :, :], op0=ALU.is_equal, op1=ALU.mult))
            step(V.scalar_tensor_tensor(out=ln[:, :, :], in0=u[:, :, :], scalar=0.0, in1=ln[:, :, :], op0=ALU.is_gt, op1=ALU.mult))
            step(V.tensor_scalar(u[:, :, :], u[:, :, :], 2.0 ** -24, None, ALU.max))
            step(V.reciprocal(u[:, :, :], u[:, :, :]))
            step(V.tensor_tensor(ln[:, :, :], ln[:, :, :], u[:, :, :], ALU.mult))
            step(V.tensor_tensor(ln[:, :, :], ln[:, :, :], ab[:, :, :], ALU.add))
            step(V.tensor_tensor(H[:, DT, :, :], pos[:, :, :], ln[:, :, :], ALU.add))
            V.scalar_tensor_tensor(out=H[:, DTA, :, :], in0=rate[:, :, :], scalar=-1.0, in1=H[:, DT, :, :], op0=ALU.mult,
                                   op1=ALU.mult).then_inc(dta_ok, 1)
            for chunk in range(1, 2 * ROUNDS):
                low(chunk % 2, chunk * Q)
            dve.wait_ge(cs_done, 1 + PRIMED)
            step(V.tensor_copy(H[:, CS, :, :], pcs[:, 0, :, :]))
            step(V.tensor_copy(H[:, ECS, :, :], pcs[:, 0, :, :]))
            step(V.tensor_copy(H[:, ETOT, :, :], pcs[:, 1, :, :]))
            V.tensor_tensor(H[:, TOEND, :, :], H[:, ETOT, :, :], H[:, CS, :, :], ALU.subtract).then_inc(small_in, 1)


def conv_stage(nc, K, A):
    LEFT = CONV - 1
    with Stage(nc, "conv") as st:
        raw = [st.sb(f"raw{a}", [P, ND, P]) for a in range(2)]
        wh, wl = ([st.sb(f"{n}{a}", [P, ND, P], F32R) for a in range(2)] for n in ("w_high", "w_low"))
        tap = [st.sb(f"tap{a}", [P, CONV + 1]) for a in range(2)]
        u = [st.sb(f"u{a}", [P, LEFT + S]) for a in range(2)]
        acc = [st.sb(f"acc{a}", [P, S]) for a in range(2)]
        c = [st.sb(f"c{a}", [P, S]) for a in range(2)]
        prj = [st.ps(f"prj{a}", [P, S]) for a in range(2)]
        w_loaded, high_ok, low_ok, tap_loaded, done, u_ok, steps, c_ok, stored = ([st.sem(f"{n}{a}") for a in range(2)] for n in (
            "w_loaded", "w_high_ready", "w_low_ready", "tap_loaded", "done", "u_ready", "steps", "c_ready", "stored"))
        padded = st.sem("padded")
        block = st.primed_block()
        win = A["w_in_ssd"].rearrange("(k p) n -> p k n", p=P)
        ROUNDS = XBC // P // 2

        @block.sync
        def _(sp):
            with sp.Fori(0, ROUNDS) as i:
                for a in range(2):
                    sp.wait_ge(low_ok[a], i + PRIMED)
                    sp.dma_start(raw[a][:, :, :], win[:, :, bass.ds((i * 2 + a) * P + DI, P)]).then_inc(w_loaded[a], 16)
                    sp.wait_ge(c_ok[a], i + PRIMED)
                    sp.dma_start(tap[a][:, :], A["conv"][bass.ds(i * 2 + a, 1)].rearrange("a p n -> p (a n)")).then_inc(tap_loaded[a], 16)

        @block.tensor
        def _(pe):
            with pe.Fori(0, ROUNDS) as i:
                for a in range(2):
                    pe.wait_ge(low_ok[a], i + 1 + PRIMED)
                    pe.wait_ge(u_ok[a], i + PRIMED)
                    for h in range(2):
                        cols = slice(h * HALF, (h + 1) * HALF)
                        for k in range(ND):
                            last = split_product(nc, prj[a][:, cols], (wh[a][:, k, :], wl[a][:, k, :]),
                                                 (K.HH[:, k, cols], K.HL[:, k, cols]), k == 0, k == ND - 1)
                    last.then_inc(done[a], 1)

        @block.gpsimd
        def _(pool):
            with pool.Fori(0, ROUNDS) as i:
                for a in range(2):
                    pool.wait_ge(w_loaded[a], i * 16 + 16 + PRIMED)
                    pool.wait_ge(done[a], i + PRIMED)
                    nc.gpsimd.tensor_tensor(wh[a][:, :, :], raw[a][:, :, :], K.ones[:, 0:ND].unsqueeze(2).to_broadcast([P, ND, P]), ALU.mult).then_inc(high_ok[a], 1)
                    pool.wait_ge(high_ok[a], i + 1 + PRIMED)
                    nc.gpsimd.tensor_tensor(wl[a][:, :, :], raw[a][:, :, :], bits(wh[a][:, :, :]), ALU.subtract).then_inc(low_ok[a], 1)

        @block.vector
        def _(dve):
            for a in range(2):
                last = nc.vector.memset(u[a][:, 0:LEFT], 0.0)
            last.then_inc(padded, 1)
            dve.wait_ge(padded, 1 + PRIMED)
            with dve.Fori(0, ROUNDS) as i:
                for a in range(2):
                    dve.wait_ge(u_ok[a], i + 1 + PRIMED)
                    dve.wait_ge(tap_loaded[a], i * 16 + 16 + PRIMED)
                    dve.wait_ge(c_ok[a], i + PRIMED)
                    nc.vector.tensor_scalar(acc[a][:, :], u[a][:, 0:S], tap[a][:, 0:1], None, ALU.mult).then_inc(steps[a], 1)
                    for n in range(1, CONV):
                        dve.wait_ge(steps[a], i * CONV + n + PRIMED)
                        nc.vector.scalar_tensor_tensor(out=acc[a][:, :], in0=u[a][:, n:n + S], scalar=tap[a][:, n:n + 1], in1=acc[a][:, :],
                                                       op0=ALU.mult, op1=ALU.add).then_inc(steps[a], 1)

        @block.scalar
        def _(act):
            act.wait_ge(padded, 1 + PRIMED)
            with act.Fori(0, ROUNDS) as i:
                def keep(a):
                    act.wait_ge(done[a], i + 1 + PRIMED)
                    nc.scalar.activation(u[a][:, LEFT:], prj[a][:, :], ACT.Copy).then_inc(u_ok[a], 1)

                def silu(a):
                    act.wait_ge(steps[a], i * CONV + CONV + PRIMED)
                    act.wait_ge(stored[a], i * 16 + PRIMED)
                    nc.scalar.activation(c[a][:, :], acc[a][:, :], ACT.Silu, bias=tap[a][:, CONV:CONV + 1]).then_inc(c_ok[a], 1)
                    act.wait_ge(c_ok[a], i + 1 + PRIMED)
                    act.dma_start(K.XC[bass.ds(i * 2 + a, 1)].rearrange("a p n -> p (a n)"), c[a][:, :]).then_inc(stored[a], 16)

                keep(0)
                silu(0)
                keep(1)
                silu(1)
            for a in range(2):
                act.wait_ge(stored[a], ROUNDS * 16 + PRIMED)
            act.nop()


def scan_stage(nc, K, A, early_dma):
    GW = HG * HD
    with Stage(nc, "scan") as st:
        PAR = range(2)
        RING = 4
        xT = [st.sb(f"xT{a}", [P, GW // P, P]) for a in range(RING)]
        bT, cT = [st.sb(f"bT{a}", [P, P]) for a in range(RING)], [st.sb(f"cT{a}", [P, P]) for a in range(RING)]
        z = [st.sb(f"z{a}", [P, GW]) for a in range(RING)]
        H = st.sb("H", [P, 7, NT, HG])
        cbm = [st.sb(f"cbm{a}", [P, P]) for a in PAR]
        dec, W = ([st.sb(f"{n}{a}", [P, HG, P]) for a in PAR] for n in ("dec", "W"))
        bt = [st.sb(f"bt{a}", [P, N]) for a in PAR]
        y = [st.sb(f"y{a}", [P, GW]) for a in range(RING)]
        xs, xdt, xde, xsk, yi, sq = ([st.sb(f"{n}{a}", [P, GW]) for a in PAR] for n in ("xs", "xdt", "xde", "xsk", "yi", "sq"))
        state = st.sb("state", [P, GW])
        ssg = st.sb("ssg", [P, NT])
        pcb, pbt = st.ps("pcb", [P, HALF])[:, 0:P], st.ps("pbt", [P, HALF])[:, 0:P]
        pr, px, pyi, py, pst = st.ps("pr", [P, HG, P]), st.ps("px", [P, GW]), st.ps("pyi", [P, GW]), st.ps("py", [P, GW]), st.ps("pst", [P, GW])
        loaded, y_stored = [st.sem(f"loaded{a}") for a in range(RING)], [st.sem(f"y_stored{a}") for a in range(RING)]
        heads_ok, cb_done, r_done, x_turned, yi_done, st_done, y_done = (st.sem(n) for n in (
            "heads_ready", "cb_done", "r_done", "x_turned", "yi_done", "st_done", "y_done"))
        bt_ok, xs_ok, e_ok, ss_ok = (st.sem(n) for n in ("bt_ready", "xs_ready", "decay_ready", "squares"))
        cbm_ok, seg_ok, xdt_ok, yi_ok, y_ok, st_ok = (st.sem(n) for n in ("cbm_ready", "seg_ready", "xdt_ready", "yi_ready", "y_ready", "state_ready"))
        w_lo, w_ok, xde_ok, faded, skip_ok, skipped, gated = (st.sem(n) for n in ("w_low_ready", "w_ready", "xde_ready", "faded", "skip_ready", "skipped", "gated"))
        LO = HG // 2
        block = st.primed_block()

        def heads(q, c, width):
            return H[:, q, c, :].unsqueeze(2).to_broadcast([P, HG, width])

        def byhead(x):
            return x.rearrange("p (h d) -> p h d", h=HG)

        def before(base, c, back):
            return base + (c - back + 1)

        @block.sync
        def _(sp):
            early_dma(sp)
            with sp.Fori(0, G) as i:
                base = i * NT
                for c in range(NT):
                    a, tok = c % RING, slice(c * P, (c + 1) * P)
                    sp.wait_ge(y_done, before(base, c, RING) + PRIMED)
                    sp.wait_ge(gated, before(base, c, RING) + PRIMED)
                    sp.dma_start(xT[a][:, :, :], K.XC[bass.ds(i * (GW // P), GW // P), :, tok].rearrange("k p n -> p k n")).then_inc(loaded[a], 16)
                    for buf, first in ((bT, DI // P), (cT, DI // P + G)):
                        sp.dma_start(buf[a][:, :], K.XC[bass.ds(i + first, 1), :, tok].rearrange("k p n -> p (k n)")).then_inc(loaded[a], 16)
                    sp.dma_start(z[a][:, :], K.Z[tok, bass.ds(i * GW, GW)]).then_inc(loaded[a], 16)

        def arrived(eng, i, c):
            eng.wait_ge(loaded[c % RING], i * (NT // RING * 64) + (c // RING + 1) * 64 + PRIMED)

        @block.tensor
        def _(pe):
            with pe.Fori(0, G) as i:
                base = i * NT

                def front(c):
                    r = c % RING
                    arrived(pe, i, c)
                    pe.wait_ge(cbm_ok, base + c + PRIMED)
                    pe.wait_ge(bt_ok, base + c + PRIMED)
                    nc.tensor.matmul(pcb[:, :], bT[r][:, :], cT[r][:, :], start=True, stop=True).then_inc(cb_done, 1)
                    if c == 0:
                        pe.wait_ge(heads_ok, i + 1 + PRIMED)
                    pe.wait_ge(seg_ok, base + c + PRIMED)
                    for h in range(HG):
                        last = nc.tensor.matmul(pr[:, h, :], H[:, DTA, c, h:h + 1].to_broadcast([P, P]), K.upper, start=True, stop=True)
                    last.then_inc(r_done, 1)
                    pe.wait_ge(xs_ok, base + c + PRIMED)
                    for k in range(GW // P):
                        nc.tensor.transpose(px[:, k * P:(k + 1) * P], xT[r][:, k, :], K.ident)
                    nc.tensor.transpose(pbt[:, :], bT[r][:, :], K.ident).then_inc(x_turned, 1)

                def back(c):
                    a = c % 2
                    pe.wait_ge(st_ok, base + (c + 1) + PRIMED)
                    pe.wait_ge(y_ok, base + c + PRIMED)
                    nc.tensor.matmul(pyi[:, :], cT[c % RING][:, :], state[:, :], start=True, stop=True).then_inc(yi_done, 1)
                    if c + 1 < NT:
                        pe.wait_ge(bt_ok, base + (c + 1) + PRIMED)
                        pe.wait_ge(xde_ok, base + (c + 1) + PRIMED)
                        nc.tensor.matmul(pst[:, :], bt[a][:, :], xde[a][:, :], start=True, stop=True).then_inc(st_done, 1)
                    pe.wait_ge(w_lo, base + (c + 1) + PRIMED)
                    pe.wait_ge(w_ok, base + (c + 1) + PRIMED)
                    pe.wait_ge(xdt_ok, base + (c + 1) + PRIMED)
                    for h in range(HG):
                        last = nc.tensor.matmul(py[:, h * HD:(h + 1) * HD], W[a][:, h, :], xdt[a][:, h * HD:(h + 1) * HD], start=True, stop=True)
                    last.then_inc(y_done, 1)

                front(0)
                for c in range(NT):
                    if c + 1 < NT:
                        front(c + 1)
                    back(c)

        @block.scalar
        def _(act):
            with act.Fori(0, G) as i:
                base = i * NT

                def squares(c):
                    a, r = c % 2, c % RING
                    act.wait_ge(ss_ok, before(base, c, 2) + PRIMED)
                    act.wait_ge(gated, base + (c + 1) + PRIMED)
                    if c == 0:
                        act.wait_ge(heads_ok, i + 1 + PRIMED)
                    nc.scalar.activation(sq[a][:, :], y[r][:, :], ACT.Square, accum_out=ssg[:, c:c + 1]).then_inc(ss_ok, 1)
                    act.dma_start(K.YS[c * P:(c + 1) * P, bass.ds(i * GW, GW)], y[r][:, :]).then_inc(y_stored[r], 16)

                for c in range(NT):
                    a = c % 2
                    act.wait_ge(x_turned, base + (c + 1) + PRIMED)
                    act.wait_ge(y_done, before(base, c, 2) + PRIMED)
                    nc.scalar.activation(bt[a][:, :], pbt[:, :], ACT.Copy).then_inc(bt_ok, 1)
                    act.wait_ge(skip_ok, before(base, c, 2) + PRIMED)
                    act.wait_ge(xdt_ok, before(base, c, 2) + PRIMED)
                    nc.scalar.activation(xs[a][:, :], px[:, :], ACT.Copy).then_inc(xs_ok, 1)
                    act.wait_ge(seg_ok, base + (c + 1) + PRIMED)
                    nc.scalar.activation(dec[a][:, :, :], dec[a][:, :, :], ACT.Exp).then_inc(e_ok, 1)
                    if c >= 2:
                        squares(c - 2)
                squares(NT - 2)
                squares(NT - 1)
            for r in range(RING):
                act.wait_ge(y_stored[r], G * NT // RING * 16 + PRIMED)
            act.nop()

        @block.vector
        def _(dve):
            V = nc.vector
            with dve.Fori(0, G) as i:
                base = i * NT

                def front(c):
                    a = c % 2
                    dve.wait_ge(cb_done, base + (c + 1) + PRIMED)
                    dve.wait_ge(w_ok, before(base, c, 2) + PRIMED)
                    V.tensor_tensor(cbm[a][:, :], pcb[:, :], K.upper, ALU.mult).then_inc(cbm_ok, 1)
                    dve.wait_ge(r_done, base + (c + 1) + PRIMED)
                    for h in range(HG):
                        last = V.tensor_scalar(dec[a][:, h, :], pr[:, h, :], H[:, CS, c, h:h + 1], 0.0, ALU.subtract, ALU.min)
                    last.then_inc(seg_ok, 1)
                    dve.wait_ge(xs_ok, base + (c + 1) + PRIMED)
                    dve.wait_ge(y_done, before(base, c, 2) + PRIMED)
                    dve.wait_ge(xde_ok, before(base, c, 2) + PRIMED)
                    V.tensor_tensor(byhead(xdt[a][:, :]), byhead(xs[a][:, :]), heads(DT, c, HD), ALU.mult).then_inc(xdt_ok, 1)

                def back(c):
                    a = c % 2
                    dve.wait_ge(yi_done, base + (c + 1) + PRIMED)
                    dve.wait_ge(skipped, before(base, c, 2) + PRIMED)
                    V.tensor_tensor(byhead(yi[a][:, :]), byhead(pyi[:, :]), heads(ECS, c, HD), ALU.mult).then_inc(yi_ok, 1)
                    if c + 1 < NT:
                        dve.wait_ge(faded, i * (NT - 1) + (c + 1) + PRIMED)
                        dve.wait_ge(st_done, i * (NT - 1) + (c + 1) + PRIMED)
                        V.tensor_tensor(state[:, :], state[:, :], pst[:, :], ALU.add).then_inc(st_ok, 1)
                    dve.wait_ge(y_done, base + (c + 1) + PRIMED)
                    dve.wait_ge(yi_ok, base + (c + 1) + PRIMED)
                    V.tensor_tensor(yi[a][:, :], yi[a][:, :], py[:, :], ALU.add).then_inc(y_ok, 1)

                def weights(c):
                    a = c % 2
                    dve.wait_ge(e_ok, base + (c + 1) + PRIMED)
                    dve.wait_ge(cbm_ok, base + (c + 1) + PRIMED)
                    dve.wait_ge(y_done, before(base, c, 2) + PRIMED)
                    V.tensor_tensor(W[a][:, 0:LO, :], dec[a][:, 0:LO, :], cbm[a][:, :].unsqueeze(1).to_broadcast([P, LO, P]),
                                    ALU.mult).then_inc(w_lo, 1)

                dve.wait_ge(gated, base + PRIMED)
                dve.wait_ge(ss_ok, base + PRIMED)
                V.tensor_copy(H[:, :, :, :], K.heads[:, :, :, bass.ds(i * HG, HG)]).then_inc(heads_ok, 1)
                V.memset(state[:, :], 0.0).then_inc(st_ok, 1)
                dve.wait_ge(heads_ok, i + 1 + PRIMED)
                front(0)
                weights(0)
                for c in range(NT):
                    if c + 1 < NT:
                        front(c + 1)
                    back(c)
                    if c + 1 < NT:
                        weights(c + 1)
                dve.wait_ge(ss_ok, base + NT + PRIMED)
                V.tensor_copy(K.ss[:, :, bass.ds(i, 1)].rearrange("p c a -> p (c a)"), ssg[:, :])

        @block.gpsimd
        def _(pool):
            Q = nc.gpsimd
            with pool.Fori(0, G) as i:
                base = i * NT

                def tail(c):
                    a = c % 2
                    pool.wait_ge(xs_ok, base + (c + 1) + PRIMED)
                    Q.tensor_tensor(byhead(xsk[a][:, :]), byhead(xs[a][:, :]), heads(SKIP, c, HD), ALU.mult).then_inc(skip_ok, 1)
                    pool.wait_ge(y_ok, base + (c + 1) + PRIMED)
                    pool.wait_ge(skip_ok, base + (c + 1) + PRIMED)
                    Q.tensor_tensor(xsk[a][:, :], xsk[a][:, :], yi[a][:, :], ALU.add).then_inc(skipped, 1)
                    pool.wait_ge(skipped, base + (c + 1) + PRIMED)
                    pool.wait_ge(y_stored[c % RING], i * (NT // RING * 16) + (c // RING) * 16 + PRIMED)
                    pool.wait_ge(ss_ok, before(base, c, RING) + PRIMED)
                    arrived(pool, i, c)
                    Q.tensor_tensor(y[c % RING][:, :], xsk[a][:, :], z[c % RING][:, :], ALU.mult).then_inc(gated, 1)

                for c in range(NT):
                    a = c % 2
                    pool.wait_ge(cbm_ok, base + (c + 1) + PRIMED)
                    pool.wait_ge(e_ok, base + (c + 1) + PRIMED)
                    pool.wait_ge(y_done, before(base, c, 2) + PRIMED)
                    Q.tensor_tensor(W[a][:, LO:, :], dec[a][:, LO:, :], cbm[a][:, :].unsqueeze(1).to_broadcast([P, HG - LO, P]),
                                    ALU.mult).then_inc(w_ok, 1)
                    pool.wait_ge(xdt_ok, base + (c + 1) + PRIMED)
                    Q.tensor_tensor(byhead(xde[a][:, :]), byhead(xdt[a][:, :]), heads(TOEND, c, HD), ALU.mult).then_inc(xde_ok, 1)
                    if c >= 1:
                        tail(c - 1)
                    if c + 1 < NT:
                        pool.wait_ge(yi_done, base + (c + 1) + PRIMED)
                        Q.tensor_tensor(byhead(state[:, :]), byhead(state[:, :]), heads(ETOT, c, HD), ALU.mult).then_inc(faded, 1)
                tail(NT - 1)


def ssd_out_stage(nc, K, A):
    NK, GP = DI // P // 2, G // 2
    PASSES = 2
    ITEMS = PASSES * NT
    with Stage(nc, "sout") as st:
        w, loaded = K.w_out, K.wo_loaded
        wh, wl = (st.sb(n, [P, NK, D], F32R) for n in ("w_high", "w_low"))
        y = [st.sb(f"y{a}", [P, GP, DI // G]) for a in range(2)]
        whole = [st.sb(f"whole{a}", [P, NK, P]) for a in range(2)]
        yh, yl = ([st.sb(f"{n}{a}", [P, NK, P], F32R) for a in range(2)] for n in ("y_high", "y_low"))
        tp = [st.ps(f"tp{a}", [P, NK, P]) for a in range(2)]
        py = [st.ps(f"py{a}", [P, D]) for a in range(2)]
        mean, root, rstd_ok, scaled, turned, kept, high_ok, low_ok, w_high, w_low, done, added = (st.sem(n) for n in (
            "mean", "root", "rstd_ready", "scaled", "turned", "kept", "high_ready", "low_ready", "w_high_ready", "w_low_ready",
            "done", "added"))
        y_loaded = [st.sem(f"y_loaded{a}") for a in range(2)]
        block = st.ctx.enter_context(nc.Block())

        @block.sync
        def _(sp):
            for n in range(ITEMS):
                half, t = n // NT, n % NT
                if n >= 2:
                    sp.wait_ge(turned, n - 1)
                sp.dma_start(y[n % 2][:, :, :].rearrange("p g n -> p (g n)"),
                             K.YS[t * P:(t + 1) * P, half * NK * P:(half + 1) * NK * P]).then_inc(y_loaded[n % 2], 16)
                if n == 2:
                    sp.wait_ge(w_low, NK)
                    sp.dma_start(w[:, :, :], A["w_out_ssd"][NK * P:, :].rearrange("(k p) n -> p k n", p=P)).then_inc(loaded, 16)

        @block.scalar
        def _(act):
            act.wait_ge(mean, 1)
            nc.scalar.activation(K.ss[:, :, :], K.ss[:, :, :], ACT.Sqrt).then_inc(root, 1)
            for n in range(ITEMS):
                half, t = n // NT, n % NT
                act.wait_ge(kept, n + 1)
                if n >= 2:
                    act.wait_ge(done, n - 1)
                nc.scalar.activation(yh[n % 2][:, :, :], whole[n % 2][:, :, :], ACT.Copy).then_inc(high_ok, 1)
                if t == 0:
                    act.wait_ge(loaded, 16 * (half + 1))
                    if half:
                        act.wait_ge(done, half * NT)
                    for k in range(NK):
                        nc.scalar.activation(wh[:, k, :], w[:, k, :], ACT.Copy).then_inc(w_high, 1)

        @block.vector
        def _(dve):
            V = nc.vector

            def scale(n):
                half, t = n // NT, n % NT
                dve.wait_ge(y_loaded[n % 2], (n // 2 + 1) * 16)
                r = K.ss[:, t, half * GP:(half + 1) * GP].unsqueeze(2).to_broadcast([P, GP, DI // G])
                V.tensor_tensor(y[n % 2][:, :, :], y[n % 2][:, :, :], r, ALU.mult).then_inc(scaled, 1)

            def add(n):
                t = n % NT
                dve.wait_ge(done, n + 1)
                if n >= NT:
                    dve.wait_ge(added, n - NT + 1)
                V.tensor_tensor(K.X[:, t, :], K.X[:, t, :], py[n % 2][:, :], ALU.add).then_inc(added, 1)

            V.tensor_scalar(K.ss[:, :, :], K.ss[:, :, :], 1.0 / (DI // G), EPS, ALU.mult, ALU.add).then_inc(mean, 1)
            dve.wait_ge(root, 1)
            V.reciprocal(K.ss[:, :, :], K.ss[:, :, :]).then_inc(rstd_ok, 1)
            dve.wait_ge(rstd_ok, 1)
            scale(0)
            for n in range(ITEMS):
                half, t = n // NT, n % NT
                if n + 1 < ITEMS:
                    scale(n + 1)
                dve.wait_ge(turned, n + 1)
                if n >= 2:
                    dve.wait_ge(high_ok, n - 1)
                    dve.wait_ge(low_ok, n - 1)
                g = K.vecs[:, V_GATE + half * NK:V_GATE + (half + 1) * NK].unsqueeze(2).to_broadcast([P, NK, P])
                V.tensor_tensor(whole[n % 2][:, :, :], tp[n % 2][:, :, :], g, ALU.mult).then_inc(kept, 1)
                dve.wait_ge(high_ok, n + 1)
                dve.wait_ge(kept, n + 1)
                V.tensor_tensor(yl[n % 2][:, :, :], whole[n % 2][:, :, :], bits(yh[n % 2][:, :, :]), ALU.subtract).then_inc(low_ok, 1)
                if n >= 1:
                    add(n - 1)
                if t == 0:
                    for k in range(NK):
                        dve.wait_ge(w_high, half * NK + k + 1)
                        V.tensor_tensor(wl[:, k, :], w[:, k, :], bits(wh[:, k, :]), ALU.subtract).then_inc(w_low, 1)
            add(ITEMS - 1)

        @block.tensor
        def _(pe):
            def turn(n):
                pe.wait_ge(scaled, n + 1)
                if n >= 2:
                    pe.wait_ge(kept, n - 1)
                rows = y[n % 2][:, :, :].rearrange("p g n -> p (g n)")
                for j in range(NK):
                    last = nc.tensor.transpose(tp[n % 2][:, j, :], rows[:, j * P:(j + 1) * P], K.ident)
                last.then_inc(turned, 1)

            turn(0)
            for n in range(ITEMS):
                half, t = n // NT, n % NT
                if n + 1 < ITEMS:
                    turn(n + 1)
                pe.wait_ge(low_ok, n + 1)
                if n >= 2:
                    pe.wait_ge(added, n - 1)
                a = n % 2
                for k in range(NK):
                    if t == 0:
                        pe.wait_ge(w_low, half * NK + k + 1)
                    for h in range(2):
                        cols = slice(h * HALF, (h + 1) * HALF)
                        last = split_product(nc, py[a][:, cols], (yh[a][:, k, :], yl[a][:, k, :]), (wh[:, k, cols], wl[:, k, cols]),
                                             k == 0, k == NK - 1)
                last.then_inc(done, 1)


def ssd_layer(nc, K, A):
    with Stage(nc, "ssd_layer") as outer:
        ctx, K.wo_loaded = outer.ctx, outer.sem("wo_loaded")

        def sb(name, shape):
            return ctx.enter_context(nc.sbuf_tensor(name, shape, F32))

        K.heads, K.ss = sb("heads", [P, 7, NT, HS]), sb("gate_ss", [P, NT, G])
        with ExitStack() as early:
            K.HH, K.HL = (early.enter_context(nc.sbuf_tensor(f"ssd_{n}", [P, ND, S], F32R)) for n in ("high", "low"))
            norm_stage(nc, K, V_SSD, "norm_s", split=True)
            gate_stage(nc, K, A)
            conv_stage(nc, K, A)
        K.w_out = sb("w_out", [P, DI // P // 2, D])

        def out_weights(sp):
            sp.dma_start(K.w_out[:, :, :], A["w_out_ssd"][0:DI // 2, :].rearrange("(k p) n -> p k n", p=P)).then_inc(K.wo_loaded, 16)

        scan_stage(nc, K, A, out_weights)
        ssd_out_stage(nc, K, A)


def router_stage(nc, K, A, layer, M):
    C, T2 = K.consts, 2 * NT
    with Stage(nc, f"route{layer}") as st:
        L = st.sb("L", [P, NT, NL])
        gm, gv, m1, m2, ex, den = (st.sb(n, [P, NT]) for n in ("gm", "gv", "m1", "m2", "ex", "den"))
        goh, gt = st.sb("goh", [P, NT, NG]), st.sb("gt", [P, NT, NG])
        pick = st.sb("pick", [P, NT, EPG, NG])
        ing, et = st.sb("ing", [P, NT, EPG]), st.sb("et", [P, NT, EPG])
        oh = [st.sb(f"oh{k}", [P, NT, EPG]) for k in range(2)]
        choice = st.sb("choice", [P, 2, NT, NE])
        both = st.sb("both", [P, NT, NE])
        before = st.sb("before", [P, NT + 1, NE])
        cum = st.sb("cum", [P, NT, NE])
        prod = st.sb("prod", [P, 2, NT, NE])
        rank, extra, where, expert, start = (st.sb(n, [P, T2]) for n in ("rank", "extra", "where", "expert", "start"))
        more = st.sb("more", [P, NE])
        upto = [st.sb(f"upto{a}", [P, NE]) for a in range(2)]
        first = st.sb("first", [P, NE])
        owner = st.sb("owner", [P, NBLK - NE, NE])
        planf = st.sb("planf", [P, 1 + NBLK])
        row1 = [st.sb(f"row1{a}", [P, P]) for a in range(2)]
        col1 = [st.sb(f"col1{a}", [P, NBLK]) for a in range(2)]
        plg, pcum, ptab = st.ps("plg", [P, NT, NL]), st.ps("pcum", [P, 2, NT, NE]), st.ps("ptab", [P, NBLK])
        logits, chain, expin, expd, masked, counted, onehot, placed = (st.sem(n) for n in (
            "logits", "chain", "exp_in", "exp_done", "chosen", "counted", "one_hot", "placed"))
        block = st.ctx.enter_context(nc.Block())

        @block.tensor
        def _(pe):
            pe.wait_ge(M.wr_loaded, 16)
            for t in range(NT):
                for k in range(ND):
                    last = nc.tensor.matmul(plg[:, t, :], K.B1[:, k, t * P:(t + 1) * P], M.wr[:, k, :], start=(k == 0), stop=(k == ND - 1))
            last.then_inc(logits, 1)
            pe.wait_ge(masked, 1)
            nc.tensor.matmul(pcum[:, 0, :, :], K.strict, both[:, :, :], start=True, stop=True)
            nc.tensor.matmul(pcum[:, 1, :, :], K.ones, both[:, :, :], start=True, stop=True).then_inc(counted, 1)
            for n in range(T2):
                pe.wait_ge(onehot, 2 * n + 2)
                nc.tensor.matmul(ptab[:, :], row1[n % 2][:, :], col1[n % 2][:, :], start=(n == 0), stop=(n == T2 - 1)).then_inc(placed, 1)

        @block.scalar
        def _(act):
            act.wait_ge(expin, 1)
            nc.scalar.activation(gt[:, :, :], gt[:, :, :], ACT.Exp).then_inc(expd, 1)
            act.wait_ge(expin, 2)
            nc.scalar.activation(ex[:, :], ex[:, :], ACT.Exp).then_inc(expd, 1)

        @block.vector
        def _(dve):
            step = Chain(dve, chain)
            V = nc.vector

            def over(x, shape, axis):
                return x.unsqueeze(axis).to_broadcast(shape)

            def best(value, top, hot, scratch, width, desc):
                shape = [P, NT, width]
                order = C[:, desc:desc + width].unsqueeze(1).to_broadcast(shape)
                step(V.tensor_reduce(top[:, :], value, AX.X, ALU.max))
                step(V.tensor_tensor(scratch, value, over(top[:, :], shape, 2), ALU.is_equal))
                step(V.tensor_tensor(scratch, scratch, order, ALU.mult))
                step(V.tensor_reduce(den[:, :], scratch, AX.X, ALU.max))
                step(V.tensor_tensor(hot, scratch, over(den[:, :], shape, 2), ALU.is_equal))

            def whole(out, x, unit):
                step(V.tensor_scalar(out, x, 1.0 / unit, -(unit - 1) / (2 * unit), ALU.mult, ALU.add))
                step(V.tensor_scalar(out, out, MAGIC, MAGIC, ALU.add, ALU.subtract))

            dve.wait_ge(logits, 1)
            bias = K.vecs[:, V_BR + layer * NL:V_BR + (layer + 1) * NL].unsqueeze(1).to_broadcast([P, NT, NL])
            step(V.tensor_tensor(L[:, :, :], plg[:, :, :], bias, ALU.add))
            group, each = L[:, :, 0:NG], L[:, :, NG:NL].rearrange("p t (g e) -> p t e g", g=NG)
            best(group, gm, goh[:, :, :], gt[:, :, :], NG, C_GDESC)
            V.tensor_tensor(gt[:, :, :], group, over(gm[:, :], [P, NT, NG], 2), ALU.subtract).then_inc(expin, 1)
            step(V.tensor_tensor(pick[:, :, :, :], each, over(goh[:, :, :], [P, NT, EPG, NG], 2), ALU.mult))
            step(V.tensor_reduce(ing[:, :, :], pick[:, :, :, :], AX.X, ALU.add))
            best(ing[:, :, :], m1, oh[0][:, :, :], et[:, :, :], EPG, C_DESC)
            step(V.scalar_tensor_tensor(out=ing[:, :, :], in0=oh[0][:, :, :], scalar=NEG, in1=ing[:, :, :], op0=ALU.mult, op1=ALU.add))
            best(ing[:, :, :], m2, oh[1][:, :, :], et[:, :, :], EPG, C_DESC)
            V.tensor_tensor(ex[:, :], m2[:, :], m1[:, :], ALU.subtract).then_inc(expin, 1)
            dve.wait_ge(expd, 2)
            step(V.tensor_reduce(gv[:, :], gt[:, :, :], AX.X, ALU.add))
            step(V.tensor_scalar(den[:, :], ex[:, :], 1.0, None, ALU.add))
            step(V.tensor_tensor(den[:, :], den[:, :], gv[:, :], ALU.mult))
            step(V.reciprocal(M.weight[:, 0, :], den[:, :]))
            step(V.tensor_tensor(M.weight[:, 1, :], M.weight[:, 0, :], ex[:, :], ALU.mult))
            for k in range(2):
                hot = choice[:, k, :, :].rearrange("p t (g e) -> p t g e", g=NG)
                shape = [P, NT, NG, EPG]
                step(V.tensor_tensor(hot, over(goh[:, :, :], shape, 3), over(oh[k][:, :, :], shape, 2), ALU.mult))
            V.tensor_tensor(both[:, :, :], choice[:, 0, :, :], choice[:, 1, :, :], ALU.add).then_inc(masked, 1)
            dve.wait_ge(counted, 1)
            step(V.memset(before[:, 0, :], 0.0))
            for t in range(NT):
                step(V.tensor_tensor(before[:, t + 1, :], before[:, t, :], pcum[:, 1, t, :], ALU.add))
            step(V.tensor_tensor(cum[:, :, :], before[:, 0:NT, :], pcum[:, 0, :, :], ALU.add))
            step(V.tensor_scalar(more[:, :], before[:, NT, :], -1.0, 0.0, ALU.add, ALU.max))
            whole(more[:, :], more[:, :], P)
            step(V.tensor_copy(upto[0][:, :], more[:, :]))
            a, d = 0, 1
            while d < NE:
                step(V.tensor_copy(upto[1 - a][:, 0:d], upto[a][:, 0:d]))
                step(V.tensor_tensor(upto[1 - a][:, d:], upto[a][:, d:], upto[a][:, 0:NE - d], ALU.add))
                a, d = 1 - a, 2 * d
            total = upto[a]
            step(V.tensor_tensor(first[:, :], total[:, :], more[:, :], ALU.subtract))
            flat = choice[:, :, :, :].rearrange("p k t e -> p (k t) e")
            pflat = prod[:, :, :, :].rearrange("p k t e -> p (k t) e")
            for k in range(2):
                step(V.tensor_tensor(prod[:, k, :, :], choice[:, k, :, :], cum[:, :, :], ALU.mult))
            step(V.tensor_reduce(rank[:, :], pflat, AX.X, ALU.add))
            for out, row in ((expert, C[:, C_IOTA:C_IOTA + NE]), (start, first[:, :])):
                step(V.tensor_tensor(pflat, flat, row.unsqueeze(1).to_broadcast([P, T2, NE]), ALU.mult))
                step(V.tensor_reduce(out[:, :], pflat, AX.X, ALU.add))
            whole(extra[:, :], rank[:, :], P)
            step(V.scalar_tensor_tensor(out=rank[:, :], in0=extra[:, :], scalar=-float(P), in1=rank[:, :], op0=ALU.mult, op1=ALU.add))
            step(V.tensor_tensor(start[:, :], start[:, :], extra[:, :], ALU.add))
            step(V.scalar_tensor_tensor(out=start[:, :], in0=start[:, :], scalar=float(NE - 1), in1=expert[:, :], op0=ALU.add, op1=ALU.subtract))
            step(V.tensor_scalar(extra[:, :], extra[:, :], 0.0, None, ALU.is_gt))
            step(V.tensor_tensor(start[:, :], start[:, :], extra[:, :], ALU.mult))
            step(V.tensor_tensor(where[:, :], expert[:, :], start[:, :], ALU.add))
            step(V.scalar_tensor_tensor(out=expert[:, :], in0=where[:, :], scalar=float(P), in1=rank[:, :], op0=ALU.mult, op1=ALU.add))
            step(V.tensor_copy(M.slot[:, :], expert[:, :]))
            step(V.tensor_copy(planf[:, 1:1 + NE], C[:, C_IOTA:C_IOTA + NE]))
            shape = [P, NBLK - NE, NE]
            step(V.tensor_tensor(owner[:, :, :], over(total[:, :], shape, 1), over(C[:, C_BLK:C_BLK + NBLK - NE], shape, 2), ALU.is_le))
            step(V.tensor_reduce(planf[:, 1 + NE:], owner[:, :, :], AX.X, ALU.add))
            step(V.tensor_scalar(planf[:, 1 + NE:], planf[:, 1 + NE:], float(NE - 1), None, ALU.min))
            step(V.tensor_scalar(planf[:, 0:1], total[:, NE - 1:NE], 1.0, None, ALU.add))
            whole(planf[:, 0:1], planf[:, 0:1], 2)
            step(V.tensor_scalar(planf[:, 0:1], planf[:, 0:1], float(NE // 2 - 1), None, ALU.add))
            step(V.tensor_copy(M.plan[:, :], planf[:, :]))
            for n in range(T2):
                if n >= 2:
                    dve.wait_ge(placed, n - 1)
                V.tensor_scalar(row1[n % 2][:, :], C[:, C_IOTA:C_IOTA + P], rank[:, n:n + 1], None, ALU.is_equal).then_inc(onehot, 1)
                V.tensor_scalar(col1[n % 2][:, :], C[:, C_IOTA:C_IOTA + NBLK], where[:, n:n + 1], C[:, C_TOK + n % NT:C_TOK + n % NT + 1],
                                ALU.is_equal, ALU.mult).then_inc(onehot, 1)
            step(V.memset(M.tokens[:, NBLK:], 0))
            dve.wait_ge(placed, T2)
            step(V.tensor_copy(M.tokens[:, 0:NBLK], ptab[:, :]))


def expert_stage(nc, K, A, layer, M):
    Y = K.Y
    FK = DE // P
    with Stage(nc, f"moe{layer}") as st:
        pick = [st.sb(f"pick{a}", [P, 1], I32) for a in range(2)]
        spare = st.sb("spare", [P, 2], I32)
        xg = [st.sb(f"xg{a}", [P, D]) for a in range(2)]
        xT = [st.sb(f"xT{a}", [P, ND, P]) for a in range(2)]
        sg = [st.sb(f"sg{a}", [P, DE]) for a in range(2)]
        hid = [st.sb(f"hid{a}", [P, DE]) for a in range(2)]
        hT = [st.sb(f"hT{a}", [P, FK, P]) for a in range(2)]
        y = [st.sb(f"y{a}", [P, D]) for a in range(2)]
        pg = [st.ps(f"pg{a}", [P, DE]) for a in range(2)]
        pu = [st.ps(f"pu{a}", [P, DE]) for a in range(2)]
        px, ph = st.ps("px", [P, FK, P]), st.ps("ph", [P, FK, P])
        py = [st.ps(f"py{h}", [P, HALF]) for h in range(2)]
        x_turned, x_kept, h_kept = (st.sem(n) for n in ("x_turned", "x_kept", "h_kept"))
        gathered = [st.sem(f"gathered{a}", primed=False) for a in range(2)]
        picked, gate_done, up_done, silu_done, hid_ok, h_turned, stored = (
            [st.sem(f"{n}{a}") for a in range(2)] for n in
            ("picked", "gate_done", "up_done", "silu_done", "hidden", "h_turned", "stored"))
        y_done, y_kept = ([st.sem(f"{n}{h}") for h in range(2)] for n in ("y_done", "y_kept"))
        block = st.primed_block()

        def rounds_less_one(eng):
            return eng.value_load(M.plan[0:1, 0:1], min_val=NE // 2 - 1, max_val=NBLK // 2 - 1)

        def rounds(eng):
            return rounds_less_one(eng) + 1

        @block.sync
        def _(sp):
            n = rounds_less_one(sp)

            def expert(b):
                return sp.value_load(M.plan[0:1, bass.ds(b + 1, 1)], min_val=0, max_val=NE - 1)

            def load_down(e, a):
                sp.dma_start(M.wd[a][:, :, :], M.down(e)).then_inc(M.wd_loaded[a], 16)

            with sp.Fori(0, n) as i:
                for a in range(2):
                    e, e_down = expert(i * 2 + (2 + a)), expert(i * 2 + (1 + a))
                    sp.wait_ge(up_done[a], i + 1 + PRIMED)
                    sp.dma_start(M.wg[a][:, :, :], M.gate(e)).then_inc(M.wg_loaded[a], 16)
                    sp.dma_start(M.wu[a][:, :, :], M.up(e)).then_inc(M.wu_loaded[a], 16)
                    if a == 0:
                        sp.wait_ge(y_done[1], i * 2 + PRIMED)
                        load_down(e_down, 1)
                    else:
                        sp.wait_ge(y_done[1], i * 2 + 1 + PRIMED)
                        load_down(e_down, 0)
            e_down = expert(n * 2 + 1)
            sp.wait_ge(y_done[1], n * 2 + PRIMED)
            load_down(e_down, 1)

        @block.gpsimd
        def _(pool):
            n = rounds(pool)

            def gather(b, a, done):
                nc.gpsimd.tensor_copy(pick[a][:, :], M.tokens[:, bass.ds(b, 1)]).then_inc(picked[a], 1)
                pool.wait_ge(picked[a], done + 1 + PRIMED)
                nc.gpsimd.tensor_tensor(spare[:, a:a + 1], pick[a][:, :], pick[a][:, :], ALU.add)
                nc.gpsimd.indirect_dma_start(out=xg[a][:, :], out_offset=None, in_=K.HN[:, :],
                                             in_offset=bass.IndirectOffsetOnAxis(ap=pick[a][:, :], axis=0)).then_inc(gathered[a], 16)

            for a in range(2):
                gather(a, a, 0)
            with pool.Fori(0, n) as i:
                for a in range(2):
                    pool.wait_ge(gathered[a], i * 16 + 16)
                    pool.wait_ge(x_turned, i * 4 + 2 * (a + 1) + PRIMED)
                    gather(i * 2 + (2 + a), a, i + 1)

        @block.tensor
        def _(pe):
            def turn_x(a, half, seq, round_):
                pe.wait_ge(gathered[a], round_ * 16 + 16)
                pe.wait_ge(x_kept, seq + PRIMED)
                for j in range(FK):
                    c = (half * FK + j) * P
                    last = nc.tensor.transpose(px[:, j, :], xg[a][:, c:c + P], K.ident)
                last.then_inc(x_turned, 1)

            n = rounds(pe)
            for a in range(2):
                for half in range(2):
                    turn_x(a, half, 2 * a + half, 0)
            with pe.Fori(0, n) as i:
                def first(a, out, w, loaded, done):
                    pe.wait_ge(loaded[a], i * 16 + 16)
                    for k in range(ND):
                        last = nc.tensor.matmul(out[a][:, :], xT[a][:, k, :], w[a][:, k, :], start=(k == 0), stop=(k == ND - 1))
                    last.then_inc(done[a], 1)

                def gate(a):
                    pe.wait_ge(x_kept, i * 4 + 2 * (a + 1) + PRIMED)
                    pe.wait_ge(hid_ok[a], i + PRIMED)
                    first(a, pg, M.wg, M.wg_loaded, gate_done)

                def up(a):
                    first(a, pu, M.wu, M.wu_loaded, up_done)

                def turn_h(a):
                    pe.wait_ge(hid_ok[a], i + 1 + PRIMED)
                    pe.wait_ge(h_kept, i * 2 + a + PRIMED)
                    for j in range(FK):
                        last = nc.tensor.transpose(ph[:, j, :], hid[a][:, j * P:(j + 1) * P], K.ident)
                    last.then_inc(h_turned[a], 1)

                def down(a, h):
                    pe.wait_ge(h_kept, i * 2 + (a + 1) + PRIMED)
                    pe.wait_ge(M.wd_loaded[a], i * 16 + 16)
                    pe.wait_ge(y_kept[h], i * 2 + a + PRIMED)
                    for k in range(FK):
                        last = nc.tensor.matmul(py[h][:, :], hT[a][:, k, :], M.wd[a][:, k, h * HALF:(h + 1) * HALF],
                                                start=(k == 0), stop=(k == FK - 1))
                    last.then_inc(y_done[h], 1)

                gate(0)
                up(0)
                gate(1)
                turn_h(0)
                turn_x(0, 0, i * 4 + 4, i + 1)
                up(1)
                turn_x(0, 1, i * 4 + 5, i + 1)
                down(0, 0)
                turn_h(1)
                turn_x(1, 0, i * 4 + 6, i + 1)
                down(0, 1)
                turn_x(1, 1, i * 4 + 7, i + 1)
                down(1, 0)
                down(1, 1)
            for a in range(2):
                pe.wait_ge(stored[a], n * 16 + PRIMED)

        @block.scalar
        def _(act):
            n = rounds(act)
            with act.Fori(0, n) as i:
                def silu(a):
                    act.wait_ge(gate_done[a], i + 1 + PRIMED)
                    act.wait_ge(hid_ok[a], i + PRIMED)
                    nc.scalar.activation(sg[a][:, :], pg[a][:, :], ACT.Silu).then_inc(silu_done[a], 1)

                def keep_h(a):
                    act.wait_ge(h_turned[a], i + 1 + PRIMED)
                    act.wait_ge(y_done[1], i * 2 + PRIMED)
                    nc.scalar.activation(hT[a][:, :, :], ph[:, :, :], ACT.Copy).then_inc(h_kept, 1)

                def keep_y(a, h):
                    act.wait_ge(y_done[h], i * 2 + (a + 1) + PRIMED)
                    act.wait_ge(stored[a], i * 16 + PRIMED)
                    nc.scalar.activation(y[a][:, h * HALF:(h + 1) * HALF], py[h][:, :], ACT.Copy).then_inc(y_kept[h], 1)

                def store(a):
                    for h in range(2):
                        act.wait_ge(y_kept[h], i * 2 + (a + 1) + PRIMED)
                    act.dma_start(Y[bass.ds((i * 2 + a) * P, P), :], y[a][:, :]).then_inc(stored[a], 16)

                silu(0)
                silu(1)
                keep_h(0)
                keep_y(0, 0)
                keep_h(1)
                keep_y(0, 1)
                store(0)
                keep_y(1, 0)
                keep_y(1, 1)
                store(1)

        @block.vector
        def _(dve):
            n = rounds(dve)

            def keep_x(a, half, seq, used):
                dve.wait_ge(x_turned, seq + 1 + PRIMED)
                dve.wait_ge(up_done[a], used + PRIMED)
                c = V_MOE + layer * ND + half * FK
                g = K.vecs[:, c:c + FK].unsqueeze(2).to_broadcast([P, FK, P])
                nc.vector.tensor_tensor(xT[a][:, half * FK:(half + 1) * FK, :], px[:, :, :], g, ALU.mult).then_inc(x_kept, 1)

            for a in range(2):
                for half in range(2):
                    keep_x(a, half, 2 * a + half, 0)
            with dve.Fori(0, n) as i:
                def hidden(a):
                    dve.wait_ge(silu_done[a], i + 1 + PRIMED)
                    dve.wait_ge(up_done[a], i + 1 + PRIMED)
                    dve.wait_ge(h_turned[a], i + PRIMED)
                    nc.vector.tensor_tensor(hid[a][:, :], sg[a][:, :], pu[a][:, :], ALU.mult).then_inc(hid_ok[a], 1)

                hidden(0)
                keep_x(0, 0, i * 4 + 4, i + 1)
                keep_x(0, 1, i * 4 + 5, i + 1)
                hidden(1)
                keep_x(1, 0, i * 4 + 6, i + 1)
                keep_x(1, 1, i * 4 + 7, i + 1)


def combine_stage(nc, K, layer, M):
    with Stage(nc, f"comb{layer}") as st:
        rows = [[st.sb(f"rows{k}{a}", [P, D]) for a in range(2)] for k in range(2)]
        got = [[st.sem(f"got{k}{a}") for a in range(2)] for k in range(2)]
        added = [st.sem(f"added{k}") for k in range(2)]
        block = st.ctx.enter_context(nc.Block())

        @block.gpsimd
        def _(pool):
            for t in range(NT):
                for k in range(2):
                    if t >= 2:
                        pool.wait_ge(added[k], t - 1)
                    c = k * NT + t
                    nc.gpsimd.indirect_dma_start(out=rows[k][t % 2][:, :], out_offset=None, in_=K.Y[:, :],
                                                 in_offset=bass.IndirectOffsetOnAxis(ap=M.slot[:, c:c + 1], axis=0)).then_inc(got[k][t % 2], 16)

        @block.vector
        def _(dve):
            for t in range(NT):
                for k in range(2):
                    dve.wait_ge(got[k][t % 2], 16 * (t // 2 + 1))
                    if k:
                        dve.wait_ge(added[0], t + 1)
                    nc.vector.scalar_tensor_tensor(out=K.X[:, t, :], in0=rows[k][t % 2][:, :], scalar=M.weight[:, k, t:t + 1],
                                                   in1=K.X[:, t, :], op0=ALU.mult, op1=ALU.add).then_inc(added[k], 1)


def moe_layer(nc, K, A, layer):
    M = Names()
    with Stage(nc, f"moes{layer}") as st:
        M.wg, M.wu = ([st.sb(f"{n}{a}", [P, ND, DE]) for a in range(2)] for n in ("wg", "wu"))
        M.wd = [st.sb(f"wd{a}", [P, DE // P, D]) for a in range(2)]
        M.wg_loaded, M.wu_loaded, M.wd_loaded = ([st.sem(f"{n}_loaded{a}") for a in range(2)] for n in ("wg", "wu", "wd"))
        M.weight, M.slot = st.sb("weight", [P, 2, NT]), st.sb("slot", [P, 2 * NT], I32)
        M.plan, M.tokens = st.sb("plan", [P, 1 + NBLK], I32), st.sb("tokens", [P, NBLK + 2], I32)

        def weights(name):
            w = A[name][layer].rearrange("e (k p) n -> e p k n", p=P)
            return lambda e: w[bass.ds(e, 1)].rearrange("a p k n -> p (a k) n")

        M.gate, M.up, M.down = (weights(n) for n in ("w_gate", "w_up", "w_down"))

        def first_weights(sp):
            sp.dma_start(M.wr[:, :, :], A["w_route"][layer].rearrange("(k p) n -> p k n", p=P)).then_inc(M.wr_loaded, 16)
            for a in range(2):
                sp.dma_start(M.wg[a][:, :, :], M.gate(a)).then_inc(M.wg_loaded[a], 16)
                sp.dma_start(M.wu[a][:, :, :], M.up(a)).then_inc(M.wu_loaded[a], 16)
                if a == 0:
                    sp.dma_start(M.wd[a][:, :, :], M.down(a)).then_inc(M.wd_loaded[a], 16)

        M.wr_loaded = st.sem("wr_loaded")
        with ExitStack() as early:
            M.wr = early.enter_context(nc.sbuf_tensor(f"moe_wr{layer}", [P, ND, NL], F32))
            K.B1 = early.enter_context(nc.sbuf_tensor(f"moe_hT{layer}", [P, ND, S], F32))
            norm_stage(nc, K, V_MOE + layer * ND, f"norm_m{layer}", hn_dram=K.HN, prefetch=first_weights)
            router_stage(nc, K, A, layer, M)
        expert_stage(nc, K, A, layer, M)
        combine_stage(nc, K, layer, M)






def program(nc, A, out):
    K = Names()
    K.out = out
    K.QA = nc.dram_tensor("QA", (HA, DH, S), F32).ap()
    K.KA = nc.dram_tensor("KA", (HA, DH, S), F32).ap()
    K.QB = nc.dram_tensor("QB_", (HB, KB, S), F32).ap()
    K.KB = nc.dram_tensor("KB_", (HB, KB, S), F32).ap()
    K.HN = nc.dram_tensor("HN", (S, D), F32).ap()
    K.Z, K.YS = (nc.dram_tensor(n, (S, DI), F32).ap() for n in ("Z", "YS"))
    K.XC = nc.dram_tensor("XC", (XBC // P, P, S), F32).ap()
    K.Y = nc.dram_tensor("Y", (NBLK * P, D), F32).ap()
    with ExitStack() as ctx:
        def sb(name, shape):
            return ctx.enter_context(nc.sbuf_tensor(name, shape, F32))

        K.X, K.consts, K.vecs = sb("X", [P, NT, D]), sb("consts", [P, NC_]), sb("vecs", [P, NV])
        c = K.consts
        K.ident, K.rotA, K.rotB = c[:, C_ID:C_ID + P], c[:, C_ROTA:C_ROTA + P], c[:, C_ROTB:C_ROTB + KB]
        K.maskA, K.maskB = c[:, C_MASKA:C_MASKA + S], c[:, C_MASKB:C_MASKB + S]
        K.upper, K.strict, K.ones = (c[:, n:n + P] for n in (C_UPPER, C_STRICT, C_ONES))
        attention_layer(nc, K, A)
        moe_layer(nc, K, A, 0)
        ssd_layer(nc, K, A)
        moe_layer(nc, K, A, 1)
        norm_stage(nc, K, None, "norm_f", final=A["final_norm"])


def arrange(inputs):
    a = {k: np.asarray(v) for k, v in inputs.items()}

    def columns(v):
        return v.reshape(-1, P).T

    def rows(v):
        return np.broadcast_to(v.reshape(1, -1), (P, v.size))

    vecs = [columns(a["attn_norm"][0]), columns(a["moe_norm"][0]), columns(a["moe_norm"][1]), columns(a["ssd_norm"][0]),
            columns(a["mla_q_norm"][0]), columns(a["mla_kv_norm"][0]), columns(a["gate_norm"][0])]
    for layer in range(2):
        vecs += [rows(a["b_group"][layer]), rows(a["b_router"][layer])]
    vecs += [rows(a["dt_bias"][0]), rows(a["a_log"][0]), rows(a["d_skip"][0])]
    uq = a["w_uq"][0].reshape(QR, HB, KB)
    conv = np.concatenate([a["conv_w"][0], a["conv_b"][0][None]], axis=0)
    wr = np.concatenate([a["w_group"], a["w_router"]], axis=2)
    out = {
        "consts": constants(), "vecs": np.concatenate(vecs, axis=1),
        "x": a["x"].reshape(S, D), "positions": a["positions"].reshape(S),
        "w_in_attn": a["w_in_attn"][0],
        "w_uq": np.concatenate([uq[:, :, NOPE:], uq[:, :, :NOPE]], axis=2).reshape(QR, HB * KB),
        "w_ukv": a["w_ukv"][0], "w_out_attn": a["w_out_attn"][0],
        "w_in_ssd": a["w_in_ssd"][0], "conv": conv.T.reshape(XBC // P, P, CONV + 1),
        "w_out_ssd": a["w_out_ssd"][0],
        "w_route": wr, "w_gate": a["w_gate"], "w_up": a["w_up"], "w_down": a["w_down"],
        "final_norm": a["final_norm"],
    }
    return {k: np.ascontiguousarray(v) for k, v in out.items()}


def declare(nc, arrays):
    A = {n: nc.dram_tensor(f"in_{n}", v.shape, mybir.dt.from_np(v.dtype), kind="ExternalInput").ap() for n, v in arrays.items()}
    out = nc.dram_tensor("out", (S, D), F32, kind="ExternalOutput").ap()
    program(nc, A, out)


def kernel(**inputs):
    import concourse.bacc as bacc
    from concourse.bass_utils import run_bass_kernel_spmd

    nc = bacc.Bacc("TRN2", target_bir_lowering=False, num_devices=1)
    arrays = arrange(inputs)
    declare(nc, arrays)
    r = run_bass_kernel_spmd(nc, [{f"in_{n}": v for n, v in arrays.items()}], core_ids=[0])
    return r.results[0]["out"].reshape(1, S, D)
```
